# Optimizing a Trainium2 kernel written in Bass

```python
import math
import jax
import jax.numpy as jnp
from jax import lax
import numpy as np

D_MODEL = 1024
BATCH = 1
SEQ = 512
DEPTH = 2

CTX_LEN = 256
GRID_W = 64
ROPE_BASE = 10000.0
Q_BLOCK = 128
EPS = 1e-6
NEG_INF = -1e30

MLA_HEADS = 8
MLA_Q_RANK = 384
MLA_KV_RANK = 256
MLA_NOPE = 64
MLA_ROPE = 32
MLA_V = 64
SWA_HEADS = 8
SWA_KV_HEADS = 2
SWA_HEAD_DIM = 64
WINDOW = 128
DIFF_HEADS = 8
DIFF_HALF = 64
DIFF_V = 128
N_EXPERTS = 64
N_GROUPS = 8
TOPK_GROUPS = 4
TOP_K = 8
EXPERT_FF = 256
SHARED_FF = 256
ROUTED_SCALE = 2.5
MOE_BLOCK = 128

EVEN_SPLITS = [MLA_Q_RANK, MLA_KV_RANK, MLA_ROPE, SWA_HEADS * SWA_HEAD_DIM,
               SWA_KV_HEADS * SWA_HEAD_DIM, SWA_KV_HEADS * SWA_HEAD_DIM]
EVEN_IN = sum(EVEN_SPLITS)
EVEN_OUT = MLA_HEADS * MLA_V + SWA_HEADS * SWA_HEAD_DIM
ODD_IN = DIFF_HEADS * (4 * DIFF_HALF + DIFF_V)
ODD_OUT = DIFF_HEADS * DIFF_V
N_EVEN = (DEPTH + 1) // 2
N_ODD = DEPTH // 2

kernel_name = 'hybrid_mla_swa_diffattn_moe_dit'

def split_last(x, sizes):
    points = [int(p) for p in np.cumsum(sizes)[:-1]]
    return jnp.split(x, points, axis=-1)

def rmsnorm(x, g):
    xf = x.astype(jnp.float32)
    y = xf * lax.rsqrt(jnp.mean(xf * xf, axis=-1, keepdims=True) + EPS)
    return (y * g.astype(jnp.float32)).astype(x.dtype)

def modulate(h, shift, scale):
    return h * (1 + scale) + shift

def axial_rope_tables(rows, rot_dim):
    half = rot_dim // 2
    inv_freq = ROPE_BASE ** (-jnp.arange(0, half, 2, dtype=jnp.float32) / half)
    row = jnp.repeat(jnp.arange(rows, dtype=jnp.float32), GRID_W)
    col = jnp.tile(jnp.arange(GRID_W, dtype=jnp.float32), rows)
    ang_r = row[:, None] * inv_freq
    ang_c = col[:, None] * inv_freq
    ang = jnp.concatenate([ang_r, ang_r, ang_c, ang_c], axis=-1)
    return jnp.cos(ang), jnp.sin(ang)

def rotate_half(x):
    x1, x2 = jnp.split(x, 2, axis=-1)
    return jnp.concatenate([-x2, x1], axis=-1)

def apply_rope(x, cos, sin):
    x_r, x_c = jnp.split(x, 2, axis=-1)
    rot = jnp.concatenate([rotate_half(x_r), rotate_half(x_c)], axis=-1)
    return (x * cos[None, :, None, :] + rot * sin[None, :, None, :]).astype(x.dtype)

def full_attention(q, k, v):
    s = jnp.einsum('bqhd,bkhd->bhqk', q, k).astype(jnp.float32) * (q.shape[-1] ** -0.5)
    p = jax.nn.softmax(s, axis=-1).astype(v.dtype)
    return jnp.einsum('bhqk,bkhd->bqhd', p, v)

def sweep_query_blocks(fn, *qs):
    b, n = qs[0].shape[:2]
    nb = n // Q_BLOCK
    blocks = tuple(jnp.moveaxis(q.reshape((b, nb, Q_BLOCK) + q.shape[2:]), 1, 0) for q in qs)
    out = lax.map(lambda qb: fn(*qb), blocks)
    out = jnp.moveaxis(out, 0, 1)
    return out.reshape((b, n) + out.shape[3:])

def softmax_with_sink(s, sink):
    m = jnp.maximum(s.max(axis=-1, keepdims=True), sink)
    e = jnp.exp(s - m)
    return e / (e.sum(axis=-1, keepdims=True) + jnp.exp(sink - m))

def window_sink_attention(q, k, v, k_ctx, v_ctx, sink):
    b, n, hq, d = q.shape
    nb = n // Q_BLOCK
    g = hq // SWA_KV_HEADS
    qb = q.reshape(b, nb, Q_BLOCK, SWA_KV_HEADS, g, d)

    def band(t):
        tp = jnp.pad(t, ((0, 0), (Q_BLOCK, Q_BLOCK), (0, 0), (0, 0)))
        tp = tp.reshape(b, nb + 2, Q_BLOCK, SWA_KV_HEADS, d)
        return jnp.concatenate([tp[:, :-2], tp[:, 1:-1], tp[:, 2:]], axis=2)

    kb, vb = band(k), band(v)
    qq = jnp.arange(Q_BLOCK)[:, None]
    kk = jnp.arange(3 * Q_BLOCK)[None, :]
    rel = kk - Q_BLOCK - qq
    key_pos = jnp.arange(nb)[:, None, None] * Q_BLOCK - Q_BLOCK + kk[None]
    valid = (jnp.abs(rel) <= WINDOW)[None] & (key_pos >= 0) & (key_pos < n)
    scale = d ** -0.5
    s_band = jnp.einsum('bnqhgd,bnkhd->bnhgqk', qb, kb).astype(jnp.float32) * scale
    s_band = jnp.where(valid[None, :, None, None], s_band, NEG_INF)
    s_ctx = jnp.einsum('bnqhgd,bchd->bnhgqc', qb, k_ctx).astype(jnp.float32) * scale
    s = jnp.concatenate([s_band, s_ctx], axis=-1)
    sink_l = sink.astype(jnp.float32).reshape(SWA_KV_HEADS, g)[:, :, None, None]
    p = softmax_with_sink(s, sink_l).astype(v.dtype)
    p_band, p_ctx = p[..., :3 * Q_BLOCK], p[..., 3 * Q_BLOCK:]
    o = (jnp.einsum('bnhgqk,bnkhd->bnqhgd', p_band, vb)
         + jnp.einsum('bnhgqc,bchd->bnqhgd', p_ctx, v_ctx))
    return o.reshape(b, n, hq, d)

def ctx_sink_attention(q, k, v, sink):
    b, n, hq, d = q.shape
    g = hq // SWA_KV_HEADS
    qg = q.reshape(b, n, SWA_KV_HEADS, g, d)
    s = jnp.einsum('bqhgd,bkhd->bhgqk', qg, k).astype(jnp.float32) * (d ** -0.5)
    sink_l = sink.astype(jnp.float32).reshape(SWA_KV_HEADS, g)[:, :, None, None]
    p = softmax_with_sink(s, sink_l).astype(v.dtype)
    return jnp.einsum('bhgqk,bkhd->bqhgd', p, v).reshape(b, n, hq, d)

def even_mixer(a_lat, a_ctx, rope_mla, rope_swa, w_in, g_q, g_kv, w_uq, w_ukv, sink, w_out, ctx_out):
    def project(a):
        b, n = a.shape[:2]
        cq, ckv, kr, qs, ks, vs = split_last(a @ w_in, EVEN_SPLITS)
        q = (rmsnorm(cq, g_q) @ w_uq).reshape(b, n, MLA_HEADS, MLA_NOPE + MLA_ROPE)
        kv = (rmsnorm(ckv, g_kv) @ w_ukv).reshape(b, n, MLA_HEADS, MLA_NOPE + MLA_V)
        q_nope, q_rope = split_last(q, [MLA_NOPE, MLA_ROPE])
        k_nope, v_m = split_last(kv, [MLA_NOPE, MLA_V])
        return (q_nope, q_rope, k_nope, kr[:, :, None, :], v_m,
                qs.reshape(b, n, SWA_HEADS, SWA_HEAD_DIM),
                ks.reshape(b, n, SWA_KV_HEADS, SWA_HEAD_DIM),
                vs.reshape(b, n, SWA_KV_HEADS, SWA_HEAD_DIM))

    def mla_qk(q_nope, q_rope, k_nope, k_rope):
        q = jnp.concatenate([q_nope, q_rope], axis=-1)
        k_rope_h = jnp.broadcast_to(k_rope, k_nope.shape[:3] + (MLA_ROPE,))
        return q, jnp.concatenate([k_nope, k_rope_h], axis=-1)

    b, n = a_lat.shape[:2]
    lq_n, lq_r, lk_n, lk_r, lv_m, lq_s, lk_s, lv_s = project(a_lat)
    cq_n, cq_r, ck_n, ck_r, cv_m, cq_s, ck_s, cv_s = project(a_ctx)
    lq_m, lk_m = mla_qk(lq_n, apply_rope(lq_r, *rope_mla), lk_n, apply_rope(lk_r, *rope_mla))
    ck_m = mla_qk(cq_n, cq_r, ck_n, ck_r)[1]
    lq_s = apply_rope(lq_s, *rope_swa)
    lk_s = apply_rope(lk_s, *rope_swa)
    k_all = jnp.concatenate([ck_m, lk_m], axis=1)
    v_all = jnp.concatenate([cv_m, lv_m], axis=1)
    o_mla = sweep_query_blocks(lambda qb: full_attention(qb, k_all, v_all), lq_m)
    o_swa = window_sink_attention(lq_s, lk_s, lv_s, ck_s, cv_s, sink)
    y_lat = jnp.concatenate([o_mla.reshape(b, n, -1), o_swa.reshape(b, n, -1)], axis=-1) @ w_out
    y_ctx = None
    if ctx_out:
        bc, nc = a_ctx.shape[:2]
        cq_m = mla_qk(cq_n, cq_r, ck_n, ck_r)[0]
        o_mla_c = full_attention(cq_m, ck_m, cv_m)
        o_swa_c = ctx_sink_attention(cq_s, ck_s, cv_s, sink)
        y_ctx = jnp.concatenate([o_mla_c.reshape(bc, nc, -1), o_swa_c.reshape(bc, nc, -1)], axis=-1) @ w_out
    return y_lat, y_ctx

def diff_attention(q1, q2, k1, k2, v, lam):
    scale = q1.shape[-1] ** -0.5
    a1 = jax.nn.softmax(jnp.einsum('bqhd,bkhd->bhqk', q1, k1).astype(jnp.float32) * scale, axis=-1)
    a2 = jax.nn.softmax(jnp.einsum('bqhd,bkhd->bhqk', q2, k2).astype(jnp.float32) * scale, axis=-1)
    return jnp.einsum('bhqk,bkhd->bqhd', (a1 - lam * a2).astype(v.dtype), v)

def odd_mixer(a_lat, a_ctx, rope, w_in, lam_q1, lam_k1, lam_q2, lam_k2, g_sub, w_out, lam_init, ctx_out):
    def project(a):
        b, n = a.shape[:2]
        p = (a @ w_in).reshape(b, n, DIFF_HEADS, 4 * DIFF_HALF + DIFF_V)
        return split_last(p, [DIFF_HALF] * 4 + [DIFF_V])

    def finish(o):
        b, n = o.shape[:2]
        o = rmsnorm(o, g_sub) * (1.0 - lam_init)
        return o.reshape(b, n, ODD_OUT) @ w_out

    f32 = jnp.float32
    lam = (jnp.exp(jnp.sum(lam_q1.astype(f32) * lam_k1.astype(f32)))
           - jnp.exp(jnp.sum(lam_q2.astype(f32) * lam_k2.astype(f32))) + lam_init)
    lq1, lq2, lk1, lk2, lv = project(a_lat)
    cq1, cq2, ck1, ck2, cv = project(a_ctx)
    lq1, lq2, lk1, lk2 = (apply_rope(t, *rope) for t in (lq1, lq2, lk1, lk2))
    k1_all = jnp.concatenate([ck1, lk1], axis=1)
    k2_all = jnp.concatenate([ck2, lk2], axis=1)
    v_all = jnp.concatenate([cv, lv], axis=1)
    o_lat = sweep_query_blocks(lambda a, b: diff_attention(a, b, k1_all, k2_all, v_all, lam), lq1, lq2)
    y_lat = finish(o_lat)
    y_ctx = None
    if ctx_out:
        y_ctx = finish(diff_attention(cq1, cq2, ck1, ck2, cv, lam))
    return y_lat, y_ctx

def route(xf, w_router, b_router):
    n = xf.shape[0]
    scores = jax.nn.sigmoid((xf @ w_router).astype(jnp.float32))
    biased = scores + b_router.astype(jnp.float32)
    grouped = biased.reshape(n, N_GROUPS, N_EXPERTS // N_GROUPS)
    group_score = lax.top_k(grouped, 2)[0].sum(axis=-1)
    _, keep = lax.top_k(group_score, TOPK_GROUPS)
    group_mask = jax.nn.one_hot(keep, N_GROUPS, dtype=jnp.float32).sum(axis=1) > 0
    expert_mask = jnp.repeat(group_mask, N_EXPERTS // N_GROUPS, axis=1)
    _, top_idx = lax.top_k(jnp.where(expert_mask, biased, NEG_INF), TOP_K)
    top_s = jnp.take_along_axis(scores, top_idx, axis=1)
    top_w = top_s / top_s.sum(axis=-1, keepdims=True) * ROUTED_SCALE
    return top_idx, top_w

def routed_experts(xf, top_idx, top_w, w_gate, w_up, w_down):
    n_tok, d = xf.shape
    n_assign = n_tok * TOP_K
    n_slots = ((n_assign + MOE_BLOCK - 1) // MOE_BLOCK + N_EXPERTS) * MOE_BLOCK
    n_blocks = n_slots // MOE_BLOCK
    e_flat = top_idx.reshape(-1)
    order = jnp.argsort(e_flat)
    e_sorted = e_flat[order]
    counts = jnp.bincount(e_flat, length=N_EXPERTS)
    padded = (counts + MOE_BLOCK - 1) // MOE_BLOCK * MOE_BLOCK
    pad_end = jnp.cumsum(padded)
    pad_start = pad_end - padded
    raw_start = jnp.cumsum(counts) - counts
    dest = pad_start[e_sorted] + jnp.arange(n_assign) - raw_start[e_sorted]
    slot_tok = jnp.full((n_slots,), n_tok, jnp.int32).at[dest].set((order // TOP_K).astype(jnp.int32))
    slot_w = jnp.zeros((n_slots,), xf.dtype).at[dest].set(top_w.reshape(-1)[order].astype(xf.dtype))
    block_expert = jnp.minimum(
        jnp.searchsorted(pad_end, jnp.arange(n_blocks) * MOE_BLOCK, side='right'), N_EXPERTS - 1)
    x_pad = jnp.concatenate([xf, jnp.zeros((1, d), xf.dtype)], axis=0)

    def body(acc, blk):
        tok, w, e = blk
        xb = x_pad[tok]
        h = jax.nn.silu(xb @ w_gate[e]) * (xb @ w_up[e])
        return acc.at[tok].add((h @ w_down[e]) * w[:, None]), None

    acc, _ = lax.scan(body, jnp.zeros_like(x_pad),
                      (slot_tok.reshape(n_blocks, MOE_BLOCK), slot_w.reshape(n_blocks, MOE_BLOCK), block_expert))
    return acc[:n_tok]

def moe_ffn(xf, w_router, b_router, we_gate, we_up, we_down, ws_gate, ws_up, ws_down):
    top_idx, top_w = route(xf, w_router, b_router)
    routed = routed_experts(xf, top_idx, top_w, we_gate, we_up, we_down)
    shared = (jax.nn.silu(xf @ ws_gate) * (xf @ ws_up)) @ ws_down
    return routed + shared

def setup_inputs(seed: int = 0) -> dict:
    key = jax.random.key(seed)
    ks = iter(jax.random.split(key, 32))
    D = D_MODEL

    def nrm(shape, scale=1.0):
        return jax.random.normal(next(ks), shape, jnp.float32) * scale

    def gain(shape):
        return 1.0 + nrm(shape, 0.02)

    return {
        'x': nrm((BATCH, SEQ, D)),
        'c': nrm((BATCH, D)),
        'ctx': nrm((BATCH, CTX_LEN, D)),
        'c_ctx': nrm((D,)),
        'w_ada': nrm((DEPTH, D, 6 * D), 0.5 * D ** -0.5),
        'b_ada': nrm((DEPTH, 6 * D), 0.02),
        'g_mix': gain((DEPTH, D)),
        'g_ffn': gain((DEPTH, D)),
        'wa_in': nrm((N_EVEN, D, EVEN_IN), D ** -0.5),
        'ga_q': gain((N_EVEN, MLA_Q_RANK)),
        'ga_kv': gain((N_EVEN, MLA_KV_RANK)),
        'wa_uq': nrm((N_EVEN, MLA_Q_RANK, MLA_HEADS * (MLA_NOPE + MLA_ROPE)), MLA_Q_RANK ** -0.5),
        'wa_ukv': nrm((N_EVEN, MLA_KV_RANK, MLA_HEADS * (MLA_NOPE + MLA_V)), MLA_KV_RANK ** -0.5),
        'wa_sink': nrm((N_EVEN, SWA_HEADS)),
        'wa_out': nrm((N_EVEN, EVEN_OUT, D), EVEN_OUT ** -0.5),
        'wc_in': nrm((N_ODD, D, ODD_IN), D ** -0.5),
        'lam_q1': nrm((N_ODD, DIFF_HALF), 0.1),
        'lam_k1': nrm((N_ODD, DIFF_HALF), 0.1),
        'lam_q2': nrm((N_ODD, DIFF_HALF), 0.1),
        'lam_k2': nrm((N_ODD, DIFF_HALF), 0.1),
        'gc_sub': gain((N_ODD, DIFF_V)),
        'wc_out': nrm((N_ODD, ODD_OUT, D), ODD_OUT ** -0.5),
        'w_router': nrm((DEPTH, D, N_EXPERTS), D ** -0.5),
        'b_router': nrm((DEPTH, N_EXPERTS), 0.01),
        'we_gate': nrm((DEPTH, N_EXPERTS, D, EXPERT_FF), D ** -0.5),
        'we_up': nrm((DEPTH, N_EXPERTS, D, EXPERT_FF), D ** -0.5),
        'we_down': nrm((DEPTH, N_EXPERTS, EXPERT_FF, D), EXPERT_FF ** -0.5),
        'ws_gate': nrm((DEPTH, D, SHARED_FF), D ** -0.5),
        'ws_up': nrm((DEPTH, D, SHARED_FF), D ** -0.5),
        'ws_down': nrm((DEPTH, SHARED_FF, D), SHARED_FF ** -0.5),
        'g_final': gain((D,)),
    }

def reference(x, c, ctx, c_ctx, w_ada, b_ada, g_mix, g_ffn, wa_in, ga_q, ga_kv, wa_uq, wa_ukv,
              wa_sink, wa_out, wc_in, lam_q1, lam_k1, lam_q2, lam_k2, gc_sub, wc_out, w_router,
              b_router, we_gate, we_up, we_down, ws_gate, ws_up, ws_down, g_final):
    b, n, d = x.shape
    n_ctx = ctx.shape[1]
    rows = n // GRID_W
    rope_mla = axial_rope_tables(rows, MLA_ROPE)
    rope_64 = axial_rope_tables(rows, SWA_HEAD_DIM)
    h_lat, h_ctx = x, ctx
    for layer in range(DEPTH):
        last = layer == DEPTH - 1
        mod_l = (jax.nn.silu(c) @ w_ada[layer] + b_ada[layer])[:, None, :]
        mod_c = (jax.nn.silu(c_ctx) @ w_ada[layer] + b_ada[layer])[None, None, :]
        sh_ml, sc_ml, gt_ml, sh_fl, sc_fl, gt_fl = jnp.split(mod_l, 6, axis=-1)
        sh_mc, sc_mc, gt_mc, sh_fc, sc_fc, gt_fc = jnp.split(mod_c, 6, axis=-1)
        a_lat = modulate(rmsnorm(h_lat, g_mix[layer]), sh_ml, sc_ml)
        a_ctx = modulate(rmsnorm(h_ctx, g_mix[layer]), sh_mc, sc_mc)
        if layer % 2 == 0:
            i = layer // 2
            y_lat, y_ctx = even_mixer(a_lat, a_ctx, rope_mla, rope_64, wa_in[i], ga_q[i], ga_kv[i],
                                      wa_uq[i], wa_ukv[i], wa_sink[i], wa_out[i], not last)
        else:
            i = layer // 2
            lam_init = 0.8 - 0.6 * math.exp(-0.3 * layer)
            y_lat, y_ctx = odd_mixer(a_lat, a_ctx, rope_64, wc_in[i], lam_q1[i], lam_k1[i],
                                     lam_q2[i], lam_k2[i], gc_sub[i], wc_out[i], lam_init, not last)
        h_lat = h_lat + gt_ml * y_lat
        f_lat = modulate(rmsnorm(h_lat, g_ffn[layer]), sh_fl, sc_fl).reshape(b * n, d)
        moe_args = (w_router[layer], b_router[layer], we_gate[layer], we_up[layer], we_down[layer],
                    ws_gate[layer], ws_up[layer], ws_down[layer])
        if last:
            y = moe_ffn(f_lat, *moe_args)
            h_lat = h_lat + gt_fl * y.reshape(b, n, d)
        else:
            h_ctx = h_ctx + gt_mc * y_ctx
            f_ctx = modulate(rmsnorm(h_ctx, g_ffn[layer]), sh_fc, sc_fc).reshape(b * n_ctx, d)
            y = moe_ffn(jnp.concatenate([f_lat, f_ctx], axis=0), *moe_args)
            h_lat = h_lat + gt_fl * y[:b * n].reshape(b, n, d)
            h_ctx = h_ctx + gt_fc * y[b * n:].reshape(b, n_ctx, d)
    return rmsnorm(h_lat, g_final)


_drawn_inputs = setup_inputs


def setup_inputs(seed=0):
    import zlib

    import numpy as np

    out = dict(_drawn_inputs(seed))
    spreads = {}
    factors = {'g_mix': 4.177,
     'ga_q': 8.0,
     'ga_kv': 5.122,
     'wa_sink': 8.0,
     'gc_sub': 4.933,
     'g_final': 2.775}
    for name, (base, spread) in spreads.items():
        noise = np.random.default_rng([zlib.crc32(name.encode()), seed]).standard_normal(out[name].shape)
        drawn = base * np.exp(spread * noise) if base else spread * noise
        out[name] = jnp.asarray(drawn.astype(out[name].dtype))
    for name, factor in factors.items():
        out[name] = (out[name] * factor).astype(out[name].dtype)
    return out
```

```python
from contextlib import ExitStack

import numpy as np
import concourse.bass as bass
from concourse import mybir

F32 = mybir.dt.float32
BF16 = mybir.dt.bfloat16
I32 = mybir.dt.int32
U32 = mybir.dt.uint32
ALU = mybir.AluOpType
ACT = mybir.ActivationFunctionType
AX = mybir.AxisListType.X

P = 128
D = 1024
KD = D // P
SEQ, CTX = 512, 256
NL, NT = SEQ // P, (SEQ + CTX) // P
EPS = 1e-6
NEG = -1e30
GRID_W, ROPE_BASE = 64, 10000.0

QR, KVR, ROPE, NOPE, MV, MH = 384, 256, 32, 64, 64, 8
MQ = NOPE + ROPE
SH, SKV, SD = 8, 2, 64
DH, DHALF, DV = 8, 64, 128
DC = 4 * DHALF + DV
LAM_INIT = 0.8 - 0.6 * float(np.exp(-0.3))
EVEN_IN = QR + KVR + ROPE + SH * SD + 2 * SKV * SD

NE, NG, TOPG, TOPK, FF = 64, 8, 4, 8, 256
ROUTED = 2.5
KF = FF // P
MAXBLK = NT * TOPK + NE
TBL = MAXBLK + 4
FAR = 16384

C_ID, C_U, C_ONE, C_MP, C_MN = 0, P, 2 * P, 3 * P, 4 * P
C_IOTA = 5 * P
C_EPS = C_IOTA + 1
C_TOK = C_EPS + 1
C_TRI = C_TOK + NT
C_COS = C_TRI + NG * NG
C_SIN = C_COS + NL * SD
C_COSM = C_SIN + NL * SD
C_SINM = C_COSM + NL * ROPE
C_N = C_SINM + NL * ROPE


def shape_constants():
    c = np.zeros((P, C_N), np.float32)
    p = np.arange(P)
    c[:, C_ID:C_ID + P] = np.eye(P)
    c[:, C_U:C_U + P] = p[:, None] < p[None, :]
    c[:, C_ONE:C_ONE + P] = 1
    c[:, C_MP:C_MP + P] = np.where(p[None, :] >= p[:, None], 0, NEG)
    c[:, C_MN:C_MN + P] = np.where(p[None, :] <= p[:, None], 0, NEG)
    c[:, C_IOTA] = p
    c[:, C_EPS] = EPS
    for t in range(NT):
        c[:, C_TOK + t] = t * P + p
    g = np.arange(NG)
    c[:, C_TRI:C_TRI + NG * NG] = (g[None, :] < g[:, None]).reshape(-1)
    for dim, cc, cs in ((SD, C_COS, C_SIN), (ROPE, C_COSM, C_SINM)):
        half, q = dim // 2, dim // 4
        inv = (np.float32(ROPE_BASE) ** (-np.arange(0, half, 2, dtype=np.float32) / np.float32(half))).astype(np.float32)
        for t in range(NL):
            tok = t * P + p
            r = (tok // GRID_W).astype(np.float32)[:, None] * inv
            w = (tok % GRID_W).astype(np.float32)[:, None] * inv
            c[:, cc + t * dim:cc + (t + 1) * dim] = np.cos(np.concatenate([r, r, w, w], 1))
            s = np.sin(np.concatenate([-r, r, -w, w], 1))
            c[:, cs + t * dim:cs + (t + 1) * dim] = s
    return c


class Chain:

    def __init__(self, eng, sem):
        self.eng, self.sem, self.count = eng, sem, {}

    def __call__(self, ins, sem=None):
        sem = self.sem if sem is None else sem
        self.count[id(sem)] = self.count.get(id(sem), 0) + 1
        ins.then_inc(sem, 1)
        self.eng.wait_ge(sem, self.count[id(sem)])


def build(nc, a, out, stop="end"):
    with ExitStack() as whole:
        def sb(ctx, name, shape, dt=F32, side="left"):
            return ctx.enter_context(nc.sbuf_tensor(name, shape, dt, side=side))

        def ps(ctx, name, shape, dt=F32):
            return ctx.enter_context(nc.psum_tensor(name, shape, dt))

        held = []

        def sem(name):
            held.append(nc.alloc_semaphore(name))
            return held[-1]

        def end_stage():
            nc.clear_and_free_semaphores(held)
            held.clear()
            nc.all_engine_barrier()

        def dram(name, shape, dt=F32):
            return nc.dram_tensor(name, shape, dt, kind="Internal").ap()

        mod_d = dram("mod_d", [2, 2, 6 * D])
        f_d = [dram(f"f_d{l}", [NT * P, D]) for l in range(2)]
        acc_d = [dram(f"acc_d{l}", [(NT + 1) * P, D]) for l in range(2)]
        slot_d = [dram(f"slot_d{l}", [P * TBL, 2], I32) for l in range(2)]
        be_d = [dram(f"be_d{l}", [1, P], I32) for l in range(2)]

        cst = sb(whole, "cst", [P, C_N])
        h = sb(whole, "h", [P, NT, D])
        ident = cst[:, C_ID:C_ID + P]
        eps = cst[:, C_EPS:C_EPS + 1]
        ident_b = sb(whole, "ident_b", [P, P], BF16)
        mask_b = sb(whole, "mask_b", [P, 2, P], BF16)
        nblk_i = sb(whole, "nblk_i", [1, 2], I32)

        def kview(w):
            return w.rearrange("(p k) n -> p k n", p=P)

        def stage_modulation():
            CH, NCH, WB = 512, 6 * D // 512, 3
            with ExitStack() as ctx:
                craw = sb(ctx, "craw", [P, 2, KD])
                cs = sb(ctx, "cs", [P, KD, 2])
                wada = sb(ctx, "wada", [P, WB, KD, CH])
                bias = sb(ctx, "bias", [2, 2, 6 * D])
                row = sb(ctx, "row", [2, 2, 6 * D])
                gains = sb(ctx, "gains", [2, 2, 2, D])
                empty = sb(ctx, "empty", [P, TBL, 2], I32)
                psA = ps(ctx, "psA", [2, 4, CH])
                s_cst, s_c, s_h, s_b = sem("A_cst"), sem("A_c"), sem("A_h"), sem("A_b")
                s_w = [sem(f"A_w{i}") for i in range(WB)]
                s_silu, s_mm, s_ev, s_dve = sem("A_silu"), sem("A_mm"), sem("A_ev"), sem("A_dve")
                s_row, s_mod, s_emp, s_emps = sem("A_row"), sem("A_mod"), sem("A_emp"), sem("A_emps")
                wv = [a["w_ada"][l].rearrange("(p k) n -> p k n", p=P) for l in range(2)]
                with nc.Block() as block:
                    @block.sync
                    def _(sp):
                        sp.dma_start(craw[:, 0, :], a["c"][0].rearrange("(p k) -> p k", p=P)).then_inc(s_c, 16)
                        sp.dma_start(craw[:, 1, :], a["c_ctx"].rearrange("(p k) -> p k", p=P)).then_inc(s_c, 16)
                        for i in range(2 * NCH):
                            if i >= WB:
                                sp.wait_ge(s_mm, i - WB + 1)
                            l, n = i // NCH, i % NCH
                            sp.dma_start(wada[:, i % WB], wv[l][:, :, n * CH:(n + 1) * CH]).then_inc(s_w[i % WB], 16)

                    @block.scalar
                    def _(act):
                        act.dma_start(cst[:], a["cst"]).then_inc(s_cst, 16)
                        for v in range(2):
                            act.dma_start(bias[v:v + 1], a["b_ada"].rearrange("(o l) n -> o l n", o=1)).then_inc(s_b, 16)
                            act.dma_start(gains[v:v + 1, :, 0], a["g_mix"].rearrange("(o l) n -> o l n", o=1)).then_inc(s_b, 16)
                            act.dma_start(gains[v:v + 1, :, 1], a["g_ffn"].rearrange("(o l) n -> o l n", o=1)).then_inc(s_b, 16)
                        act.wait_ge(s_c, 32)
                        for v in range(2):
                            ins = nc.scalar.activation(cs[:, :, v], craw[:, v, :], ACT.Silu)
                        ins.then_inc(s_silu, 1)
                        act.dma_start(h[:, 0:NL], a["x"][0].rearrange("(t p) d -> p t d", p=P)).then_inc(s_h, 16)
                        act.dma_start(h[:, NL:NT], a["ctx"][0].rearrange("(t p) d -> p t d", p=P)).then_inc(s_h, 16)
                        act.wait_ge(s_emp, 2)
                        for l in range(2):
                            act.dma_start(slot_d[l].rearrange("(p b) c -> p (b c)", p=P), empty[:].rearrange("p b c -> p (b c)")).then_inc(s_emps, 16)
                        for l in range(2):
                            act.wait_ge(s_row, l + 1)
                            act.dma_start(mod_d[l], row[:, l]).then_inc(s_mod, 16)
                        act.wait_ge(s_mod, 32)
                        act.wait_ge(s_h, 32)
                        act.wait_ge(s_emps, 32)

                    @block.gpsimd
                    def _(pool):
                        pool.wait_ge(s_cst, 16)
                        nc.gpsimd.tensor_scalar(empty[:, :, 0], cst[:, C_IOTA:C_IOTA + 1].to_broadcast([P, TBL]), float(NT * P), None, ALU.add).then_inc(s_emp, 1)
                        nc.gpsimd.memset(empty[:, :, 1:2], 0).then_inc(s_emp, 1)

                    @block.tensor
                    def _(pe):
                        pe.wait_ge(s_silu, 1)
                        for i in range(2 * NCH):
                            pe.wait_ge(s_w[i % WB], 16 * (i // WB + 1))
                            if i >= 4:
                                pe.wait_ge(s_ev, i - 3)
                            for k in range(KD):
                                ins = nc.tensor.matmul(psA[:, i % 4], cs[:, k], wada[:, i % WB, k], start=(k == 0), stop=(k == KD - 1))
                            ins.then_inc(s_mm, 1)

                    @block.vector
                    def _(dve):
                        link = Chain(dve, s_dve)
                        dve.wait_ge(s_cst, 16)
                        nc.vector.tensor_copy(ident_b[:], ident)
                        nc.vector.tensor_copy(mask_b[:, 0], cst[:, C_MP:C_MP + P])
                        nc.vector.tensor_copy(mask_b[:, 1], cst[:, C_MN:C_MN + P])
                        dve.wait_ge(s_b, 96)
                        for i in range(2 * NCH):
                            l, n = i // NCH, i % NCH
                            j, half = n // 2, n % 2
                            dve.wait_ge(s_mm, i + 1)
                            seg = row[:, l, n * CH:(n + 1) * CH]
                            ins = nc.vector.tensor_tensor(seg, psA[:, i % 4], bias[:, l, n * CH:(n + 1) * CH], ALU.add)
                            ins.then_inc(s_ev, 1)
                            if j % 3 == 1:
                                dve.wait_ge(s_ev, i + 1)
                                ins = nc.vector.scalar_tensor_tensor(seg, seg, 1.0, gains[:, l, j // 3, half * CH:(half + 1) * CH], ALU.add, ALU.mult)
                                link(ins)
                            if n == NCH - 1:
                                dve.wait_ge(s_ev, i + 1)
                                nc.vector.tensor_copy(row[:, l, 0:1], row[:, l, 0:1]).then_inc(s_row, 1)

        def mod_rows(l, v, j):
            return mod_d[l, v:v + 1, j * D:(j + 1) * D].to_broadcast([P, D])

        def rope(dst, src, cos, sin, t1, t2, q, link):
            nc.vector.tensor_tensor(t1, src, cos, ALU.mult)
            s4 = src.rearrange("p g (b two q) -> p g b two q", two=2, q=q)
            t4 = t2.rearrange("p g (b two q) -> p g b two q", two=2, q=q)
            n4 = sin.rearrange("p g (b two q) -> p g b two q", two=2, q=q)
            for b in range(2):
                nc.vector.tensor_tensor(t4[:, :, b, 0], s4[:, :, b, 1], n4[:, :, b, 0], ALU.mult)
                ins = nc.vector.tensor_tensor(t4[:, :, b, 1], s4[:, :, b, 0], n4[:, :, b, 1], ALU.mult)
            link(ins)
            return nc.vector.tensor_tensor(dst, t1, t2, ALU.add)

        def bc(ap, n):
            return ap.unsqueeze(1).to_broadcast([ap.shape[0], n, ap.shape[1]])

        def bcl(ap, n):
            return ap.unsqueeze(len(ap.shape)).to_broadcast(list(ap.shape) + [n])

        def stage_project0(t_):
            qmT, kmT, vM, qsT, ksT, vS = (t_[n] for n in ("qmT", "kmT", "vM", "qsT", "ksT", "vS"))
            with ExitStack() as ctx:
                amul = sb(ctx, "B_amul", [P, D])
                aadd = sb(ctx, "B_aadd", [P, D])
                an = sb(ctx, "B_an", [P, D])
                aT = sb(ctx, "B_aT", [P, KD, P])
                w_in = sb(ctx, "w_in", [P, KD, EVEN_IN])
                w_uq = sb(ctx, "w_uq", [P, QR // P, MH * MQ])
                w_ukv = sb(ctx, "w_ukv", [P, KVR // P, MH * (NOPE + MV)])
                gq = sb(ctx, "B_gq", [P, QR // P])
                gkv = sb(ctx, "B_gkv", [P, KVR // P])
                junk = sb(ctx, "B_junk", [P, D], BF16)
                cn = sb(ctx, "B_cn", [P, QR + KVR])
                cT = sb(ctx, "B_cT", [P, 5, P])
                krr = sb(ctx, "B_krr", [P, ROPE])
                qst = sb(ctx, "B_qst", [P, SH // 2, 2, SD])
                kst = sb(ctx, "B_kst", [P, SKV * SD])
                qm = sb(ctx, "B_qm", [P, MH, MQ])
                km = sb(ctx, "B_km", [P, MH, MQ])
                t1 = sb(ctx, "B_t1", [P, 512])
                t2 = sb(ctx, "B_t2", [P, 512])
                st = sb(ctx, "B_st", [P, 3, 3])
                psC = ps(ctx, "B_psC", [P, 2, 512])
                psT = ps(ctx, "B_psT", [P, 2, KD, P])
                psU = ps(ctx, "B_psU", [P, 1024])
                s_w, s_ab = sem("B_w"), sem("B_ab")
                s_rt, s_an0, s_an = sem("B_rt"), sem("B_an0"), sem("B_an")
                s_tp, s_tev, s_ch, s_chev = sem("B_tp"), sem("B_tev"), sem("B_ch"), sem("B_chev")
                s_ss, s_crt, s_cn = sem("B_ss"), sem("B_crt"), sem("B_cn")
                s_st, s_u, s_uev = sem("B_st_ready"), sem("B_u"), sem("B_uev")
                s_dve, s_act = sem("B_dve"), sem("B_act")
                chunks = [(0, QR), (QR, KVR + ROPE), (QR + KVR + ROPE, SH * SD), (EVEN_IN - 2 * SKV * SD, 2 * SKV * SD)]
                cos = cst[:, C_COS:C_COS + NL * SD].rearrange("p (t d) -> p t d", t=NL)
                sin = cst[:, C_SIN:C_SIN + NL * SD].rearrange("p (t d) -> p t d", t=NL)
                cosm = cst[:, C_COSM:C_COSM + NL * ROPE].rearrange("p (t d) -> p t d", t=NL)
                sinm = cst[:, C_SINM:C_SINM + NL * ROPE].rearrange("p (t d) -> p t d", t=NL)
                uses = []
                for s in range(NT + 1):
                    if s < NT:
                        uses.append(("A", s))
                    if s >= 1:
                        uses += [("QS", s - 1), ("QM", s - 1)]
                    if s < NT:
                        uses.append(("C", s))
                    if s >= 1:
                        uses.append(("KM", s - 1))
                use = {u: n for n, u in enumerate(uses)}

                with nc.Block() as block:
                    @block.sync
                    def _(sp):
                        sp.dma_start(amul[:], mod_rows(0, 0, 1)).then_inc(s_ab, 16)
                        sp.dma_start(aadd[:], mod_rows(0, 0, 0)).then_inc(s_ab, 16)
                        wv = kview(a["wa_in"][0])
                        for c0, n in chunks:
                            sp.dma_start(w_in[:, :, c0:c0 + n], wv[:, :, c0:c0 + n]).then_inc(s_w, 16)
                        sp.dma_start(w_uq[:], kview(a["wa_uq"][0])).then_inc(s_w, 16)
                        sp.dma_start(w_ukv[:], kview(a["wa_ukv"][0])).then_inc(s_w, 16)
                        sp.dma_start(gq[:], a["ga_q"][0].rearrange("(p k) -> p k", p=P)).then_inc(s_w, 16)
                        sp.dma_start(gkv[:], a["ga_kv"][0].rearrange("(p k) -> p k", p=P)).then_inc(s_w, 16)
                        sp.wait_ge(s_an, NL)
                        sp.dma_start(amul[:], mod_rows(0, 1, 1)).then_inc(s_ab, 16)
                        sp.dma_start(aadd[:], mod_rows(0, 1, 0)).then_inc(s_ab, 16)

                    @block.gpsimd
                    def _(pool):
                        for t in range(NT):
                            pool.wait_ge(s_an0, t + 1)
                            nc.gpsimd.tensor_tensor(an[:], an[:], aadd[:], ALU.add).then_inc(s_an, 1)

                    @block.scalar
                    def _(act):
                        link = Chain(act, s_act)

                        def norm(t):
                            if t >= 1:
                                act.wait_ge(s_an0, t)
                            link(nc.scalar.activation(junk[:], h[:, t], ACT.Square, accum_out=st[:, 0, 0:1]))
                            nc.scalar.activation(st[:, 0, 1:2], st[:, 0, 0:1], ACT.Sqrt, bias=eps, scale=1.0 / D).then_inc(s_rt, 1)

                        def root_c(t):
                            act.wait_ge(s_ss, 2 * t + 2)
                            nc.scalar.activation(st[:, 1, 1:2], st[:, 1, 0:1], ACT.Sqrt, bias=eps, scale=1.0 / QR)
                            nc.scalar.activation(st[:, 2, 1:2], st[:, 2, 0:1], ACT.Sqrt, bias=eps, scale=1.0 / KVR).then_inc(s_crt, 1)

                        def evac(kind, t):
                            n = use[kind, t]
                            act.wait_ge(s_tp, n + 1)
                            src = psT[:, n % 2]
                            tok = slice(t * P, (t + 1) * P)
                            if kind == "A":
                                ins = nc.scalar.activation(aT[:], src, ACT.Copy)
                            elif kind == "C":
                                for k in range(3):
                                    nc.scalar.activation(cT[:, k], src[:, k], ACT.Copy, scale=gq[:, k:k + 1])
                                for k in range(2):
                                    ins = nc.scalar.activation(cT[:, 3 + k], src[:, 3 + k], ACT.Copy, scale=gkv[:, k:k + 1])
                            elif kind == "QS":
                                nc.scalar.activation(qsT[:, :, tok], src[:, 0:4], ACT.Copy, scale=float(SD) ** -0.5)
                                ins = nc.scalar.activation(ksT[:, tok], src[:, 4], ACT.Copy)
                            elif kind == "QM":
                                ins = nc.scalar.activation(qmT[:, :, tok], src[0:MQ], ACT.Copy, scale=float(MQ) ** -0.5)
                            else:
                                ins = nc.scalar.activation(kmT[:, :, tok], src[0:MQ], ACT.Copy)
                            ins.then_inc(s_tev, 1)

                        norm(0)
                        act.wait_ge(s_w, 16 * 8)
                        for s in range(NT + 1):
                            if s < NT:
                                evac("A", s)
                            if s + 1 < NT:
                                norm(s + 1)
                            if s >= 1:
                                evac("QS", s - 1)
                            if s < NT:
                                root_c(s)
                            if s >= 1:
                                evac("QM", s - 1)
                            if s < NT:
                                evac("C", s)
                            if s >= 1:
                                evac("KM", s - 1)

                    @block.vector
                    def _(dve):
                        link = Chain(dve, s_dve)

                        def norm(t):
                            dve.wait_ge(s_rt, t + 1)
                            link(nc.vector.reciprocal(st[:, 0, 2:3], st[:, 0, 1:2]))
                            dve.wait_ge(s_ab, 32 if t < NL else 64)
                            if t >= 1:
                                dve.wait_ge(s_ch, 4 * (t - 1) + 1)
                            nc.vector.scalar_tensor_tensor(an[:], h[:, t], st[:, 0, 2:3], amul[:], ALU.mult, ALU.mult).then_inc(s_an0, 1)

                        def chunk(t, c):
                            g = 4 * t + c
                            dve.wait_ge(s_ch, g + 1)
                            src = psC[:, g % 2]
                            lat = t < NL
                            if c < 2:
                                n, o = (QR, 0) if c == 0 else (KVR, QR)
                                if c == 0 and t >= 1:
                                    dve.wait_ge(s_tp, use["C", t - 1] + 1)
                                ins = nc.vector.tensor_copy(cn[:, o:o + n], src[:, 0:n])
                                if c == 1:
                                    if lat:
                                        link(ins)
                                        v = lambda x: x.rearrange("p (g d) -> p g d", g=1)
                                        ins = rope(v(krr[:]), v(src[:, n:n + ROPE]), v(cosm[:, t]), v(sinm[:, t]),
                                                   v(t1[:, 0:ROPE]), v(t2[:, 0:ROPE]), ROPE // 4, link)
                                    else:
                                        link(ins)
                                        ins = nc.vector.tensor_copy(krr[:], src[:, n:n + ROPE])
                                link(ins, s_chev)
                                link(nc.vector.tensor_tensor_reduce(t1[:, 0:n], cn[:, o:o + n], cn[:, o:o + n], 1.0, 0.0,
                                                                    ALU.mult, ALU.add, st[:, 1 + c, 0:1]), s_ss)
                            elif c == 2:
                                if t >= 1:
                                    dve.wait_ge(s_tp, use["QS", t - 1] + 1)
                                o = qst[:].rearrange("p j g d -> p g j d")
                                if lat:
                                    heads = src.rearrange("p (h d) -> p h d", d=SD)
                                    tt1 = t1[:].rearrange("p (h d) -> p h d", d=SD)
                                    tt2 = t2[:].rearrange("p (h d) -> p h d", d=SD)
                                    ins = rope_into(o, heads, t, tt1, tt2, link)
                                else:
                                    ins = nc.vector.tensor_copy(o, src.rearrange("p (g j d) -> p g j d", g=2, d=SD))
                                link(ins, s_chev)
                            else:
                                n = SKV * SD
                                if lat:
                                    v = lambda x: x.rearrange("p (h d) -> p h d", d=SD)
                                    link(rope(v(kst[:]), v(src[:, 0:n]), bc(cos[:, t], SKV), bc(sin[:, t], SKV),
                                              v(t1[:, 0:n]), v(t2[:, 0:n]), SD // 4, link))
                                else:
                                    nc.vector.tensor_copy(kst[:], src[:, 0:n])
                                link(nc.vector.tensor_copy(vS[:, t], src[:, n:2 * n]), s_chev)

                        def rope_into(o, heads, t, tt1, tt2, link):
                            nc.vector.tensor_tensor(tt1, heads, bc(cos[:, t], SH), ALU.mult)
                            q = SD // 4
                            s4 = heads.rearrange("p g (b two q) -> p g b two q", two=2, q=q)
                            t4 = tt2.rearrange("p g (b two q) -> p g b two q", two=2, q=q)
                            n4 = bc(sin[:, t], SH).rearrange("p g (b two q) -> p g b two q", two=2, q=q)
                            for b in range(2):
                                nc.vector.tensor_tensor(t4[:, :, b, 0], s4[:, :, b, 1], n4[:, :, b, 0], ALU.mult)
                                ins = nc.vector.tensor_tensor(t4[:, :, b, 1], s4[:, :, b, 0], n4[:, :, b, 1], ALU.mult)
                            link(ins)
                            g4 = lambda x: x.rearrange("p (g j) d -> p g j d", g=2)
                            return nc.vector.tensor_tensor(o, g4(tt1), g4(tt2), ALU.add)

                        def scale_c(t):
                            dve.wait_ge(s_crt, t + 1)
                            link(nc.vector.reciprocal(st[:, 1:3, 2], st[:, 1:3, 1]))
                            nc.vector.tensor_scalar(cn[:, 0:QR], cn[:, 0:QR], st[:, 1, 2:3], None, ALU.mult)
                            link(nc.vector.tensor_scalar(cn[:, QR:], cn[:, QR:], st[:, 2, 2:3], None, ALU.mult), s_cn)

                        def up_q(t):
                            dve.wait_ge(s_u, 2 * t + 1)
                            if t >= 1:
                                dve.wait_ge(s_tp, use["QM", t - 1] + 1)
                            src = psU[:, 0:MH * MQ].rearrange("p (h d) -> p h d", d=MQ)
                            ins = nc.vector.tensor_copy(qm[:, :, 0:NOPE], src[:, :, 0:NOPE])
                            r = src[:, :, NOPE:MQ]
                            if t < NL:
                                v = lambda x: x[:, 0:MH * ROPE].rearrange("p (h d) -> p h d", d=ROPE)
                                link(ins)
                                ins = rope(qm[:, :, NOPE:MQ], r, bc(cosm[:, t], MH), bc(sinm[:, t], MH), v(t1), v(t2), ROPE // 4, link)
                            else:
                                ins = nc.vector.tensor_copy(qm[:, :, NOPE:MQ], r)
                            link(ins, s_uev)

                        def up_kv(t):
                            dve.wait_ge(s_u, 2 * t + 2)
                            if t >= 1:
                                dve.wait_ge(s_tp, use["KM", t - 1] + 1)
                            src = psU[:].rearrange("p (h d) -> p h d", d=NOPE + MV)
                            nc.vector.tensor_copy(km[:, :, NOPE:MQ], bc(krr[:], MH))
                            nc.vector.tensor_copy(km[:, :, 0:NOPE], src[:, :, 0:NOPE])
                            link(nc.vector.tensor_copy(vM[:, t].rearrange("p (h d) -> p h d", d=MV), src[:, :, NOPE:]), s_uev)

                        norm(0)
                        for s in range(NT + 1):
                            if s >= 1:
                                up_kv(s - 1)
                            if s < NT:
                                chunk(s, 0)
                                chunk(s, 1)
                                scale_c(s)
                                if s + 1 < NT:
                                    norm(s + 1)
                                chunk(s, 2)
                                chunk(s, 3)
                                up_q(s)

                    @block.tensor
                    def _(pe):
                        def turn(kind, t):
                            n = use[kind, t]
                            if n >= 2:
                                pe.wait_ge(s_tev, n - 1)
                            dst = psT[:, n % 2]
                            if kind == "A":
                                pe.wait_ge(s_an, t + 1)
                                v = an[:].rearrange("q (p k) -> q k p", k=KD)
                                for k in range(KD):
                                    ins = nc.tensor.transpose(dst[:, k], v[:, k], ident)
                            elif kind == "C":
                                pe.wait_ge(s_cn, t + 1)
                                v = cn[:, 0:QR].rearrange("q (p k) -> q k p", k=3)
                                for k in range(3):
                                    nc.tensor.transpose(dst[:, k], v[:, k], ident)
                                v = cn[:, QR:].rearrange("q (p k) -> q k p", k=2)
                                for k in range(2):
                                    ins = nc.tensor.transpose(dst[:, 3 + k], v[:, k], ident)
                            elif kind == "QS":
                                pe.wait_ge(s_chev, 4 * t + 4)
                                for j in range(SH // 2):
                                    nc.tensor.transpose(dst[:, j], qst[:, j].rearrange("p g d -> p (g d)"), ident)
                                ins = nc.tensor.transpose(dst[:, 4], kst[:], ident)
                            else:
                                pe.wait_ge(s_uev, 2 * t + (1 if kind == "QM" else 2))
                                x = qm if kind == "QM" else km
                                for i in range(MH):
                                    ins = nc.tensor.transpose(dst[0:MQ, i], x[:, i], ident)
                            ins.then_inc(s_tp, 1)

                        def chunk(t, c):
                            g = 4 * t + c
                            if g >= 2:
                                pe.wait_ge(s_chev, g - 1)
                            if c == 0:
                                pe.wait_ge(s_tev, use["A", t] + 1)
                            c0, n = chunks[c]
                            for k in range(KD):
                                ins = nc.tensor.matmul(psC[:, g % 2, 0:n], aT[:, k], w_in[:, k, c0:c0 + n], start=(k == 0), stop=(k == KD - 1))
                            ins.then_inc(s_ch, 1)

                        def up(t, i):
                            n = 2 * t + i
                            if n >= 1:
                                pe.wait_ge(s_uev, n)
                            if i == 0:
                                pe.wait_ge(s_tev, use["C", t] + 1)
                            w, k0, nk, cols = (w_uq, 0, 3, MH * MQ) if i == 0 else (w_ukv, 3, 2, MH * (NOPE + MV))
                            for c0 in range(0, cols, 512):
                                c1 = min(c0 + 512, cols)
                                for k in range(nk):
                                    ins = nc.tensor.matmul(psU[:, c0:c1], cT[:, k0 + k], w[:, k, c0:c1], start=(k == 0), stop=(k == nk - 1))
                            ins.then_inc(s_u, 1)

                        pe.wait_ge(s_w, 16 * 8)
                        for s in range(NT + 1):
                            if s < NT:
                                turn("A", s)
                            if s >= 1:
                                up(s - 1, 1)
                            if s < NT:
                                chunk(s, 0)
                            if s >= 1:
                                turn("QS", s - 1)
                            if s < NT:
                                chunk(s, 1)
                            if s >= 1:
                                turn("QM", s - 1)
                            if s < NT:
                                chunk(s, 2)
                                turn("C", s)
                            if s >= 1:
                                turn("KM", s - 1)
                            if s < NT:
                                chunk(s, 3)
                                up(s, 0)

        def stage_attend0(t_, o):
            qmT, kmT, vM, qsT, ksT, vS = (t_[n] for n in ("qmT", "kmT", "vM", "qsT", "ksT", "vS"))
            units = [(t, kind, hd) for t in range(NT) for kind in range(2) for hd in range(8)]
            N = len(units)

            def keys(t, kind):
                lat = [] if t >= NL else list(range(NL)) if kind == 0 else list(range(max(0, t - 1), min(NL, t + 2)))
                return lat + list(range(NL, NT)), 512 - P * len(lat)

            with ExitStack() as ctx:
                prob = sb(ctx, "C_prob", [P, 3, NT * P])
                pT = sb(ctx, "C_pT", [P, 2, NT, P])
                sink = sb(ctx, "C_sink", [P, 8])
                nsink = sb(ctx, "C_nsink", [P, 8])
                nmax = sb(ctx, "C_nmax", [P, 2 * NT, 8])
                ssum = sb(ctx, "C_ssum", [P, 2 * NT, 8])
                sdif = sb(ctx, "C_sdif", [P, 2, 8])
                psS = ps(ctx, "C_psS", [P, 2, 1024])
                psP = ps(ctx, "C_psP", [P, 2, 4, P])
                psO = ps(ctx, "C_psO", [P, 2, 512])
                s_sink, s_s, s_nm, s_e = sem("C_sink_in"), sem("C_s"), sem("C_nm"), sem("C_e")
                s_t, s_pv, s_evd, s_eva = sem("C_t"), sem("C_pv"), sem("C_evd"), sem("C_eva")
                s_sd, s_se, s_o, s_dve, s_act = sem("C_sd"), sem("C_se"), sem("C_o"), sem("C_dve"), sem("C_act")

                def place(n, b):
                    first = (n + 1) // 2
                    return (0, b) if b < first else (1, b - first)

                with nc.Block() as block:
                    @block.sync
                    def _(sp):
                        sp.dma_start(sink[:], a["wa_sink"][0:1, :].to_broadcast([P, 8])).then_inc(s_sink, 16)

                    @block.tensor
                    def _(pe):
                        def scores(i):
                            t, kind, hd = units[i]
                            if i >= 2:
                                pe.wait_ge(s_e, i - 1)
                            ks, c0 = keys(t, kind)
                            if kind == 0:
                                q, kT = qmT[:, hd, t * P:(t + 1) * P], kmT[:, hd]
                            else:
                                g, j = divmod(hd, SH // SKV)
                                q, kT = qsT[64 * g:64 * g + 64, j, t * P:(t + 1) * P], ksT[64 * g:64 * g + 64]
                            masks = []
                            if kind == 1 and t < NL:
                                masks = [(c0 + n * P, 0 if k < t else 1) for n, k in enumerate(ks) if k < NL and k != t]
                            if c0 < 512:
                                nc.tensor.matmul(psS[:, i % 2, c0:512], q, kT[:, ks[0] * P:ks[0] * P + 512 - c0], start=True, stop=not masks)
                            for n, (c, m) in enumerate(masks):
                                nc.tensor.matmul(psS[:, i % 2, c:c + P], ident_b[:], mask_b[:, m], start=False, stop=n == len(masks) - 1)
                            nc.tensor.matmul(psS[:, i % 2, 512:512 + CTX], q, kT[:, SEQ:], start=True, stop=True).then_inc(s_s, 1)

                        def turn(i):
                            t, kind, hd = units[i]
                            pe.wait_ge(s_e, i + 1)
                            if i >= 1:
                                pe.wait_ge(s_evd, i)
                                pe.wait_ge(s_eva, i)
                            n = len(keys(t, kind)[0])
                            for b in range(n):
                                bank, c = place(n, b)
                                ins = nc.tensor.transpose(psP[:, bank, c], prob[:, i % 3, b * P:(b + 1) * P], ident)
                            ins.then_inc(s_t, 1)

                        def values(i):
                            t, kind, hd = units[i]
                            pe.wait_ge(s_evd, i + 1)
                            pe.wait_ge(s_eva, i + 1)
                            g = i // 8
                            if i % 8 == 0 and g >= 2:
                                pe.wait_ge(s_o, g - 1)
                            ks, _ = keys(t, kind)
                            for n, k in enumerate(ks):
                                v = vM[:, k, hd * MV:(hd + 1) * MV] if kind == 0 else vS[:, k, hd // 4 * SD:hd // 4 * SD + SD]
                                ins = nc.tensor.matmul(psO[:, g % 2, hd * 64:(hd + 1) * 64], pT[:, i % 2, n], v, start=(n == 0), stop=(n == len(ks) - 1))
                            ins.then_inc(s_pv, 1)

                        for i in range(N + 3):
                            if i < N:
                                scores(i)
                            if 2 <= i < N + 2:
                                turn(i - 2)
                            if i >= 3:
                                values(i - 3)

                    @block.vector
                    def _(dve):
                        link = Chain(dve, s_dve)
                        dve.wait_ge(s_sink, 16)
                        link(nc.vector.tensor_scalar(nsink[:], sink[:], -1.0, None, ALU.mult))

                        def maximum(i):
                            t, kind, hd = units[i]
                            g = i // 8
                            dve.wait_ge(s_s, i + 1)
                            ks, c0 = keys(t, kind)
                            m = nmax[:, g, hd:hd + 1]
                            ins = nc.vector.tensor_reduce(m, psS[:, i % 2, c0:512 + CTX], AX, ALU.max, negate=True)
                            if kind == 1:
                                link(ins)
                                ins = nc.vector.tensor_tensor(m, m, nsink[:, hd:hd + 1], ALU.min)
                            link(ins, s_nm)

                        def evac(i):
                            n = len(keys(*units[i][:2])[0])
                            dve.wait_ge(s_t, i + 1)
                            if i >= 2:
                                dve.wait_ge(s_pv, i - 1)
                            f = (n + 1) // 2
                            nc.vector.tensor_copy(pT[:, i % 2, 0:f], psP[:, 0, 0:f]).then_inc(s_evd, 1)

                        def divide(g):
                            t, kind = g // 2, g % 2
                            sl = ssum[:, g]
                            if kind == 1:
                                dve.wait_ge(s_se, t + 1)
                                link(nc.vector.tensor_tensor(sl, sl, sdif[:, t % 2], ALU.add))
                            else:
                                dve.wait_ge(s_e, 8 * g + 8)
                            link(nc.vector.reciprocal(sl, sl))
                            dve.wait_ge(s_pv, 8 * g + 8)
                            nc.vector.tensor_tensor(o[:, t, kind * 512:(kind + 1) * 512].rearrange("p (h d) -> p h d", d=64),
                                                    psO[:, g % 2].rearrange("p (h d) -> p h d", d=64), bcl(sl, 64), ALU.mult).then_inc(s_o, 1)

                        for i in range(N + 4):
                            if i < N:
                                maximum(i)
                            if 2 <= i < N + 2:
                                evac(i - 2)
                            if i % 8 == 1 and i > 8 and (i // 8 - 1) % 2 == 1:
                                g = i // 8 - 1
                                if g // 2 >= 2:
                                    dve.wait_ge(s_se, g // 2 - 1)
                                link(nc.vector.tensor_tensor(sdif[:, g // 2 % 2], sink[:], nmax[:, g], ALU.add), s_sd)
                            if i >= 11 and (i - 11) % 8 == 0:
                                divide((i - 11) // 8)

                    @block.scalar
                    def _(act):
                        link = Chain(act, s_act)
                        for i in range(N + 4):
                            if i < N:
                                t, kind, hd = units[i]
                                ks, c0 = keys(t, kind)
                                act.wait_ge(s_nm, i + 1)
                                if i >= 3:
                                    act.wait_ge(s_t, i - 2)
                                g = i // 8
                                nc.scalar.activation(prob[:, i % 3, 0:len(ks) * P], psS[:, i % 2, c0:512 + CTX], ACT.Exp,
                                                     bias=nmax[:, g, hd:hd + 1], accum_out=ssum[:, g, hd:hd + 1]).then_inc(s_e, 1)
                            if 2 <= i < N + 2:
                                j = i - 2
                                n = len(keys(*units[j][:2])[0])
                                f = (n + 1) // 2
                                act.wait_ge(s_t, j + 1)
                                if j >= 2:
                                    act.wait_ge(s_pv, j - 1)
                                nc.scalar.activation(pT[:, j % 2, f:n], psP[:, 1, 0:n - f], ACT.Copy).then_inc(s_eva, 1)
                            if i % 8 == 1 and i > 8 and (i // 8 - 1) % 2 == 1:
                                g = i // 8 - 1
                                act.wait_ge(s_sd, g // 2 + 1)
                                nc.scalar.activation(sdif[:, g // 2 % 2], sdif[:, g // 2 % 2], ACT.Exp).then_inc(s_se, 1)

        def stage_out(l, nt, o, fT, lg, w_out_in, gain_in):
            with ExitStack() as ctx:
                w_out = sb(ctx, f"D{l}_w", [P, KD, D])
                w_r = sb(ctx, f"D{l}_wr", [P, KD, NE])
                gsub = sb(ctx, f"D{l}_gs", [P, 1])
                gate = sb(ctx, f"D{l}_gate", [P, 2, D])
                fmul = sb(ctx, f"D{l}_fmul", [P, 2, D])
                fadd = sb(ctx, f"D{l}_fadd", [P, 2, D])
                oT = sb(ctx, f"D{l}_oT", [P, 2, KD, P])
                y = sb(ctx, f"D{l}_y", [P, D])
                f = sb(ctx, f"D{l}_f", [P, 2, D])
                junk = sb(ctx, f"D{l}_junk", [P, D], BF16)
                st = sb(ctx, f"D{l}_st", [P, 3])
                psT = ps(ctx, f"D{l}_psT", [P, 2, KD, P])
                psY = ps(ctx, f"D{l}_psY", [P, 2, 512])
                psR = ps(ctx, f"D{l}_psR", [P, 512])
                S = lambda n: sem(f"D{l}_{n}_s")
                s_w, s_v, s_to, s_oT, s_y, s_yev, s_h = S("w"), S("v"), S("to"), S("oT"), S("y"), S("yev"), S("h")
                s_rt, s_f0, s_f, s_r, s_lg, s_act, s_dve = S("rt"), S("f0"), S("f"), S("r"), S("lg"), S("act"), S("dve")
                s_fd = [S("fd0"), S("fd1")]
                nv = 2 if nt > NL else 1

                uses = [("O", 0)]
                for t in range(nt + 1):
                    if t + 1 < nt:
                        uses.append(("O", t + 1))
                    if t >= 1:
                        uses.append(("F", t - 1))
                use = {u: n for n, u in enumerate(uses)}

                with nc.Block() as block:
                    @block.sync
                    def _(sp):
                        sp.dma_start(w_out[:], w_out_in.rearrange("(k p) n -> p k n", p=P)).then_inc(s_w, 16)
                        sp.dma_start(w_r[:], kview(a["w_router"][l])).then_inc(s_w, 16)
                        for t in range(nt):
                            sp.wait_ge(s_f, t + 1)
                            sp.dma_start(f_d[l][t * P:(t + 1) * P], f[:, t % 2]).then_inc(s_fd[t % 2], 16)
                        for b in range(2):
                            sp.wait_ge(s_fd[b], 16 * ((nt - b + 1) // 2))

                    @block.scalar
                    def _(act):
                        link = Chain(act, s_act)
                        for v in range(nv):
                            act.dma_start(gate[:, v], mod_rows(l, v, 2)).then_inc(s_v, 16)
                            act.dma_start(fmul[:, v], mod_rows(l, v, 4)).then_inc(s_v, 16)
                            act.dma_start(fadd[:, v], mod_rows(l, v, 3)).then_inc(s_v, 16)
                        if gain_in is not None:
                            act.dma_start(gsub[:], gain_in.rearrange("(p o) -> p o", o=1)).then_inc(s_v, 16)
                            act.wait_ge(s_v, 16 * (3 * nv + 1))
                            link(nc.scalar.mul(gsub[:], gsub[:], 1.0 - LAM_INIT))

                        def evac(kind, t):
                            n = use[kind, t]
                            act.wait_ge(s_to, n + 1)
                            if kind == "O":
                                for b in range(2):
                                    sl = slice(4 * b, 4 * b + 4)
                                    ins = nc.scalar.activation(oT[:, t % 2, sl], psT[:, n % 2, sl], ACT.Copy, scale=1.0 if gain_in is None else gsub[:, 0:1])
                            else:
                                ins = nc.scalar.activation(fT[:, :, t * P:(t + 1) * P], psT[:, n % 2], ACT.Copy)
                            ins.then_inc(s_oT, 1)

                        def norm(t):
                            act.wait_ge(s_h, t + 1)
                            if t >= 1:
                                act.wait_ge(s_f0, t)
                            link(nc.scalar.activation(junk[:], h[:, t], ACT.Square, accum_out=st[:, 0:1]))
                            nc.scalar.activation(st[:, 1:2], st[:, 0:1], ACT.Sqrt, bias=eps, scale=1.0 / D).then_inc(s_rt, 1)

                        evac("O", 0)
                        for t in range(nt + 1):
                            if t + 1 < nt:
                                evac("O", t + 1)
                            if t >= 1:
                                evac("F", t - 1)
                            if t < nt:
                                norm(t)

                    @block.vector
                    def _(dve):
                        link = Chain(dve, s_dve)
                        dve.wait_ge(s_v, 16 * (3 * nv + (gain_in is not None)))

                        def logits(t):
                            dve.wait_ge(s_r, t + 1)
                            nc.vector.tensor_copy(lg[:, t], psR[:, 0:NE]).then_inc(s_lg, 1)

                        for t in range(nt):
                            v = 0 if t < NL else 1
                            dve.wait_ge(s_y, t + 1)
                            if t >= 1:
                                dve.wait_ge(s_h, t)
                            for b in range(2):
                                sl = slice(512 * b, 512 * b + 512)
                                ins = nc.vector.tensor_tensor(y[:, sl], psY[:, b], gate[:, v, sl], ALU.mult)
                            ins.then_inc(s_yev, 1)
                            if t >= 1:
                                logits(t - 1)
                            dve.wait_ge(s_rt, t + 1)
                            link(nc.vector.reciprocal(st[:, 2:3], st[:, 1:2]))
                            if t >= 2:
                                dve.wait_ge(s_fd[t % 2], 16 * (t // 2))
                                dve.wait_ge(s_to, use["F", t - 2] + 1)
                            nc.vector.scalar_tensor_tensor(f[:, t % 2], h[:, t], st[:, 2:3], fmul[:, v], ALU.mult, ALU.mult).then_inc(s_f0, 1)
                        logits(nt - 1)

                    @block.gpsimd
                    def _(pool):
                        for t in range(nt):
                            v = 0 if t < NL else 1
                            pool.wait_ge(s_yev, t + 1)
                            nc.gpsimd.tensor_tensor(h[:, t], h[:, t], y[:], ALU.add).then_inc(s_h, 1)
                            pool.wait_ge(s_f0, t + 1)
                            nc.gpsimd.tensor_tensor(f[:, t % 2], f[:, t % 2], fadd[:, v], ALU.add).then_inc(s_f, 1)

                    @block.tensor
                    def _(pe):
                        def turn(kind, t):
                            n = use[kind, t]
                            if n >= 2:
                                pe.wait_ge(s_oT, n - 1)
                            if kind == "F":
                                pe.wait_ge(s_f, t + 1)
                                v = f[:, t % 2].rearrange("q (p k) -> q k p", k=KD)
                            else:
                                v = o[:, t].rearrange("q (k p) -> q k p", p=P)
                            for k in range(KD):
                                ins = nc.tensor.transpose(psT[:, n % 2, k], v[:, k], ident)
                            ins.then_inc(s_to, 1)

                        turn("O", 0)
                        pe.wait_ge(s_w, 32)
                        for t in range(nt + 1):
                            if t + 1 < nt:
                                turn("O", t + 1)
                            if t < nt:
                                pe.wait_ge(s_oT, use["O", t] + 1)
                                if t >= 1:
                                    pe.wait_ge(s_yev, t)
                                for b in range(2):
                                    for k in range(KD):
                                        ins = nc.tensor.matmul(psY[:, b], oT[:, t % 2, k], w_out[:, k, b * 512:(b + 1) * 512], start=(k == 0), stop=(k == KD - 1))
                                ins.then_inc(s_y, 1)
                            if t >= 1:
                                turn("F", t - 1)
                                pe.wait_ge(s_oT, use["F", t - 1] + 1)
                                if t >= 2:
                                    pe.wait_ge(s_lg, t - 1)
                                for k in range(KD):
                                    ins = nc.tensor.matmul(psR[:, 0:NE], fT[:, k, (t - 1) * P:t * P], w_r[:, k], start=(k == 0), stop=(k == KD - 1))
                                ins.then_inc(s_r, 1)

        def stage_route(l, nt, fT, lg):
            NB8 = nt * TOPK
            with ExitStack() as ctx:
                S = lambda n: sem(f"E{l}_{n}_s")
                T = lambda n, shape, dt=F32: sb(ctx, f"E{l}_{n}", shape, dt)
                wgu = T("wgu", [P, 2, KD, FF])
                wd = T("wd", [P, KF, D])
                sg = T("sg", [P, 2, FF])
                up = T("up", [P, 2, FF])
                hT = T("hT", [P, 2, KF, P])
                ysh = T("ysh", [P, 2, D])
                brt = T("brt", [P, NE])
                sc = T("sc", [P, nt, NE])
                bi = T("bi", [P, nt, NE])
                srt = T("srt", [P, nt * NG, 8])
                gs = T("gs", [P, nt, NG])
                cmp1 = T("cmp1", [P, nt, NG, NG])
                cmp2 = T("cmp2", [P, nt, NG, NG])
                gm = T("gm", [P, nt * NG])
                rep = T("rep", [P, nt, NE])
                top8 = T("top8", [P, nt, 8])
                sel = T("sel", [P, nt, NE])
                wt = T("wt", [P, nt, NE])
                tot = T("tot", [P, nt])
                nb = T("nb", [P, NE])
                bend = T("bend", [P, NE])
                bst = T("bst", [P, NE])
                v = T("v", [P, nt, NE])
                v8 = T("v8", [P, nt, 8])
                w8 = T("w8", [P, nt, 8])
                eq = T("eq", [P, nt, 8, NE])
                d8 = T("d8", [P, NB8], I32)
                d8p = T("d8p", [P, NB8], I32)
                d8b = T("d8b", [P, NB8], I32)
                dest = T("dest", [P, NB8], I32)
                pay = T("pay", [P, NB8, 2], I32)
                bei = T("bei", [P, 1], I32)
                bef = T("bef", [P, 1])
                zero = T("zero", [P, D])
                ones = cst[:, C_ONE:C_ONE + P]
                upper = cst[:, C_U:C_U + P]
                psG = ps(ctx, f"E{l}_psG", [P, 2, 512])
                psH = ps(ctx, f"E{l}_psH", [P, 4, P])
                psY = ps(ctx, f"E{l}_psY", [P, 2, 512])
                psK = ps(ctx, f"E{l}_psK", [P, 512])
                psN = ps(ctx, f"E{l}_psN", [P, 512])
                s_w, s_br, s_sig = S("w"), S("br"), S("sig")
                s_gu, s_gc, s_hm, s_ht, s_hT, s_dn, s_ys = S("gu"), S("gc"), S("hm"), S("ht"), S("hT"), S("dn"), S("ys")
                s_yd = [S("yd0"), S("yd1")]
                s_sel, s_rk, s_tab, s_scat, s_bed, s_dve, s_nb, s_z, s_zd = S("sel"), S("rk"), S("tab"), S("scat"), S("bed"), S("dve"), S("nb"), S("z"), S("zd")
                POOLT = min(3, nt - 1)

                with nc.Block() as block:
                    @block.sync
                    def _(sp):
                        sp.dma_start(brt[:], a["b_router"][l:l + 1, :].to_broadcast([P, NE])).then_inc(s_br, 16)
                        sp.dma_start(wgu[:, 0], kview(a["ws_gate"][l])).then_inc(s_w, 16)
                        sp.dma_start(wgu[:, 1], kview(a["ws_up"][l])).then_inc(s_w, 16)
                        sp.dma_start(wd[:], kview(a["ws_down"][l])).then_inc(s_w, 16)
                        sp.wait_ge(s_z, 1)
                        sp.dma_start(acc_d[l][NT * P:], zero[:]).then_inc(s_zd, 16)
                        for t in range(nt):
                            sp.wait_ge(s_ys, t + 1)
                            sp.dma_start(acc_d[l][t * P:(t + 1) * P], ysh[:, t % 2]).then_inc(s_yd[t % 2], 16)
                        sp.wait_ge(s_tab, 1)
                        sp.dma_start(be_d[l].rearrange("o p -> p o"), bei[:]).then_inc(s_bed, 16)
                        for b in range(2):
                            sp.wait_ge(s_yd[b], 16 * ((nt - b + 1) // 2))
                        sp.wait_ge(s_bed, 16)
                        sp.wait_ge(s_zd, 16)

                    @block.tensor
                    def _(pe):
                        def gate_up(t):
                            for k in range(KD):
                                ins = nc.tensor.matmul(psG[:, t % 2].rearrange("p (v f) -> p v f", v=2), fT[:, k, t * P:(t + 1) * P], wgu[:, :, k],
                                                       start=(k == 0), stop=(k == KD - 1))
                            ins.then_inc(s_gu, 1)

                        def turn(t):
                            pe.wait_ge(s_hm, t + 1)
                            if t >= 1:
                                pe.wait_ge(s_hT, t)
                            x = up[:, t % 2].rearrange("q (p k) -> q k p", k=KF)
                            for k in range(KF):
                                ins = nc.tensor.transpose(psH[:, k], x[:, k], ident)
                            ins.then_inc(s_ht, 1)

                        def down(t):
                            pe.wait_ge(s_hT, t + 1)
                            if t >= 1:
                                pe.wait_ge(s_ys, t)
                            for b in range(2):
                                for k in range(KF):
                                    ins = nc.tensor.matmul(psY[:, b], hT[:, t % 2, k], wd[:, k, b * 512:(b + 1) * 512], start=(k == 0), stop=(k == KF - 1))
                            ins.then_inc(s_dn, 1)

                        def ranks():
                            pe.wait_ge(s_sel, 1)
                            for t in range(nt):
                                for j in range(t + 1):
                                    nc.tensor.matmul(psK[:, t * NE:(t + 1) * NE], upper if j == t else ones, sel[:, j], start=(j == 0), stop=(j == t))
                            for j in range(nt):
                                ins = nc.tensor.matmul(psN[:, 0:NE], ones, sel[:, j], start=(j == 0), stop=(j == nt - 1))
                            ins.then_inc(s_rk, 1)

                        pe.wait_ge(s_w, 48)
                        gate_up(0)
                        for t in range(nt):
                            if t + 1 < nt:
                                if t + 1 == POOLT:
                                    ranks()
                                gate_up(t + 1)
                            turn(t)
                            down(t)

                    @block.scalar
                    def _(act):
                        nc.scalar.activation(sc[:], lg[:, 0:nt], ACT.Sigmoid).then_inc(s_sig, 1)

                        def copies(t):
                            act.wait_ge(s_gu, t + 1)
                            if t >= 2:
                                act.wait_ge(s_ht, t - 1)
                            nc.scalar.activation(sg[:, t % 2], psG[:, t % 2, 0:FF], ACT.Silu)
                            nc.scalar.activation(up[:, t % 2], psG[:, t % 2, FF:2 * FF], ACT.Copy).then_inc(s_gc, 1)

                        copies(0)
                        for t in range(nt):
                            if t + 1 < nt:
                                copies(t + 1)
                            act.wait_ge(s_ht, t + 1)
                            nc.scalar.activation(hT[:, t % 2], psH[:, 0:KF], ACT.Copy).then_inc(s_hT, 1)
                            act.wait_ge(s_dn, t + 1)
                            if t >= 2:
                                act.wait_ge(s_yd[t % 2], 16 * (t // 2))
                            nc.scalar.activation(ysh[:, t % 2].rearrange("p (b n) -> p b n", b=2), psY[:], ACT.Copy).then_inc(s_ys, 1)

                    @block.gpsimd
                    def _(pool):
                        nc.gpsimd.memset(zero[:], 0.0).then_inc(s_z, 1)
                        for t in range(POOLT):
                            pool.wait_ge(s_gc, t + 1)
                            nc.gpsimd.tensor_tensor(up[:, t % 2], up[:, t % 2], sg[:, t % 2], ALU.mult).then_inc(s_hm, 1)
                        pool.wait_ge(s_tab, 1)
                        for i in range(NB8):
                            pool.indirect_dma_start(slot_d[l], bass.IndirectOffsetOnAxis(ap=dest[:, i:i + 1].bitcast(U32), axis=0),
                                                    pay[:, i], None).then_inc(s_scat, 16)
                        pool.wait_ge(s_scat, 16 * NB8)

                    @block.vector
                    def _(dve):
                        link = Chain(dve, s_dve)
                        V = nc.vector
                        dve.wait_ge(s_sig, 1)
                        dve.wait_ge(s_br, 16)
                        link(V.tensor_tensor(bi[:], sc[:], bc(brt[:], nt), ALU.add))
                        big = bi[:].rearrange("p t (g e) -> p (t g) e", g=NG)
                        for i in range(nt * NG):
                            ins = V.max(srt[:, i], big[:, i])
                        link(ins)
                        link(V.tensor_tensor(gs[:].rearrange("p t g -> p (t g)"), srt[:, :, 0], srt[:, :, 1], ALU.add))
                        me = bcl(gs[:], NG)
                        other = gs[:].unsqueeze(2).to_broadcast([P, nt, NG, NG])
                        tri = cst[:, C_TRI:C_TRI + NG * NG]
                        f3 = lambda x: x.rearrange("p t i j -> p t (i j)")
                        V.tensor_tensor(cmp1[:], other, me, ALU.is_gt)
                        link(V.tensor_tensor(cmp2[:], other, me, ALU.is_equal))
                        link(V.tensor_tensor(f3(cmp2[:]), f3(cmp2[:]), bc(tri, nt), ALU.mult))
                        link(V.tensor_tensor(cmp1[:], cmp1[:], cmp2[:], ALU.add))
                        link(V.tensor_reduce(gm[:], cmp1[:].rearrange("p t i j -> p (t i) j"), AX, ALU.add))
                        link(V.tensor_scalar(gm[:], gm[:], float(TOPG) - 0.5, None, ALU.is_lt))
                        link(V.tensor_tensor(big, big, bcl(gm[:], NE // NG), ALU.mult))
                        link(V.tensor_scalar(gm[:], gm[:], -NEG, NEG, ALU.mult, ALU.add))
                        link(V.tensor_tensor(big, big, bcl(gm[:], NE // NG), ALU.add))
                        for t in range(nt):
                            ins = V.max(top8[:, t], bi[:, t])
                        link(ins)
                        for t in range(nt):
                            ins = V.match_replace(rep[:, t], top8[:, t], bi[:, t], -3e38)
                        link(ins)
                        link(V.tensor_tensor(sel[:], bi[:], rep[:], ALU.is_gt), s_sel)
                        link(V.tensor_tensor(wt[:], sc[:], sel[:], ALU.mult))
                        link(V.tensor_reduce(tot[:], wt[:], AX, ALU.add))
                        link(V.reciprocal(tot[:], tot[:]))
                        link(V.tensor_scalar(tot[:], tot[:], ROUTED, None, ALU.mult))
                        link(V.tensor_tensor(wt[:], wt[:], bcl(tot[:], NE), ALU.mult))
                        dve.wait_ge(s_rk, 1)
                        link(V.tensor_scalar(nb[:], psN[:, 0:NE], 0.5, None, ALU.is_gt))
                        for j in range(1, nt):
                            link(V.scalar_tensor_tensor(nb[:], psN[:, 0:NE], P * j + 0.5, nb[:], ALU.is_gt, ALU.add))
                        link(V.tensor_tensor_scan(bend[:], ones[:, 0:NE], nb[:], 0.0, ALU.mult, ALU.add))
                        V.tensor_scalar(bst[:], bend[:], cst[:, C_IOTA:C_IOTA + 1], None, ALU.is_le)
                        link(V.tensor_copy(nblk_i[0:1, l:l + 1], bend[0:1, NE - 1:NE]), s_nb)
                        link(V.tensor_reduce(bef[:], bst[:], AX, ALU.add))
                        link(V.tensor_scalar(bei[:], bef[:], float(NE - 1), None, ALU.min))
                        link(V.tensor_tensor(bst[:], bend[:], nb[:], ALU.subtract))
                        link(V.tensor_scalar(bst[:], bst[:], -float(P), float(FAR), ALU.mult, ALU.add))
                        rk = psK[:, 0:nt * NE].rearrange("p (t e) -> p t e", e=NE)
                        link(V.tensor_tensor(v[:], bc(bst[:], nt), rk, ALU.subtract))
                        link(V.tensor_tensor(v[:], v[:], sel[:], ALU.mult))
                        for t in range(nt):
                            ins = V.max(v8[:, t], v[:, t])
                        link(ins)
                        for t in range(nt):
                            V.tensor_tensor(eq[:, t], v[:, t].unsqueeze(1).to_broadcast([P, 8, NE]), bcl(v8[:, t], NE), ALU.is_equal).then_inc(s_dve, 1)
                            link.count[id(s_dve)] += 1
                        dve.wait_ge(s_dve, link.count[id(s_dve)])
                        for t in range(nt):
                            ins = V.tensor_tensor(eq[:, t], eq[:, t], bc(wt[:, t], 8), ALU.mult)
                        link(ins)
                        link(V.tensor_reduce(w8[:].rearrange("p t k -> p (t k)"), eq[:].rearrange("p t k e -> p (t k) e"), AX, ALU.add))
                        v8f = v8[:].rearrange("p t k -> p (t k)")
                        link(V.tensor_scalar(d8[:], v8f, -1.0, float(FAR), ALU.mult, ALU.add))
                        V.tensor_scalar(d8p[:], d8[:], P - 1, None, ALU.bitwise_and)
                        link(V.tensor_scalar(d8b[:], d8[:], 7, None, ALU.arith_shift_right))
                        link(V.scalar_tensor_tensor(dest[:], d8p[:], float(TBL), d8b[:], ALU.mult, ALU.add))
                        tok = cst[:, C_TOK:C_TOK + nt]
                        V.tensor_copy(pay[:, :, 0].rearrange("p (t k) -> p t k", k=8), bcl(tok, 8))
                        V.tensor_copy(pay[:, :, 1].bitcast(F32), w8[:].rearrange("p t k -> p (t k)")).then_inc(s_tab, 1)
                        for t in range(POOLT, nt):
                            dve.wait_ge(s_gc, t + 1)
                            dve.wait_ge(s_hm, t)
                            V.tensor_tensor(up[:, t % 2], up[:, t % 2], sg[:, t % 2], ALU.mult).then_inc(s_hm, 1)

        def stage_experts(l, nt):
            with ExitStack() as ctx:
                S = lambda n: sem(f"F{l}_{n}_s")
                T = lambda n, shape, dt=F32: sb(ctx, f"F{l}_{n}", shape, dt)
                slots = T("slots", [P, TBL, 2], I32)
                wgu = T("wgu", [P, 2, 2, KD, FF])
                wd = T("wd", [P, 2, KF, D])
                xb = T("xb", [P, 2, D])
                xT = T("xT", [P, 2, KD, P])
                sil = T("sil", [P, 2, FF])
                hh = T("hh", [P, 2, FF])
                hT = T("hT", [P, 2, KF, P])
                yb = T("yb", [P, 2, D])
                gi = T("gi", [P, 2, 1], I32)
                si = T("si", [P, 2, 2], I32)
                psX = ps(ctx, f"F{l}_psX", [P, 2, 4, P])
                psG = ps(ctx, f"F{l}_psG", [P, 2, 512])
                psH = ps(ctx, f"F{l}_psH", [P, 4, P])
                psY = ps(ctx, f"F{l}_psY", [P, 2, 512])
                s_slots, s_xb0 = S("slots"), S("xb0")
                s_wg, s_wd_, s_x = [S("wg0"), S("wg1")], [S("wd0"), S("wd1")], [S("x0"), S("x1")]
                s_tx, s_gu, s_ht, s_dn = S("tx"), S("gu"), S("ht"), S("dn")
                s_xa, s_xd, s_sil, s_mul, s_hT, s_ya, s_yd = S("xa"), S("xd"), S("sil"), S("mul"), S("hT"), S("ya"), S("yd")
                s_bear = S("bear")
                s_gi, s_sidx, s_sc = S("gi"), S("sidx"), [S("sc0"), S("sc1")]

                def passes(eng):
                    n = eng.value_load(nblk_i[0:1, l:l + 1], min_val=1, max_val=MAXBLK)
                    return eng.snap((n + 1) // 2)

                with nc.Block() as block:
                    @block.sync
                    def _(sp):
                        sp.dma_start(slots[:].rearrange("p b c -> p (b c)"), slot_d[l].rearrange("(p b) c -> p (b c)", p=P)).then_inc(s_slots, 16)
                        np_ = passes(sp)

                        def expert(b):
                            return sp.value_load(be_d[l][0:1, bass.ds(b, 1)], min_val=0, max_val=NE - 1)

                        def load_gate_up(j, e):
                            sp.dma_start(wgu[:, j, 0], a["we_gate"][l, bass.ds(e, 1)].rearrange("o (p k) f -> p (o k) f", p=P)).then_inc(s_wg[j], 16)
                            sp.dma_start(wgu[:, j, 1], a["we_up"][l, bass.ds(e, 1)].rearrange("o (p k) f -> p (o k) f", p=P)).then_inc(s_wg[j], 16)

                        def load_down(j, e):
                            sp.dma_start(wd[:, j], a["we_down"][l, bass.ds(e, 1)].rearrange("o (p k) n -> p (o k) n", p=P)).then_inc(s_wd_[j], 16)

                        e0 = expert(0)
                        load_gate_up(0, e0)
                        load_down(0, e0)
                        load_gate_up(1, expert(1))
                        with sp.Fori(0, np_) as i:
                            for j in range(2):
                                b = 2 * i + j
                                e2, e1 = expert(b + 2), expert(b + 1)
                                sp.wait_ge(s_gu, b + 1)
                                load_gate_up(j, e2)
                                sp.wait_ge(s_dn, b + 1)
                                load_down(1 - j, e1)
                        sp.wait_ge(s_wg[1], 32 * np_ + 32)
                        sp.wait_ge(s_wd_[0], 16 * np_ + 16)
                        sp.sem_inc(s_bear, 1)

                    @block.gpsimd
                    def _(pool):
                        G = nc.gpsimd
                        G.memset(xb[:], 0.0).then_inc(s_xb0, 1)
                        pool.wait_ge(s_xb0, 1)
                        pool.wait_ge(s_slots, 16)
                        np_ = passes(pool)

                        def gather(j, b, guard=None):
                            G.tensor_copy(gi[:, j], slots[:, bass.ds(b, 1), 0]).then_inc(s_gi, 1)
                            pool.wait_ge(s_gi, b + 1)
                            pool.sem_inc(s_bear, 1)
                            pool.indirect_dma_start(xb[:, j], None, f_d[l][0:nt * P], bass.IndirectOffsetOnAxis(ap=gi[:, j].bitcast(U32), axis=0),
                                                    bounds_check=nt * P - 1, oob_is_err=False).then_inc(s_x[j], 16)

                        G.memset(yb[:], 0.0).then_inc(s_xb0, 1)
                        G.tensor_copy(si[:], slots[:, TBL - 2:TBL]).then_inc(s_xb0, 1)
                        pool.wait_ge(s_xb0, 3)
                        for j in range(2):
                            pool.indirect_dma_start(acc_d[l], bass.IndirectOffsetOnAxis(ap=si[:, j, 0:1].bitcast(U32), axis=0), yb[:, j], None,
                                                    compute_op=ALU.add).then_inc(s_sc[j], 16)
                            pool.wait_ge(s_sc[j], 16)
                        gather(0, 0)
                        gather(1, 1)
                        pool.wait_ge(s_tx, 1)
                        gather(0, 2)
                        with pool.Fori(0, np_) as i:
                            for j in range(2):
                                b = 2 * i + j
                                pool.wait_ge(s_sc[j], 16 * i + 16)
                                G.tensor_copy(si[:, j], slots[:, bass.ds(b, 1)].rearrange("p o c -> p (o c)")).then_inc(s_sidx, 1)
                                pool.wait_ge(s_tx, b + 2)
                                gather(1 - j, b + 3)
                                pool.wait_ge(s_ya, b + 2)
                                pool.wait_ge(s_yd, b + 2)
                                pool.wait_ge(s_sc[1 - j], 16 * i + 16 + 16 * j)
                                pool.sem_inc(s_bear, 1)
                                pool.indirect_dma_start(acc_d[l], bass.IndirectOffsetOnAxis(ap=si[:, j, 0:1].bitcast(U32), axis=0), yb[:, j], None,
                                                        compute_op=ALU.add).then_inc(s_sc[j], 16)

                        for j in range(2):
                            pool.wait_ge(s_sc[j], 16 * np_ + 16)
                        pool.wait_ge(s_x[0], 16 * np_ + 32)
                        pool.sem_inc(s_bear, 1)

                    @block.tensor
                    def _(pe):
                        pe.sem_inc(s_dn, 1)
                        np_ = passes(pe)

                        def turn_rows(j):
                            v = xb[:, j].rearrange("q (p k) -> q k p", k=KD)
                            for k in range(KD):
                                ins = nc.tensor.transpose(psX[:, k // 4, k % 4], v[:, k], ident)
                            ins.then_inc(s_tx, 1)

                        def gate_up(j):
                            for k in range(KD):
                                ins = nc.tensor.matmul(psG[:, j].rearrange("p (v f) -> p v f", v=2), xT[:, j, k], wgu[:, j, :, k],
                                                       start=(k == 0), stop=(k == KD - 1))
                            ins.then_inc(s_gu, 1)

                        pe.wait_ge(s_x[0], 16)
                        turn_rows(0)
                        pe.wait_ge(s_xa, 1)
                        pe.wait_ge(s_xd, 1)
                        pe.wait_ge(s_wg[0], 32)
                        gate_up(0)
                        pe.wait_ge(s_x[1], 16)
                        turn_rows(1)
                        with pe.Fori(0, np_) as i:
                            for j in range(2):
                                b = 2 * i + j
                                pe.wait_ge(s_mul, b + 1)
                                v = hh[:, j].rearrange("q (p k) -> q k p", k=KF)
                                for k in range(KF):
                                    ins = nc.tensor.transpose(psH[:, k], v[:, k], ident)
                                ins.then_inc(s_ht, 1)
                                pe.wait_ge(s_xa, b + 2)
                                pe.wait_ge(s_xd, b + 2)
                                pe.wait_ge(s_wg[1 - j], 32 * i + 32 + 32 * j)
                                gate_up(1 - j)
                                pe.wait_ge(s_x[j], 16 * i + 32)
                                turn_rows(j)
                                pe.wait_ge(s_hT, b + 1)
                                pe.wait_ge(s_wd_[j], 16 * i + 16)
                                pe.wait_ge(s_ya, b + 1)
                                pe.wait_ge(s_yd, b + 1)
                                for n in range(2):
                                    for k in range(KF):
                                        ins = nc.tensor.matmul(psY[:, n], hT[:, j, k], wd[:, j, k, n * 512:(n + 1) * 512], start=(k == 0), stop=(k == KF - 1))
                                ins.then_inc(s_dn, 1)

                    @block.scalar
                    def _(act):
                        act.sem_inc(s_ya, 1)
                        np_ = passes(act)

                        def rows(j):
                            nc.scalar.activation(xT[:, j, 0:4], psX[:, 0], ACT.Copy).then_inc(s_xa, 1)

                        def silu(j):
                            nc.scalar.activation(sil[:, j], psG[:, j, 0:FF], ACT.Silu).then_inc(s_sil, 1)

                        act.wait_ge(s_tx, 1)
                        rows(0)
                        act.wait_ge(s_gu, 1)
                        silu(0)
                        act.wait_ge(s_tx, 2)
                        rows(1)
                        with act.Fori(0, np_) as i:
                            for j in range(2):
                                b = 2 * i + j
                                act.wait_ge(s_gu, b + 2)
                                silu(1 - j)
                                act.wait_ge(s_tx, b + 3)
                                rows(j)
                                act.wait_ge(s_dn, b + 2)
                                act.wait_ge(s_sidx, b + 1)
                                nc.scalar.activation(yb[:, j, 0:512], psY[:, 0], ACT.Copy, scale=si[:, j, 1:2].bitcast(F32)).then_inc(s_ya, 1)

                    @block.vector
                    def _(dve):
                        dve.sem_inc(s_yd, 1)
                        np_ = passes(dve)

                        def rows(j):
                            nc.vector.tensor_copy(xT[:, j, 4:8], psX[:, 1]).then_inc(s_xd, 1)

                        def product(j):
                            nc.vector.tensor_tensor(hh[:, j], sil[:, j], psG[:, j, FF:2 * FF], ALU.mult).then_inc(s_mul, 1)

                        dve.wait_ge(s_tx, 1)
                        rows(0)
                        dve.wait_ge(s_sil, 1)
                        product(0)
                        dve.wait_ge(s_tx, 2)
                        rows(1)
                        with dve.Fori(0, np_) as i:
                            for j in range(2):
                                b = 2 * i + j
                                dve.wait_ge(s_ht, b + 1)
                                nc.vector.tensor_copy(hT[:, j], psH[:, 0:KF]).then_inc(s_hT, 1)
                                dve.wait_ge(s_sil, b + 2)
                                product(1 - j)
                                dve.wait_ge(s_tx, b + 3)
                                rows(j)
                                dve.wait_ge(s_dn, b + 2)
                                dve.wait_ge(s_sidx, b + 1)
                                nc.vector.tensor_scalar(yb[:, j, 512:], psY[:, 1], si[:, j, 1:2].bitcast(F32), None, ALU.mult).then_inc(s_yd, 1)


        def stage_combine(l, nt, aT):
            with ExitStack() as ctx:
                S = lambda n: sem(f"H{l}_{n}_s")
                T = lambda n, shape, dt=F32: sb(ctx, f"H{l}_{n}", shape, dt)
                nv = 2 if nt > NL else 1
                ac = T("ac", [P, 3, D])
                gate = T("gate", [P, nv, D])
                amul = T("amul", [P, nv, D])
                aadd = T("aadd", [P, nv, D])
                an = T("an", [P, 2, D])
                junk = T("junk", [P, D], BF16)
                st = T("st", [P, nt, 3])
                psT = ps(ctx, f"H{l}_psT", [P, 2, KD, P])
                s_v, s_ac = S("v"), [S(f"ac{i}") for i in range(3)]
                s_g, s_h, s_rt, s_a0, s_a, s_tp, s_tev, s_act, s_dve = (S(n) for n in ("g", "h", "rt", "a0", "a", "tp", "tev", "act", "dve"))
                s_out = [S("out0"), S("out1")]
                with nc.Block() as block:
                    @block.sync
                    def _(sp):
                        for t in range(nt):
                            if t >= 3:
                                sp.wait_ge(s_h, t - 2)
                            sp.dma_start(ac[:, t % 3], acc_d[l][t * P:(t + 1) * P]).then_inc(s_ac[t % 3], 16)
                        if aT is None:
                            for t in range(nt):
                                sp.wait_ge(s_a0, t + 1)
                                sp.dma_start(out[0, t * P:(t + 1) * P], an[:, t % 2]).then_inc(s_out[t % 2], 16)
                            for b in range(2):
                                sp.wait_ge(s_out[b], 16 * ((nt - b + 1) // 2))

                    @block.scalar
                    def _(act):
                        link = Chain(act, s_act)
                        for v in range(nv):
                            act.dma_start(gate[:, v], mod_rows(l, v, 5)).then_inc(s_v, 16)
                            if aT is not None:
                                act.dma_start(amul[:, v], mod_rows(l + 1, v, 1)).then_inc(s_v, 16)
                                act.dma_start(aadd[:, v], mod_rows(l + 1, v, 0)).then_inc(s_v, 16)
                            else:
                                act.dma_start(amul[:, v], a["g_final"].rearrange("(o d) -> o d", o=1).to_broadcast([P, D])).then_inc(s_v, 16)
                        for t in range(nt):
                            act.wait_ge(s_h, t + 1)
                            link(nc.scalar.activation(junk[:], h[:, t], ACT.Square, accum_out=st[:, t, 0:1]))
                            nc.scalar.activation(st[:, t, 1:2], st[:, t, 0:1], ACT.Sqrt, bias=eps, scale=1.0 / D).then_inc(s_rt, 1)
                            if aT is not None:
                                act.wait_ge(s_tp, t + 1)
                                nc.scalar.activation(aT[:, :, t * P:(t + 1) * P], psT[:, t % 2], ACT.Copy).then_inc(s_tev, 1)

                    @block.vector
                    def _(dve):
                        link = Chain(dve, s_dve)
                        dve.wait_ge(s_v, 16 * nv * (3 if aT is not None else 2))

                        def gated(t):
                            dve.wait_ge(s_ac[t % 3], 16 * (t // 3 + 1))
                            nc.vector.tensor_tensor(ac[:, t % 3], ac[:, t % 3], gate[:, 0 if t < NL else 1], ALU.mult).then_inc(s_g, 1)

                        gated(0)
                        for t in range(nt):
                            if t + 1 < nt:
                                gated(t + 1)
                            dve.wait_ge(s_rt, t + 1)
                            link(nc.vector.reciprocal(st[:, t, 2:3], st[:, t, 1:2]))
                            if t >= 2:
                                if aT is not None:
                                    dve.wait_ge(s_tp, t - 1)
                                else:
                                    dve.wait_ge(s_out[t % 2], 16 * (t // 2))
                            nc.vector.scalar_tensor_tensor(an[:, t % 2], h[:, t], st[:, t, 2:3], amul[:, 0 if t < NL else 1], ALU.mult, ALU.mult).then_inc(s_a0, 1)

                    @block.gpsimd
                    def _(pool):
                        def added(t):
                            pool.wait_ge(s_g, t + 1)
                            nc.gpsimd.tensor_tensor(h[:, t], h[:, t], ac[:, t % 3], ALU.add).then_inc(s_h, 1)

                        added(0)
                        for t in range(nt):
                            if t + 1 < nt:
                                added(t + 1)
                            if aT is not None:
                                pool.wait_ge(s_a0, t + 1)
                                nc.gpsimd.tensor_tensor(an[:, t % 2], an[:, t % 2], aadd[:, 0 if t < NL else 1], ALU.add).then_inc(s_a, 1)

                    @block.tensor
                    def _(pe):
                        if aT is not None:
                            for t in range(nt):
                                pe.wait_ge(s_a, t + 1)
                                if t >= 2:
                                    pe.wait_ge(s_tev, t - 1)
                                v = an[:, t % 2].rearrange("q (p k) -> q k p", k=KD)
                                for k in range(KD):
                                    ins = nc.tensor.transpose(psT[:, t % 2, k], v[:, k], ident)
                                ins.then_inc(s_tp, 1)

        def stage_attend1(aT, o):
            with ExitStack() as ctx:
                S = lambda n: sem(f"I_{n}_s")
                T = lambda n, shape, dt=F32: sb(ctx, f"I_{n}", shape, dt)
                w = T("w", [P, 2, KD, DC])
                qkT = T("qkT", [P, 2, 2, NT * P])
                vv = T("vv", [P, 2, NT, DV])
                qk = T("qk", [P, 2, 4, DHALF])
                t1 = T("t1", [P, 2, 4, DHALF])
                t2 = T("t2", [P, 2, 4, DHALF])
                prob = T("prob", [P, 2, 2, NT * P])
                pT = T("pT", [P, 2, NT, P])
                nmax = T("nmax", [P, 2, 2])
                ssum = T("ssum", [P, 2, 2])
                lamv = T("lamv", [P, 4, DHALF])
                lamj = T("lamj", [P, DHALF])
                lam2 = T("lam2", [P, 2])
                nlam = T("nlam", [P, 1])
                osq = T("osq", [P, D])
                ost = T("ost", [P, NL, DH])
                psS = ps(ctx, "I_psS", [P, 2, 1024])
                psP = ps(ctx, "I_psP", [P, 8, P])
                psO = ps(ctx, "I_psO", [P, NL, DV])
                psC = ps(ctx, "I_psC", [P, 512])
                s_lam, s_lamd, s_w = S("lam"), S("lamd"), [S("w0"), S("w1")]
                (s_pr, s_prd, s_pra, s_qk, s_tr, s_tre, s_s, s_nm, s_e, s_cb, s_p1, s_t, s_evd, s_eva, s_pv, s_o, s_act, s_dve, s_lame, s_fin, s_finr) = (
                    S(n) for n in ("pr", "prd", "pra", "qk", "tr", "tre", "s", "nm", "e", "cb", "p1", "t", "evd", "eva", "pv", "o", "act", "dve", "lame", "fin", "finr"))
                cos = cst[:, C_COS:C_COS + NL * SD].rearrange("p (t d) -> p t d", t=NL)
                sin = cst[:, C_SIN:C_SIN + NL * SD].rearrange("p (t d) -> p t d", t=NL)
                slots_ = [(hd, s) for hd in range(DH + 1) for s in range(NT)]

                def tile_no(hd, s):
                    return hd * NT + s

                def order(hd, s):
                    work = []
                    if hd < DH:
                        work.append(("project", hd, s))
                    if hd >= 1 and 2 <= s < NL + 2:
                        work.append(("values", hd - 1, s - 2))
                    if s >= 1 and hd < DH:
                        work.append(("turn_qk", hd, s - 1))
                    if s == 0 and 1 <= hd:
                        work.append(("turn_qk", hd - 1, NT - 1))
                    if hd >= 1 and s < NL:
                        work.append(("scores", hd - 1, s))
                    if hd >= 1 and 1 <= s < NL + 1:
                        work.append(("turn", hd - 1, s - 1))
                    return work

                every = [x for hd, s in slots_ for x in order(hd, s)]

                def units_before(hd, s):
                    return sum(x[0] == "turn" for x in every[:every.index(("turn_qk", hd, s))])

                def turned_before(hd, t):
                    return sum(x[0] == "turn_qk" for x in every[:every.index(("turn", hd, t))])

                with nc.Block() as block:
                    @block.sync
                    def _(sp):
                        for n, name in enumerate(("lam_q1", "lam_k1", "lam_q2", "lam_k2")):
                            sp.dma_start(lamv[:, n], a[name][0:1, :].to_broadcast([P, DHALF])).then_inc(s_lam, 16)
                        for hd in range(DH):
                            if hd >= 2:
                                sp.wait_ge(s_pr, NT * (hd - 1))
                            sp.dma_start(w[:, hd % 2], kview(a["wc_in"][0])[:, :, hd * DC:(hd + 1) * DC]).then_inc(s_w[hd % 2], 16)

                    @block.tensor
                    def _(pe):
                        def project(hd, s):
                            n = tile_no(hd, s)
                            if s == 0:
                                pe.wait_ge(s_w[hd % 2], 16 * (hd // 2 + 1))
                            if n >= 1:
                                pe.wait_ge(s_prd, n)
                                pe.wait_ge(s_pra, n)
                            c0 = 0 if s < NL else 2 * DHALF
                            for k in range(KD):
                                ins = nc.tensor.matmul(psC[:, c0:DC], aT[:, k, s * P:(s + 1) * P], w[:, hd % 2, k, c0:DC], start=(k == 0), stop=(k == KD - 1))
                            ins.then_inc(s_pr, 1)

                        def turn_qk(hd, s):
                            n = tile_no(hd, s)
                            pe.wait_ge(s_qk, n + 1)
                            if n >= 1:
                                pe.wait_ge(s_tre, n)
                            u = units_before(hd, s)
                            if u >= 1:
                                pe.wait_ge(s_eva, u)
                            if s < NL:
                                nc.tensor.transpose(psP[:, 6], qk[:, n % 2, 0:2].rearrange("p m d -> p (m d)"), ident)
                            nc.tensor.transpose(psP[:, 7], qk[:, n % 2, 2:4].rearrange("p m d -> p (m d)"), ident).then_inc(s_tr, 1)

                        def scores(hd, t):
                            u = hd * NL + t
                            if t == 0:
                                pe.wait_ge(s_tre, NT * (hd + 1))
                            for m in range(2):
                                if u >= 1:
                                    pe.wait_ge(s_e, 2 * (u - 1) + m + 1)
                                r = slice(64 * m, 64 * m + 64)
                                q = qkT[r, hd % 2, 0, t * P:(t + 1) * P]
                                nc.tensor.matmul(psS[:, m, 0:512], q, qkT[r, hd % 2, 1, 0:512], start=True, stop=True)
                                nc.tensor.matmul(psS[:, m, 512:768], q, qkT[r, hd % 2, 1, 512:768], start=True, stop=True).then_inc(s_s, 1)

                        def turn(hd, t):
                            u = hd * NL + t
                            pe.wait_ge(s_cb, u + 1)
                            if u >= 1:
                                pe.wait_ge(s_evd, u)
                                pe.wait_ge(s_eva, u)
                            n = turned_before(hd, t)
                            if n >= 1:
                                pe.wait_ge(s_tre, n)
                            for b in range(NT):
                                ins = nc.tensor.transpose(psP[:, b], prob[:, u % 2, 0, b * P:(b + 1) * P], ident)
                            ins.then_inc(s_t, 1)

                        def values(hd, t):
                            u = hd * NL + t
                            pe.wait_ge(s_evd, u + 1)
                            pe.wait_ge(s_eva, u + 1)
                            if t == 0 and hd >= 1:
                                pe.wait_ge(s_o, hd)
                            if t == 0:
                                pe.wait_ge(s_pra, NT * (hd + 1))
                            for b in range(NT):
                                ins = nc.tensor.matmul(psO[:, t], pT[:, u % 2, b], vv[:, hd % 2, b], start=(b == 0), stop=(b == NT - 1))
                            ins.then_inc(s_pv, 1)

                        for hd, s in slots_:
                            for what, x, y in order(hd, s):
                                {"project": project, "values": values, "turn_qk": turn_qk, "scores": scores, "turn": turn}[what](x, y)

                    @block.vector
                    def _(dve):
                        link = Chain(dve, s_dve)
                        V = nc.vector
                        dve.wait_ge(s_lam, 64)
                        for m in range(2):
                            link(V.tensor_tensor_reduce(lamj[:], lamv[:, 2 * m], lamv[:, 2 * m + 1], 1.0, 0.0, ALU.mult, ALU.add, lam2[:, m:m + 1]))
                        V.tensor_copy(lam2[:], lam2[:]).then_inc(s_lamd, 1)
                        dve.wait_ge(s_lame, 1)
                        link(V.tensor_tensor(nlam[:], lam2[:, 1:2], lam2[:, 0:1], ALU.subtract))
                        link(V.tensor_scalar(nlam[:], nlam[:], -LAM_INIT, None, ALU.add))

                        def rotate(hd, s):
                            n = tile_no(hd, s)
                            dve.wait_ge(s_pr, n + 1)
                            if n >= 2:
                                dve.wait_ge(s_qk, n - 1)
                                dve.wait_ge(s_tr, n - 1)
                            if s < NL:
                                src = psC[:, 0:4 * DHALF].rearrange("p (g d) -> p g d", d=DHALF)
                                q = DHALF // 4
                                V.tensor_tensor(t1[:, n % 2], src, bc(cos[:, s], 4), ALU.mult)
                                s4 = src.rearrange("p g (b two q) -> p g b two q", two=2, q=q)
                                t4 = t2[:, n % 2].rearrange("p g (b two q) -> p g b two q", two=2, q=q)
                                n4 = bc(sin[:, s], 4).rearrange("p g (b two q) -> p g b two q", two=2, q=q)
                                for b in range(2):
                                    V.tensor_tensor(t4[:, :, b, 0], s4[:, :, b, 1], n4[:, :, b, 0], ALU.mult)
                                    ins = V.tensor_tensor(t4[:, :, b, 1], s4[:, :, b, 0], n4[:, :, b, 1], ALU.mult)
                            else:
                                ins = V.tensor_copy(t1[:, n % 2, 2:4], psC[:, 2 * DHALF:4 * DHALF].rearrange("p (g d) -> p g d", d=DHALF))
                            link(ins, s_prd)

                        def maximum(hd, t):
                            u = hd * NL + t
                            for m in range(2):
                                dve.wait_ge(s_s, 2 * u + m + 1)
                                if u >= 2 and m == 0:
                                    dve.wait_ge(s_e, 2 * u - 2)
                                link(V.tensor_reduce(nmax[:, u % 2, m:m + 1], psS[:, m, 0:NT * P], AX, ALU.max, negate=True), s_nm)

                        def combine(hd, t):
                            u = hd * NL + t
                            dve.wait_ge(s_e, 2 * u + 2)
                            link(V.reciprocal(ssum[:, u % 2], ssum[:, u % 2]))
                            link(V.tensor_tensor(ssum[:, u % 2, 1:2], ssum[:, u % 2, 1:2], nlam[:], ALU.mult), s_p1)
                            link(V.tensor_scalar(prob[:, u % 2, 1], prob[:, u % 2, 1], ssum[:, u % 2, 1:2], None, ALU.mult))
                            link(V.scalar_tensor_tensor(prob[:, u % 2, 0], prob[:, u % 2, 0], ssum[:, u % 2, 0:1], prob[:, u % 2, 1], ALU.mult, ALU.add), s_cb)

                        def evac(hd, t):
                            u = hd * NL + t
                            dve.wait_ge(s_t, u + 1)
                            if u >= 2:
                                dve.wait_ge(s_pv, u - 1)
                            V.tensor_copy(pT[:, u % 2, 0:4], psP[:, 0:4]).then_inc(s_evd, 1)

                        def head_out(hd):
                            dve.wait_ge(s_pv, NL * (hd + 1))
                            V.tensor_copy(o[:, 0:NL, hd * DV:(hd + 1) * DV], psO[:]).then_inc(s_o, 1)

                        for hd, s in slots_:
                            if hd < DH:
                                rotate(hd, s)
                            if hd >= 1:
                                if s < NL:
                                    maximum(hd - 1, s)
                                    combine(hd - 1, s)
                                if 1 <= s < NL + 1:
                                    evac(hd - 1, s - 1)
                                if s == NL + 1:
                                    head_out(hd - 1)
                        dve.wait_ge(s_o, DH)
                        for t in range(NL):
                            if t >= 1:
                                dve.wait_ge(s_dve, link.count[id(s_dve)])
                            link(V.tensor_tensor(osq[:], o[:, t], o[:, t], ALU.mult))
                            link(V.tensor_reduce(ost[:, t], osq[:].rearrange("p (h d) -> p h d", d=DV), AX, ALU.add))
                        V.tensor_copy(ost[:], ost[:]).then_inc(s_fin, 1)
                        dve.wait_ge(s_finr, 1)
                        link(V.reciprocal(ost[:], ost[:]))
                        for t in range(NL):
                            ov = o[:, t].rearrange("p (h d) -> p h d", d=DV)
                            link(V.tensor_tensor(ov, ov, bcl(ost[:, t], DV), ALU.mult))

                    @block.gpsimd
                    def _(pool):
                        for hd in range(DH):
                            for s in range(NT):
                                n = tile_no(hd, s)
                                pool.wait_ge(s_prd, n + 1)
                                if n >= 2:
                                    pool.wait_ge(s_tr, n - 1)
                                if s < NL:
                                    nc.gpsimd.tensor_tensor(qk[:, n % 2], t1[:, n % 2], t2[:, n % 2], ALU.add).then_inc(s_qk, 1)
                                else:
                                    nc.gpsimd.tensor_copy(qk[:, n % 2, 2:4], t1[:, n % 2, 2:4]).then_inc(s_qk, 1)

                    @block.scalar
                    def _(act):
                        link = Chain(act, s_act)
                        act.wait_ge(s_lamd, 1)
                        nc.scalar.activation(lam2[:], lam2[:], ACT.Exp).then_inc(s_lame, 1)

                        def copy_v(hd, s):
                            n = tile_no(hd, s)
                            act.wait_ge(s_pr, n + 1)
                            act.wait_ge(s_prd, n + 1)
                            if s == 0 and hd >= 2:
                                act.wait_ge(s_pv, NL * (hd - 1))
                            nc.scalar.activation(vv[:, hd % 2, s], psC[:, 4 * DHALF:DC], ACT.Copy).then_inc(s_pra, 1)

                        def copy_qk(hd, s):
                            n = tile_no(hd, s)
                            act.wait_ge(s_tr, n + 1)
                            if s == 0 and hd >= 2:
                                act.wait_ge(s_s, 2 * NL * (hd - 1))
                            if s < NL:
                                nc.scalar.activation(qkT[:, hd % 2, 0, s * P:(s + 1) * P], psP[:, 6], ACT.Copy, scale=float(DHALF) ** -0.5)
                            nc.scalar.activation(qkT[:, hd % 2, 1, s * P:(s + 1) * P], psP[:, 7], ACT.Copy).then_inc(s_tre, 1)

                        def exps(hd, t):
                            u = hd * NL + t
                            if u >= 2:
                                act.wait_ge(s_t, u - 1)
                            for m in range(2):
                                act.wait_ge(s_nm, 2 * u + m + 1)
                                nc.scalar.activation(prob[:, u % 2, m], psS[:, m, 0:NT * P], ACT.Exp, bias=nmax[:, u % 2, m:m + 1],
                                                     accum_out=ssum[:, u % 2, m:m + 1]).then_inc(s_e, 1)

                        def evac(hd, t):
                            u = hd * NL + t
                            act.wait_ge(s_t, u + 1)
                            if u >= 2:
                                act.wait_ge(s_pv, u - 1)
                            nc.scalar.activation(pT[:, u % 2, 4:6], psP[:, 4:6], ACT.Copy).then_inc(s_eva, 1)

                        for hd, s in slots_:
                            if hd < DH:
                                copy_v(hd, s)
                            for what, x, y in order(hd, s):
                                if what == "turn_qk":
                                    copy_qk(x, y)
                                elif what == "scores":
                                    exps(x, y)
                                elif what == "turn":
                                    evac(x, y)
                        act.wait_ge(s_fin, 1)
                        nc.scalar.activation(ost[:], ost[:], ACT.Sqrt, bias=eps, scale=1.0 / DV).then_inc(s_finr, 1)

        stage_modulation()
        end_stage()
        if stop == "A":
            return
        with ExitStack() as right:
            with ExitStack() as att:
                t_ = dict(qmT=sb(att, "qmT", [MQ, MH, NT * P]), kmT=sb(att, "kmT", [MQ, MH, NT * P]),
                          vM=sb(att, "vM", [P, NT, MH * MV]), qsT=sb(att, "qsT", [P, SH // 2, NT * P]),
                          ksT=sb(att, "ksT", [P, NT * P]), vS=sb(att, "vS", [P, NT, SKV * SD]))
                stage_project0(t_)
                end_stage()
                if stop == "B":
                    return
                o = sb(right, "o", [P, NT, D], side="right")
                stage_attend0(t_, o)
                end_stage()
            if stop == "C":
                return
            lg = sb(right, "lg", [P, NT, NE], side="right")
            fT = sb(right, "fT", [P, KD, NT * P], side="right")
            stage_out(0, NT, o, fT, lg, a["wa_out"][0], None)
            end_stage()
            if stop == "D":
                return
            stage_route(0, NT, fT, lg)
            end_stage()
        if stop == "E":
            return
        stage_experts(0, NT)
        end_stage()
        if stop == "F":
            return
        with ExitStack() as right:
            o = sb(right, "o1", [P, NT, D], side="right")
            with ExitStack() as left:
                aT = sb(left, "aT", [P, KD, NT * P])
                stage_combine(0, NT, aT)
                end_stage()
                stage_attend1(aT, o)
                end_stage()
            if stop == "I":
                return
            lg = sb(right, "lg1", [P, NT, NE], side="right")
            fT = sb(right, "fT1", [P, KD, NT * P], side="right")
            stage_out(1, NL, o, fT, lg, a["wc_out"][0], a["gc_sub"][0])
            end_stage()
            stage_route(1, NL, fT, lg)
            end_stage()
        stage_experts(1, NL)
        end_stage()
        stage_combine(1, NL, None)
        end_stage()


_INS = ['x', 'c', 'ctx', 'c_ctx', 'w_ada', 'b_ada', 'g_mix', 'g_ffn', 'wa_in', 'ga_q', 'ga_kv', 'wa_uq', 'wa_ukv',
        'wa_sink', 'wa_out', 'wc_in', 'lam_q1', 'lam_k1', 'lam_q2', 'lam_k2', 'gc_sub', 'wc_out', 'w_router',
        'b_router', 'we_gate', 'we_up', 'we_down', 'ws_gate', 'ws_up', 'ws_down', 'g_final']


def kernel(**inputs):
    import concourse.bacc as bacc
    from concourse.bass_utils import run_bass_kernel_spmd

    nc = bacc.Bacc("TRN2", target_bir_lowering=False, num_devices=1)
    arrays, args = {}, {}
    for name in _INS:
        arrays[f"in_{name}_dram"] = np.ascontiguousarray(inputs[name])
    arrays["in_cst_dram"] = shape_constants()
    for name in _INS + ["cst"]:
        x = arrays[f"in_{name}_dram"]
        args[name] = nc.dram_tensor(f"in_{name}_dram", x.shape, mybir.dt.from_np(x.dtype), kind="ExternalInput").ap()
    out = nc.dram_tensor("out_0_dram", (1, SEQ, D), F32, kind="ExternalOutput").ap()
    build(nc, args, out)
    r = run_bass_kernel_spmd(nc, [arrays], core_ids=[0])
    return r.results[0]["out_0_dram"]
```

```python
from contextlib import ExitStack

import numpy as np
import concourse.bass as bass
from concourse import mybir

F32 = mybir.dt.float32
BF16 = mybir.dt.bfloat16
I32 = mybir.dt.int32
U32 = mybir.dt.uint32
F32R = mybir.dt.float32r
ALU = mybir.AluOpType
ACT = mybir.ActivationFunctionType
AX = mybir.AxisListType.X

P = 128
D = 1024
KD = D // P
SEQ, CTX = 512, 256
NL, NT = SEQ // P, (SEQ + CTX) // P
EPS = 1e-6
NEG = -1e30
GRID_W, ROPE_BASE = 64, 10000.0

QR, KVR, ROPE, NOPE, MV, MH = 384, 256, 32, 64, 64, 8
MQ = NOPE + ROPE
SH, SKV, SD = 8, 2, 64
DH, DHALF, DV = 8, 64, 128
DC = 4 * DHALF + DV
LAM_INIT = 0.8 - 0.6 * float(np.exp(-0.3))
EVEN_IN = QR + KVR + ROPE + SH * SD + 2 * SKV * SD

NE, NG, TOPG, TOPK, FF = 64, 8, 4, 8, 256
ROUTED = 2.5
KF = FF // P
MAXBLK = NT * TOPK + NE
TBL = MAXBLK + 4
FAR = 16384

C_ID, C_U, C_ONE, C_MP, C_MN = 0, P, 2 * P, 3 * P, 4 * P
C_IOTA = 5 * P
C_EPS = C_IOTA + 1
C_TOK = C_EPS + 1
C_TRI = C_TOK + NT
C_COS = C_TRI + NG * NG
C_SIN = C_COS + NL * SD
C_COSM = C_SIN + NL * SD
C_SINM = C_COSM + NL * ROPE
C_N = C_SINM + NL * ROPE


def shape_constants():
    c = np.zeros((P, C_N), np.float32)
    p = np.arange(P)
    c[:, C_ID:C_ID + P] = np.eye(P)
    c[:, C_U:C_U + P] = p[:, None] < p[None, :]
    c[:, C_ONE:C_ONE + P] = 1
    c[:, C_MP:C_MP + P] = np.where(p[None, :] >= p[:, None], 0, NEG)
    c[:, C_MN:C_MN + P] = np.where(p[None, :] <= p[:, None], 0, NEG)
    c[:, C_IOTA] = p
    c[:, C_EPS] = EPS
    for t in range(NT):
        c[:, C_TOK + t] = t * P + p
    g = np.arange(NG)
    c[:, C_TRI:C_TRI + NG * NG] = (g[None, :] < g[:, None]).reshape(-1)
    for dim, cc, cs in ((SD, C_COS, C_SIN), (ROPE, C_COSM, C_SINM)):
        half, q = dim // 2, dim // 4
        inv = (np.float32(ROPE_BASE) ** (-np.arange(0, half, 2, dtype=np.float32) / np.float32(half))).astype(np.float32)
        for t in range(NL):
            tok = t * P + p
            r = (tok // GRID_W).astype(np.float32)[:, None] * inv
            w = (tok % GRID_W).astype(np.float32)[:, None] * inv
            c[:, cc + t * dim:cc + (t + 1) * dim] = np.cos(np.concatenate([r, r, w, w], 1))
            s = np.sin(np.concatenate([-r, r, -w, w], 1))
            c[:, cs + t * dim:cs + (t + 1) * dim] = s
    return c


class Chain:

    def __init__(self, eng, sem):
        self.eng, self.sem, self.count = eng, sem, {}

    def __call__(self, ins, sem=None):
        sem = self.sem if sem is None else sem
        self.count[id(sem)] = self.count.get(id(sem), 0) + 1
        ins.then_inc(sem, 1)
        self.eng.wait_ge(sem, self.count[id(sem)])


def build(nc, a, out, stop="end"):
    with ExitStack() as whole:
        def sb(ctx, name, shape, dt=F32, side="left"):
            return ctx.enter_context(nc.sbuf_tensor(name, shape, dt, side=side))

        def ps(ctx, name, shape, dt=F32):
            return ctx.enter_context(nc.psum_tensor(name, shape, dt))

        held = []

        def sem(name):
            held.append(nc.alloc_semaphore(name))
            return held[-1]

        def end_stage():
            nc.clear_and_free_semaphores(held)
            held.clear()
            nc.all_engine_barrier()

        def dram(name, shape, dt=F32):
            return nc.dram_tensor(name, shape, dt, kind="Internal").ap()

        mod_d = dram("mod_d", [2, 2, 6 * D])
        f_d = [dram(f"f_d{l}", [NT * P, D]) for l in range(2)]
        acc_d = [dram(f"acc_d{l}", [(NT + 1) * P, D]) for l in range(2)]
        slot_d = [dram(f"slot_d{l}", [P * TBL, 2], I32) for l in range(2)]

        cst = sb(whole, "cst", [P, C_N])
        h = sb(whole, "h", [P, NT, D])
        ident = cst[:, C_ID:C_ID + P]
        eps = cst[:, C_EPS:C_EPS + 1]
        ident_b = sb(whole, "ident_b", [P, P], BF16)
        mask_b = sb(whole, "mask_b", [P, 2, P], BF16)
        starts_i = sb(whole, "starts_i", [1, NE + 1], I32)

        def kview(w):
            return w.rearrange("(p k) n -> p k n", p=P)

        def stage_modulation():
            CH, NCH, WB = 512, 6 * D // 512, 3
            with ExitStack() as ctx:
                craw = sb(ctx, "craw", [P, 2, KD])
                cs = sb(ctx, "cs", [P, KD, 2])
                wada = sb(ctx, "wada", [P, WB, KD, CH])
                bias = sb(ctx, "bias", [2, 2, 6 * D])
                row = sb(ctx, "row", [2, 2, 6 * D])
                gains = sb(ctx, "gains", [2, 2, 2, D])
                empty = sb(ctx, "empty", [P, TBL, 2], I32)
                psA = ps(ctx, "psA", [2, 4, CH])
                s_cst, s_c, s_h, s_b = sem("A_cst"), sem("A_c"), sem("A_h"), sem("A_b")
                s_w = [sem(f"A_w{i}") for i in range(WB)]
                s_silu, s_mm, s_ev, s_dve = sem("A_silu"), sem("A_mm"), sem("A_ev"), sem("A_dve")
                s_row, s_mod, s_emp, s_emps = sem("A_row"), sem("A_mod"), sem("A_emp"), sem("A_emps")
                wv = [a["w_ada"][l].rearrange("(p k) n -> p k n", p=P) for l in range(2)]
                with nc.Block() as block:
                    @block.sync
                    def _(sp):
                        sp.dma_start(craw[:, 0, :], a["c"][0].rearrange("(p k) -> p k", p=P)).then_inc(s_c, 16)
                        sp.dma_start(craw[:, 1, :], a["c_ctx"].rearrange("(p k) -> p k", p=P)).then_inc(s_c, 16)
                        for i in range(2 * NCH):
                            if i >= WB:
                                sp.wait_ge(s_mm, i - WB + 1)
                            l, n = i // NCH, i % NCH
                            sp.dma_start(wada[:, i % WB], wv[l][:, :, n * CH:(n + 1) * CH]).then_inc(s_w[i % WB], 16)

                    @block.scalar
                    def _(act):
                        act.dma_start(cst[:], a["cst"]).then_inc(s_cst, 16)
                        for v in range(2):
                            act.dma_start(bias[v:v + 1], a["b_ada"].rearrange("(o l) n -> o l n", o=1)).then_inc(s_b, 16)
                            act.dma_start(gains[v:v + 1, :, 0], a["g_mix"].rearrange("(o l) n -> o l n", o=1)).then_inc(s_b, 16)
                            act.dma_start(gains[v:v + 1, :, 1], a["g_ffn"].rearrange("(o l) n -> o l n", o=1)).then_inc(s_b, 16)
                        act.wait_ge(s_c, 32)
                        for v in range(2):
                            ins = nc.scalar.activation(cs[:, :, v], craw[:, v, :], ACT.Silu)
                        ins.then_inc(s_silu, 1)
                        act.dma_start(h[:, 0:NL], a["x"][0].rearrange("(t p) d -> p t d", p=P)).then_inc(s_h, 16)
                        act.dma_start(h[:, NL:NT], a["ctx"][0].rearrange("(t p) d -> p t d", p=P)).then_inc(s_h, 16)
                        act.wait_ge(s_emp, 2)
                        for l in range(2):
                            act.dma_start(slot_d[l].rearrange("(p b) c -> p (b c)", p=P), empty[:].rearrange("p b c -> p (b c)")).then_inc(s_emps, 16)
                        for l in range(2):
                            act.wait_ge(s_row, l + 1)
                            act.dma_start(mod_d[l], row[:, l]).then_inc(s_mod, 16)
                        act.wait_ge(s_mod, 32)
                        act.wait_ge(s_h, 32)
                        act.wait_ge(s_emps, 32)

                    @block.gpsimd
                    def _(pool):
                        pool.wait_ge(s_cst, 16)
                        nc.gpsimd.tensor_scalar(empty[:, :, 0], cst[:, C_IOTA:C_IOTA + 1].to_broadcast([P, TBL]), float(NT * P), None, ALU.add).then_inc(s_emp, 1)
                        nc.gpsimd.memset(empty[:, :, 1:2], 0).then_inc(s_emp, 1)

                    @block.tensor
                    def _(pe):
                        pe.wait_ge(s_silu, 1)
                        for i in range(2 * NCH):
                            pe.wait_ge(s_w[i % WB], 16 * (i // WB + 1))
                            if i >= 4:
                                pe.wait_ge(s_ev, i - 3)
                            for k in range(KD):
                                ins = nc.tensor.matmul(psA[:, i % 4], cs[:, k], wada[:, i % WB, k], start=(k == 0), stop=(k == KD - 1))
                            ins.then_inc(s_mm, 1)

                    @block.vector
                    def _(dve):
                        link = Chain(dve, s_dve)
                        dve.wait_ge(s_cst, 16)
                        nc.vector.tensor_copy(ident_b[:], ident)
                        nc.vector.tensor_copy(mask_b[:, 0], cst[:, C_MP:C_MP + P])
                        nc.vector.tensor_copy(mask_b[:, 1], cst[:, C_MN:C_MN + P])
                        dve.wait_ge(s_b, 96)
                        for i in range(2 * NCH):
                            l, n = i // NCH, i % NCH
                            j, half = n // 2, n % 2
                            dve.wait_ge(s_mm, i + 1)
                            seg = row[:, l, n * CH:(n + 1) * CH]
                            ins = nc.vector.tensor_tensor(seg, psA[:, i % 4], bias[:, l, n * CH:(n + 1) * CH], ALU.add)
                            ins.then_inc(s_ev, 1)
                            if j % 3 == 1:
                                dve.wait_ge(s_ev, i + 1)
                                ins = nc.vector.scalar_tensor_tensor(seg, seg, 1.0, gains[:, l, j // 3, half * CH:(half + 1) * CH], ALU.add, ALU.mult)
                                link(ins)
                            if n == NCH - 1:
                                dve.wait_ge(s_ev, i + 1)
                                nc.vector.tensor_copy(row[:, l, 0:1], row[:, l, 0:1]).then_inc(s_row, 1)

        def mod_rows(l, v, j):
            return mod_d[l, v:v + 1, j * D:(j + 1) * D].to_broadcast([P, D])

        def rope(dst, src, cos, sin, t1, t2, q, link):
            nc.vector.tensor_tensor(t1, src, cos, ALU.mult)
            s4 = src.rearrange("p g (b two q) -> p g b two q", two=2, q=q)
            t4 = t2.rearrange("p g (b two q) -> p g b two q", two=2, q=q)
            n4 = sin.rearrange("p g (b two q) -> p g b two q", two=2, q=q)
            for b in range(2):
                nc.vector.tensor_tensor(t4[:, :, b, 0], s4[:, :, b, 1], n4[:, :, b, 0], ALU.mult)
                ins = nc.vector.tensor_tensor(t4[:, :, b, 1], s4[:, :, b, 0], n4[:, :, b, 1], ALU.mult)
            link(ins)
            return nc.vector.tensor_tensor(dst, t1, t2, ALU.add)

        def bc(ap, n):
            return ap.unsqueeze(1).to_broadcast([ap.shape[0], n, ap.shape[1]])

        def bcl(ap, n):
            return ap.unsqueeze(len(ap.shape)).to_broadcast(list(ap.shape) + [n])

        def stage_project0(t_):
            qmT, kmT, vM, qsT, ksT, vS = (t_[n] for n in ("qmT", "kmT", "vM", "qsT", "ksT", "vS"))
            with ExitStack() as ctx:
                amul = sb(ctx, "B_amul", [P, D])
                aadd = sb(ctx, "B_aadd", [P, D])
                an = sb(ctx, "B_an", [P, D])
                aT = sb(ctx, "B_aT", [P, KD, P])
                w_in = sb(ctx, "w_in", [P, KD, EVEN_IN])
                w_uq = sb(ctx, "w_uq", [P, QR // P, MH * MQ])
                w_ukv = sb(ctx, "w_ukv", [P, KVR // P, MH * (NOPE + MV)])
                gq = sb(ctx, "B_gq", [P, QR // P])
                gkv = sb(ctx, "B_gkv", [P, KVR // P])
                junk = sb(ctx, "B_junk", [P, D], BF16)
                cn = sb(ctx, "B_cn", [P, QR + KVR])
                cT = sb(ctx, "B_cT", [P, 5, P])
                krr = sb(ctx, "B_krr", [P, ROPE])
                qst = sb(ctx, "B_qst", [P, SH // 2, 2, SD])
                kst = sb(ctx, "B_kst", [P, SKV * SD])
                qm = sb(ctx, "B_qm", [P, MH, MQ])
                km = sb(ctx, "B_km", [P, MH, MQ])
                t1 = sb(ctx, "B_t1", [P, 512])
                t2 = sb(ctx, "B_t2", [P, 512])
                st = sb(ctx, "B_st", [P, 3, 3])
                psC = ps(ctx, "B_psC", [P, 2, 512])
                psT = ps(ctx, "B_psT", [P, 2, KD, P])
                psU = ps(ctx, "B_psU", [P, 1024])
                s_w, s_ab = sem("B_w"), sem("B_ab")
                s_rt, s_an0, s_an = sem("B_rt"), sem("B_an0"), sem("B_an")
                s_tp, s_tev, s_ch, s_chev = sem("B_tp"), sem("B_tev"), sem("B_ch"), sem("B_chev")
                s_ss, s_crt, s_cn = sem("B_ss"), sem("B_crt"), sem("B_cn")
                s_st, s_u, s_uev = sem("B_st_ready"), sem("B_u"), sem("B_uev")
                s_dve, s_act = sem("B_dve"), sem("B_act")
                chunks = [(0, QR), (QR, KVR + ROPE), (QR + KVR + ROPE, SH * SD), (EVEN_IN - 2 * SKV * SD, 2 * SKV * SD)]
                cos = cst[:, C_COS:C_COS + NL * SD].rearrange("p (t d) -> p t d", t=NL)
                sin = cst[:, C_SIN:C_SIN + NL * SD].rearrange("p (t d) -> p t d", t=NL)
                cosm = cst[:, C_COSM:C_COSM + NL * ROPE].rearrange("p (t d) -> p t d", t=NL)
                sinm = cst[:, C_SINM:C_SINM + NL * ROPE].rearrange("p (t d) -> p t d", t=NL)
                uses = []
                for s in range(NT + 1):
                    if s < NT:
                        uses.append(("A", s))
                    if s >= 1:
                        uses += [("QS", s - 1), ("QM", s - 1)]
                    if s < NT:
                        uses.append(("C", s))
                    if s >= 1:
                        uses.append(("KM", s - 1))
                use = {u: n for n, u in enumerate(uses)}

                with nc.Block() as block:
                    @block.sync
                    def _(sp):
                        sp.dma_start(amul[:], mod_rows(0, 0, 1)).then_inc(s_ab, 16)
                        sp.dma_start(aadd[:], mod_rows(0, 0, 0)).then_inc(s_ab, 16)
                        wv = kview(a["wa_in"][0])
                        for c0, n in chunks:
                            sp.dma_start(w_in[:, :, c0:c0 + n], wv[:, :, c0:c0 + n]).then_inc(s_w, 16)
                        sp.dma_start(w_uq[:], kview(a["wa_uq"][0])).then_inc(s_w, 16)
                        sp.dma_start(w_ukv[:], kview(a["wa_ukv"][0])).then_inc(s_w, 16)
                        sp.dma_start(gq[:], a["ga_q"][0].rearrange("(p k) -> p k", p=P)).then_inc(s_w, 16)
                        sp.dma_start(gkv[:], a["ga_kv"][0].rearrange("(p k) -> p k", p=P)).then_inc(s_w, 16)
                        sp.wait_ge(s_an, NL)
                        sp.dma_start(amul[:], mod_rows(0, 1, 1)).then_inc(s_ab, 16)
                        sp.dma_start(aadd[:], mod_rows(0, 1, 0)).then_inc(s_ab, 16)

                    @block.gpsimd
                    def _(pool):
                        for t in range(NT):
                            pool.wait_ge(s_an0, t + 1)
                            nc.gpsimd.tensor_tensor(an[:], an[:], aadd[:], ALU.add).then_inc(s_an, 1)

                    @block.scalar
                    def _(act):
                        link = Chain(act, s_act)

                        def norm(t):
                            if t >= 1:
                                act.wait_ge(s_an0, t)
                            link(nc.scalar.activation(junk[:], h[:, t], ACT.Square, accum_out=st[:, 0, 0:1]))
                            nc.scalar.activation(st[:, 0, 1:2], st[:, 0, 0:1], ACT.Sqrt, bias=eps, scale=1.0 / D).then_inc(s_rt, 1)

                        def root_c(t):
                            act.wait_ge(s_ss, 2 * t + 2)
                            nc.scalar.activation(st[:, 1, 1:2], st[:, 1, 0:1], ACT.Sqrt, bias=eps, scale=1.0 / QR)
                            nc.scalar.activation(st[:, 2, 1:2], st[:, 2, 0:1], ACT.Sqrt, bias=eps, scale=1.0 / KVR).then_inc(s_crt, 1)

                        def evac(kind, t):
                            n = use[kind, t]
                            act.wait_ge(s_tp, n + 1)
                            src = psT[:, n % 2]
                            tok = slice(t * P, (t + 1) * P)
                            if kind == "A":
                                ins = nc.scalar.activation(aT[:], src, ACT.Copy)
                            elif kind == "C":
                                for k in range(3):
                                    nc.scalar.activation(cT[:, k], src[:, k], ACT.Copy, scale=gq[:, k:k + 1])
                                for k in range(2):
                                    ins = nc.scalar.activation(cT[:, 3 + k], src[:, 3 + k], ACT.Copy, scale=gkv[:, k:k + 1])
                            elif kind == "QS":
                                nc.scalar.activation(qsT[:, :, tok], src[:, 0:4], ACT.Copy, scale=float(SD) ** -0.5)
                                ins = nc.scalar.activation(ksT[:, tok], src[:, 4], ACT.Copy)
                            elif kind == "QM":
                                ins = nc.scalar.activation(qmT[:, :, tok], src[0:MQ], ACT.Copy, scale=float(MQ) ** -0.5)
                            else:
                                ins = nc.scalar.activation(kmT[:, :, tok], src[0:MQ], ACT.Copy)
                            ins.then_inc(s_tev, 1)

                        norm(0)
                        act.wait_ge(s_w, 16 * 8)
                        for s in range(NT + 1):
                            if s < NT:
                                evac("A", s)
                            if s + 1 < NT:
                                norm(s + 1)
                            if s >= 1:
                                evac("QS", s - 1)
                            if s < NT:
                                root_c(s)
                            if s >= 1:
                                evac("QM", s - 1)
                            if s < NT:
                                evac("C", s)
                            if s >= 1:
                                evac("KM", s - 1)

                    @block.vector
                    def _(dve):
                        link = Chain(dve, s_dve)

                        def norm(t):
                            dve.wait_ge(s_rt, t + 1)
                            link(nc.vector.reciprocal(st[:, 0, 2:3], st[:, 0, 1:2]))
                            dve.wait_ge(s_ab, 32 if t < NL else 64)
                            if t >= 1:
                                dve.wait_ge(s_ch, 4 * (t - 1) + 1)
                            nc.vector.scalar_tensor_tensor(an[:], h[:, t], st[:, 0, 2:3], amul[:], ALU.mult, ALU.mult).then_inc(s_an0, 1)

                        def chunk(t, c):
                            g = 4 * t + c
                            dve.wait_ge(s_ch, g + 1)
                            src = psC[:, g % 2]
                            lat = t < NL
                            if c < 2:
                                n, o = (QR, 0) if c == 0 else (KVR, QR)
                                if c == 0 and t >= 1:
                                    dve.wait_ge(s_tp, use["C", t - 1] + 1)
                                ins = nc.vector.tensor_copy(cn[:, o:o + n], src[:, 0:n])
                                if c == 1:
                                    if lat:
                                        link(ins)
                                        v = lambda x: x.rearrange("p (g d) -> p g d", g=1)
                                        ins = rope(v(krr[:]), v(src[:, n:n + ROPE]), v(cosm[:, t]), v(sinm[:, t]),
                                                   v(t1[:, 0:ROPE]), v(t2[:, 0:ROPE]), ROPE // 4, link)
                                    else:
                                        link(ins)
                                        ins = nc.vector.tensor_copy(krr[:], src[:, n:n + ROPE])
                                link(ins, s_chev)
                                link(nc.vector.tensor_tensor_reduce(t1[:, 0:n], cn[:, o:o + n], cn[:, o:o + n], 1.0, 0.0,
                                                                    ALU.mult, ALU.add, st[:, 1 + c, 0:1]), s_ss)
                            elif c == 2:
                                if t >= 1:
                                    dve.wait_ge(s_tp, use["QS", t - 1] + 1)
                                o = qst[:].rearrange("p j g d -> p g j d")
                                if lat:
                                    heads = src.rearrange("p (h d) -> p h d", d=SD)
                                    tt1 = t1[:].rearrange("p (h d) -> p h d", d=SD)
                                    tt2 = t2[:].rearrange("p (h d) -> p h d", d=SD)
                                    ins = rope_into(o, heads, t, tt1, tt2, link)
                                else:
                                    ins = nc.vector.tensor_copy(o, src.rearrange("p (g j d) -> p g j d", g=2, d=SD))
                                link(ins, s_chev)
                            else:
                                n = SKV * SD
                                if lat:
                                    v = lambda x: x.rearrange("p (h d) -> p h d", d=SD)
                                    link(rope(v(kst[:]), v(src[:, 0:n]), bc(cos[:, t], SKV), bc(sin[:, t], SKV),
                                              v(t1[:, 0:n]), v(t2[:, 0:n]), SD // 4, link))
                                else:
                                    nc.vector.tensor_copy(kst[:], src[:, 0:n])
                                link(nc.vector.tensor_copy(vS[:, t], src[:, n:2 * n]), s_chev)

                        def rope_into(o, heads, t, tt1, tt2, link):
                            nc.vector.tensor_tensor(tt1, heads, bc(cos[:, t], SH), ALU.mult)
                            q = SD // 4
                            s4 = heads.rearrange("p g (b two q) -> p g b two q", two=2, q=q)
                            t4 = tt2.rearrange("p g (b two q) -> p g b two q", two=2, q=q)
                            n4 = bc(sin[:, t], SH).rearrange("p g (b two q) -> p g b two q", two=2, q=q)
                            for b in range(2):
                                nc.vector.tensor_tensor(t4[:, :, b, 0], s4[:, :, b, 1], n4[:, :, b, 0], ALU.mult)
                                ins = nc.vector.tensor_tensor(t4[:, :, b, 1], s4[:, :, b, 0], n4[:, :, b, 1], ALU.mult)
                            link(ins)
                            g4 = lambda x: x.rearrange("p (g j) d -> p g j d", g=2)
                            return nc.vector.tensor_tensor(o, g4(tt1), g4(tt2), ALU.add)

                        def scale_c(t):
                            dve.wait_ge(s_crt, t + 1)
                            link(nc.vector.reciprocal(st[:, 1:3, 2], st[:, 1:3, 1]))
                            nc.vector.tensor_scalar(cn[:, 0:QR], cn[:, 0:QR], st[:, 1, 2:3], None, ALU.mult)
                            link(nc.vector.tensor_scalar(cn[:, QR:], cn[:, QR:], st[:, 2, 2:3], None, ALU.mult), s_cn)

                        def up_q(t):
                            dve.wait_ge(s_u, 2 * t + 1)
                            if t >= 1:
                                dve.wait_ge(s_tp, use["QM", t - 1] + 1)
                            src = psU[:, 0:MH * MQ].rearrange("p (h d) -> p h d", d=MQ)
                            ins = nc.vector.tensor_copy(qm[:, :, 0:NOPE], src[:, :, 0:NOPE])
                            r = src[:, :, NOPE:MQ]
                            if t < NL:
                                v = lambda x: x[:, 0:MH * ROPE].rearrange("p (h d) -> p h d", d=ROPE)
                                link(ins)
                                ins = rope(qm[:, :, NOPE:MQ], r, bc(cosm[:, t], MH), bc(sinm[:, t], MH), v(t1), v(t2), ROPE // 4, link)
                            else:
                                ins = nc.vector.tensor_copy(qm[:, :, NOPE:MQ], r)
                            link(ins, s_uev)

                        def up_kv(t):
                            dve.wait_ge(s_u, 2 * t + 2)
                            if t >= 1:
                                dve.wait_ge(s_tp, use["KM", t - 1] + 1)
                            src = psU[:].rearrange("p (h d) -> p h d", d=NOPE + MV)
                            nc.vector.tensor_copy(km[:, :, NOPE:MQ], bc(krr[:], MH))
                            nc.vector.tensor_copy(km[:, :, 0:NOPE], src[:, :, 0:NOPE])
                            link(nc.vector.tensor_copy(vM[:, t].rearrange("p (h d) -> p h d", d=MV), src[:, :, NOPE:]), s_uev)

                        norm(0)
                        for s in range(NT + 1):
                            if s >= 1:
                                up_kv(s - 1)
                            if s < NT:
                                chunk(s, 0)
                                chunk(s, 1)
                                scale_c(s)
                                if s + 1 < NT:
                                    norm(s + 1)
                                chunk(s, 2)
                                chunk(s, 3)
                                up_q(s)

                    @block.tensor
                    def _(pe):
                        def turn(kind, t):
                            n = use[kind, t]
                            if n >= 2:
                                pe.wait_ge(s_tev, n - 1)
                            dst = psT[:, n % 2]
                            if kind == "A":
                                pe.wait_ge(s_an, t + 1)
                                v = an[:].rearrange("q (p k) -> q k p", k=KD)
                                for k in range(KD):
                                    ins = nc.tensor.transpose(dst[:, k], v[:, k], ident)
                            elif kind == "C":
                                pe.wait_ge(s_cn, t + 1)
                                v = cn[:, 0:QR].rearrange("q (p k) -> q k p", k=3)
                                for k in range(3):
                                    nc.tensor.transpose(dst[:, k], v[:, k], ident)
                                v = cn[:, QR:].rearrange("q (p k) -> q k p", k=2)
                                for k in range(2):
                                    ins = nc.tensor.transpose(dst[:, 3 + k], v[:, k], ident)
                            elif kind == "QS":
                                pe.wait_ge(s_chev, 4 * t + 4)
                                for j in range(SH // 2):
                                    nc.tensor.transpose(dst[:, j], qst[:, j].rearrange("p g d -> p (g d)"), ident)
                                ins = nc.tensor.transpose(dst[:, 4], kst[:], ident)
                            else:
                                pe.wait_ge(s_uev, 2 * t + (1 if kind == "QM" else 2))
                                x = qm if kind == "QM" else km
                                for i in range(MH):
                                    ins = nc.tensor.transpose(dst[0:MQ, i], x[:, i], ident)
                            ins.then_inc(s_tp, 1)

                        def chunk(t, c):
                            g = 4 * t + c
                            if g >= 2:
                                pe.wait_ge(s_chev, g - 1)
                            if c == 0:
                                pe.wait_ge(s_tev, use["A", t] + 1)
                            c0, n = chunks[c]
                            for k in range(KD):
                                ins = nc.tensor.matmul(psC[:, g % 2, 0:n], aT[:, k], w_in[:, k, c0:c0 + n], start=(k == 0), stop=(k == KD - 1))
                            ins.then_inc(s_ch, 1)

                        def up(t, i):
                            n = 2 * t + i
                            if n >= 1:
                                pe.wait_ge(s_uev, n)
                            if i == 0:
                                pe.wait_ge(s_tev, use["C", t] + 1)
                            w, k0, nk, cols = (w_uq, 0, 3, MH * MQ) if i == 0 else (w_ukv, 3, 2, MH * (NOPE + MV))
                            for c0 in range(0, cols, 512):
                                c1 = min(c0 + 512, cols)
                                for k in range(nk):
                                    ins = nc.tensor.matmul(psU[:, c0:c1], cT[:, k0 + k], w[:, k, c0:c1], start=(k == 0), stop=(k == nk - 1))
                            ins.then_inc(s_u, 1)

                        pe.wait_ge(s_w, 16 * 8)
                        for s in range(NT + 1):
                            if s < NT:
                                turn("A", s)
                            if s >= 1:
                                up(s - 1, 1)
                            if s < NT:
                                chunk(s, 0)
                            if s >= 1:
                                turn("QS", s - 1)
                            if s < NT:
                                chunk(s, 1)
                            if s >= 1:
                                turn("QM", s - 1)
                            if s < NT:
                                chunk(s, 2)
                                turn("C", s)
                            if s >= 1:
                                turn("KM", s - 1)
                            if s < NT:
                                chunk(s, 3)
                                up(s, 0)

        def stage_attend0(t_, o):
            qmT, kmT, vM, qsT, ksT, vS = (t_[n] for n in ("qmT", "kmT", "vM", "qsT", "ksT", "vS"))
            units = [(t, kind, hd) for t in range(NT) for kind in range(2) for hd in range(8)]
            N = len(units)

            def keys(t, kind):
                lat = [] if t >= NL else list(range(NL)) if kind == 0 else list(range(max(0, t - 1), min(NL, t + 2)))
                return lat + list(range(NL, NT)), 512 - P * len(lat)

            with ExitStack() as ctx:
                prob = sb(ctx, "C_prob", [P, 3, NT * P])
                pT = sb(ctx, "C_pT", [P, 2, NT, P])
                sink = sb(ctx, "C_sink", [P, 8])
                nsink = sb(ctx, "C_nsink", [P, 8])
                nmax = sb(ctx, "C_nmax", [P, 2 * NT, 8])
                ssum = sb(ctx, "C_ssum", [P, 2 * NT, 8])
                sdif = sb(ctx, "C_sdif", [P, 2, 8])
                psS = ps(ctx, "C_psS", [P, 2, 1024])
                psP = ps(ctx, "C_psP", [P, 2, 4, P])
                psO = ps(ctx, "C_psO", [P, 2, 512])
                s_sink, s_s, s_nm, s_e = sem("C_sink_in"), sem("C_s"), sem("C_nm"), sem("C_e")
                s_t, s_pv, s_evd, s_eva = sem("C_t"), sem("C_pv"), sem("C_evd"), sem("C_eva")
                s_sd, s_se, s_o, s_dve, s_act = sem("C_sd"), sem("C_se"), sem("C_o"), sem("C_dve"), sem("C_act")

                def place(n, b):
                    first = (n + 1) // 2
                    return (0, b) if b < first else (1, b - first)

                with nc.Block() as block:
                    @block.sync
                    def _(sp):
                        sp.dma_start(sink[:], a["wa_sink"][0:1, :].to_broadcast([P, 8])).then_inc(s_sink, 16)

                    @block.tensor
                    def _(pe):
                        def scores(i):
                            t, kind, hd = units[i]
                            if i >= 2:
                                pe.wait_ge(s_e, i - 1)
                            ks, c0 = keys(t, kind)
                            if kind == 0:
                                q, kT = qmT[:, hd, t * P:(t + 1) * P], kmT[:, hd]
                            else:
                                g, j = divmod(hd, SH // SKV)
                                q, kT = qsT[64 * g:64 * g + 64, j, t * P:(t + 1) * P], ksT[64 * g:64 * g + 64]
                            masks = []
                            if kind == 1 and t < NL:
                                masks = [(c0 + n * P, 0 if k < t else 1) for n, k in enumerate(ks) if k < NL and k != t]
                            if c0 < 512:
                                nc.tensor.matmul(psS[:, i % 2, c0:512], q, kT[:, ks[0] * P:ks[0] * P + 512 - c0], start=True, stop=not masks)
                            for n, (c, m) in enumerate(masks):
                                nc.tensor.matmul(psS[:, i % 2, c:c + P], ident_b[:], mask_b[:, m], start=False, stop=n == len(masks) - 1)
                            nc.tensor.matmul(psS[:, i % 2, 512:512 + CTX], q, kT[:, SEQ:], start=True, stop=True).then_inc(s_s, 1)

                        def turn(i):
                            t, kind, hd = units[i]
                            pe.wait_ge(s_e, i + 1)
                            if i >= 1:
                                pe.wait_ge(s_evd, i)
                                pe.wait_ge(s_eva, i)
                            n = len(keys(t, kind)[0])
                            for b in range(n):
                                bank, c = place(n, b)
                                ins = nc.tensor.transpose(psP[:, bank, c], prob[:, i % 3, b * P:(b + 1) * P], ident)
                            ins.then_inc(s_t, 1)

                        def values(i):
                            t, kind, hd = units[i]
                            pe.wait_ge(s_evd, i + 1)
                            pe.wait_ge(s_eva, i + 1)
                            g = i // 8
                            if i % 8 == 0 and g >= 2:
                                pe.wait_ge(s_o, g - 1)
                            ks, _ = keys(t, kind)
                            for n, k in enumerate(ks):
                                v = vM[:, k, hd * MV:(hd + 1) * MV] if kind == 0 else vS[:, k, hd // 4 * SD:hd // 4 * SD + SD]
                                ins = nc.tensor.matmul(psO[:, g % 2, hd * 64:(hd + 1) * 64], pT[:, i % 2, n], v, start=(n == 0), stop=(n == len(ks) - 1))
                            ins.then_inc(s_pv, 1)

                        for i in range(N + 3):
                            if i < N:
                                scores(i)
                            if 2 <= i < N + 2:
                                turn(i - 2)
                            if i >= 3:
                                values(i - 3)

                    @block.vector
                    def _(dve):
                        link = Chain(dve, s_dve)
                        dve.wait_ge(s_sink, 16)
                        link(nc.vector.tensor_scalar(nsink[:], sink[:], -1.0, None, ALU.mult))

                        def maximum(i):
                            t, kind, hd = units[i]
                            g = i // 8
                            dve.wait_ge(s_s, i + 1)
                            ks, c0 = keys(t, kind)
                            m = nmax[:, g, hd:hd + 1]
                            ins = nc.vector.tensor_reduce(m, psS[:, i % 2, c0:512 + CTX], AX, ALU.max, negate=True)
                            if kind == 1:
                                link(ins)
                                ins = nc.vector.tensor_tensor(m, m, nsink[:, hd:hd + 1], ALU.min)
                            link(ins, s_nm)

                        def evac(i):
                            n = len(keys(*units[i][:2])[0])
                            dve.wait_ge(s_t, i + 1)
                            if i >= 2:
                                dve.wait_ge(s_pv, i - 1)
                            f = (n + 1) // 2
                            nc.vector.tensor_copy(pT[:, i % 2, 0:f], psP[:, 0, 0:f]).then_inc(s_evd, 1)

                        def divide(g):
                            t, kind = g // 2, g % 2
                            sl = ssum[:, g]
                            if kind == 1:
                                dve.wait_ge(s_se, t + 1)
                                link(nc.vector.tensor_tensor(sl, sl, sdif[:, t % 2], ALU.add))
                            else:
                                dve.wait_ge(s_e, 8 * g + 8)
                            link(nc.vector.reciprocal(sl, sl))
                            dve.wait_ge(s_pv, 8 * g + 8)
                            nc.vector.tensor_tensor(o[:, t, kind * 512:(kind + 1) * 512].rearrange("p (h d) -> p h d", d=64),
                                                    psO[:, g % 2].rearrange("p (h d) -> p h d", d=64), bcl(sl, 64), ALU.mult).then_inc(s_o, 1)

                        for i in range(N + 4):
                            if i < N:
                                maximum(i)
                            if 2 <= i < N + 2:
                                evac(i - 2)
                            if i % 8 == 1 and i > 8 and (i // 8 - 1) % 2 == 1:
                                g = i // 8 - 1
                                if g // 2 >= 2:
                                    dve.wait_ge(s_se, g // 2 - 1)
                                link(nc.vector.tensor_tensor(sdif[:, g // 2 % 2], sink[:], nmax[:, g], ALU.add), s_sd)
                            if i >= 11 and (i - 11) % 8 == 0:
                                divide((i - 11) // 8)

                    @block.scalar
                    def _(act):
                        link = Chain(act, s_act)
                        for i in range(N + 4):
                            if i < N:
                                t, kind, hd = units[i]
                                ks, c0 = keys(t, kind)
                                act.wait_ge(s_nm, i + 1)
                                if i >= 3:
                                    act.wait_ge(s_t, i - 2)
                                g = i // 8
                                nc.scalar.activation(prob[:, i % 3, 0:len(ks) * P], psS[:, i % 2, c0:512 + CTX], ACT.Exp,
                                                     bias=nmax[:, g, hd:hd + 1], accum_out=ssum[:, g, hd:hd + 1]).then_inc(s_e, 1)
                            if 2 <= i < N + 2:
                                j = i - 2
                                n = len(keys(*units[j][:2])[0])
                                f = (n + 1) // 2
                                act.wait_ge(s_t, j + 1)
                                if j >= 2:
                                    act.wait_ge(s_pv, j - 1)
                                nc.scalar.activation(pT[:, j % 2, f:n], psP[:, 1, 0:n - f], ACT.Copy).then_inc(s_eva, 1)
                            if i % 8 == 1 and i > 8 and (i // 8 - 1) % 2 == 1:
                                g = i // 8 - 1
                                act.wait_ge(s_sd, g // 2 + 1)
                                nc.scalar.activation(sdif[:, g // 2 % 2], sdif[:, g // 2 % 2], ACT.Exp).then_inc(s_se, 1)

        def stage_out(l, nt, o, fT, lg, w_out_in, gain_in):
            with ExitStack() as ctx:
                w_out = sb(ctx, f"D{l}_w", [P, KD, D])
                w_r = sb(ctx, f"D{l}_wr", [P, KD, NE])
                gsub = sb(ctx, f"D{l}_gs", [P, 1])
                gate = sb(ctx, f"D{l}_gate", [P, 2, D])
                fmul = sb(ctx, f"D{l}_fmul", [P, 2, D])
                fadd = sb(ctx, f"D{l}_fadd", [P, 2, D])
                oT = sb(ctx, f"D{l}_oT", [P, 2, KD, P])
                y = sb(ctx, f"D{l}_y", [P, D])
                f = sb(ctx, f"D{l}_f", [P, 2, D])
                junk = sb(ctx, f"D{l}_junk", [P, D], BF16)
                st = sb(ctx, f"D{l}_st", [P, 3])
                psT = ps(ctx, f"D{l}_psT", [P, 2, KD, P])
                psY = ps(ctx, f"D{l}_psY", [P, 2, 512])
                psR = ps(ctx, f"D{l}_psR", [P, 512])
                S = lambda n: sem(f"D{l}_{n}_s")
                s_w, s_v, s_to, s_oT, s_y, s_yev, s_h = S("w"), S("v"), S("to"), S("oT"), S("y"), S("yev"), S("h")
                s_rt, s_f0, s_f, s_r, s_lg, s_act, s_dve = S("rt"), S("f0"), S("f"), S("r"), S("lg"), S("act"), S("dve")
                s_fd = [S("fd0"), S("fd1")]
                nv = 2 if nt > NL else 1

                uses = [("O", 0)]
                for t in range(nt + 1):
                    if t + 1 < nt:
                        uses.append(("O", t + 1))
                    if t >= 1:
                        uses.append(("F", t - 1))
                use = {u: n for n, u in enumerate(uses)}

                with nc.Block() as block:
                    @block.sync
                    def _(sp):
                        sp.dma_start(w_out[:], w_out_in.rearrange("(k p) n -> p k n", p=P)).then_inc(s_w, 16)
                        sp.dma_start(w_r[:], kview(a["w_router"][l])).then_inc(s_w, 16)
                        for t in range(nt):
                            sp.wait_ge(s_f, t + 1)
                            sp.dma_start(f_d[l][t * P:(t + 1) * P], f[:, t % 2]).then_inc(s_fd[t % 2], 16)
                        for b in range(2):
                            sp.wait_ge(s_fd[b], 16 * ((nt - b + 1) // 2))

                    @block.scalar
                    def _(act):
                        link = Chain(act, s_act)
                        for v in range(nv):
                            act.dma_start(gate[:, v], mod_rows(l, v, 2)).then_inc(s_v, 16)
                            act.dma_start(fmul[:, v], mod_rows(l, v, 4)).then_inc(s_v, 16)
                            act.dma_start(fadd[:, v], mod_rows(l, v, 3)).then_inc(s_v, 16)
                        if gain_in is not None:
                            act.dma_start(gsub[:], gain_in.rearrange("(p o) -> p o", o=1)).then_inc(s_v, 16)
                            act.wait_ge(s_v, 16 * (3 * nv + 1))
                            link(nc.scalar.mul(gsub[:], gsub[:], 1.0 - LAM_INIT))

                        def evac(kind, t):
                            n = use[kind, t]
                            act.wait_ge(s_to, n + 1)
                            if kind == "O":
                                for b in range(2):
                                    sl = slice(4 * b, 4 * b + 4)
                                    ins = nc.scalar.activation(oT[:, t % 2, sl], psT[:, n % 2, sl], ACT.Copy, scale=1.0 if gain_in is None else gsub[:, 0:1])
                            else:
                                ins = nc.scalar.activation(fT[:, :, t * P:(t + 1) * P], psT[:, n % 2], ACT.Copy)
                            ins.then_inc(s_oT, 1)

                        def norm(t):
                            act.wait_ge(s_h, t + 1)
                            if t >= 1:
                                act.wait_ge(s_f0, t)
                            link(nc.scalar.activation(junk[:], h[:, t], ACT.Square, accum_out=st[:, 0:1]))
                            nc.scalar.activation(st[:, 1:2], st[:, 0:1], ACT.Sqrt, bias=eps, scale=1.0 / D).then_inc(s_rt, 1)

                        evac("O", 0)
                        for t in range(nt + 1):
                            if t + 1 < nt:
                                evac("O", t + 1)
                            if t >= 1:
                                evac("F", t - 1)
                            if t < nt:
                                norm(t)

                    @block.vector
                    def _(dve):
                        link = Chain(dve, s_dve)
                        dve.wait_ge(s_v, 16 * (3 * nv + (gain_in is not None)))

                        def logits(t):
                            dve.wait_ge(s_r, t + 1)
                            nc.vector.tensor_copy(lg[:, t], psR[:, 0:NE]).then_inc(s_lg, 1)

                        for t in range(nt):
                            v = 0 if t < NL else 1
                            dve.wait_ge(s_y, t + 1)
                            if t >= 1:
                                dve.wait_ge(s_h, t)
                            for b in range(2):
                                sl = slice(512 * b, 512 * b + 512)
                                ins = nc.vector.tensor_tensor(y[:, sl], psY[:, b], gate[:, v, sl], ALU.mult)
                            ins.then_inc(s_yev, 1)
                            if t >= 1:
                                logits(t - 1)
                            dve.wait_ge(s_rt, t + 1)
                            link(nc.vector.reciprocal(st[:, 2:3], st[:, 1:2]))
                            if t >= 2:
                                dve.wait_ge(s_fd[t % 2], 16 * (t // 2))
                                dve.wait_ge(s_to, use["F", t - 2] + 1)
                            nc.vector.scalar_tensor_tensor(f[:, t % 2], h[:, t], st[:, 2:3], fmul[:, v], ALU.mult, ALU.mult).then_inc(s_f0, 1)
                        logits(nt - 1)

                    @block.gpsimd
                    def _(pool):
                        for t in range(nt):
                            v = 0 if t < NL else 1
                            pool.wait_ge(s_yev, t + 1)
                            nc.gpsimd.tensor_tensor(h[:, t], h[:, t], y[:], ALU.add).then_inc(s_h, 1)
                            pool.wait_ge(s_f0, t + 1)
                            nc.gpsimd.tensor_tensor(f[:, t % 2], f[:, t % 2], fadd[:, v], ALU.add).then_inc(s_f, 1)

                    @block.tensor
                    def _(pe):
                        def turn(kind, t):
                            n = use[kind, t]
                            if n >= 2:
                                pe.wait_ge(s_oT, n - 1)
                            if kind == "F":
                                pe.wait_ge(s_f, t + 1)
                                v = f[:, t % 2].rearrange("q (p k) -> q k p", k=KD)
                            else:
                                v = o[:, t].rearrange("q (k p) -> q k p", p=P)
                            for k in range(KD):
                                ins = nc.tensor.transpose(psT[:, n % 2, k], v[:, k], ident)
                            ins.then_inc(s_to, 1)

                        turn("O", 0)
                        pe.wait_ge(s_w, 32)
                        for t in range(nt + 1):
                            if t + 1 < nt:
                                turn("O", t + 1)
                            if t < nt:
                                pe.wait_ge(s_oT, use["O", t] + 1)
                                if t >= 1:
                                    pe.wait_ge(s_yev, t)
                                for b in range(2):
                                    for k in range(KD):
                                        ins = nc.tensor.matmul(psY[:, b], oT[:, t % 2, k], w_out[:, k, b * 512:(b + 1) * 512], start=(k == 0), stop=(k == KD - 1))
                                ins.then_inc(s_y, 1)
                            if t >= 1:
                                turn("F", t - 1)
                                pe.wait_ge(s_oT, use["F", t - 1] + 1)
                                if t >= 2:
                                    pe.wait_ge(s_lg, t - 1)
                                for k in range(KD):
                                    ins = nc.tensor.matmul(psR[:, 0:NE], fT[:, k, (t - 1) * P:t * P], w_r[:, k], start=(k == 0), stop=(k == KD - 1))
                                ins.then_inc(s_r, 1)

        def stage_route(l, nt, fT, lg):
            NB8 = nt * TOPK
            with ExitStack() as ctx:
                S = lambda n: sem(f"E{l}_{n}_s")
                T = lambda n, shape, dt=F32: sb(ctx, f"E{l}_{n}", shape, dt)
                wgu = T("wgu", [P, 2, KD, FF])
                wd = T("wd", [P, KF, D])
                sg = T("sg", [P, 2, FF])
                up = T("up", [P, 2, FF])
                hT = T("hT", [P, 2, KF, P])
                ysh = T("ysh", [P, 2, D])
                brt = T("brt", [P, NE])
                sc = T("sc", [P, nt, NE])
                bi = T("bi", [P, nt, NE])
                srt = T("srt", [P, nt * NG, 8])
                gs = T("gs", [P, nt, NG])
                cmp1 = T("cmp1", [P, nt, NG, NG])
                cmp2 = T("cmp2", [P, nt, NG, NG])
                gm = T("gm", [P, nt * NG])
                rep = T("rep", [P, nt, NE])
                top8 = T("top8", [P, nt, 8])
                sel = T("sel", [P, nt, NE])
                wt = T("wt", [P, nt, NE])
                tot = T("tot", [P, nt])
                nb = T("nb", [P, NE])
                bend = T("bend", [P, NE])
                bst = T("bst", [P, NE])
                v = T("v", [P, nt, NE])
                v8 = T("v8", [P, nt, 8])
                w8 = T("w8", [P, nt, 8])
                eq = T("eq", [P, nt, 8, NE])
                d8 = T("d8", [P, NB8], I32)
                d8p = T("d8p", [P, NB8], I32)
                d8b = T("d8b", [P, NB8], I32)
                dest = T("dest", [P, NB8], I32)
                pay = T("pay", [P, NB8, 2], I32)
                zero = T("zero", [P, D])
                ones = cst[:, C_ONE:C_ONE + P]
                upper = cst[:, C_U:C_U + P]
                psG = ps(ctx, f"E{l}_psG", [P, 2, 512])
                psH = ps(ctx, f"E{l}_psH", [P, 4, P])
                psY = ps(ctx, f"E{l}_psY", [P, 2, 512])
                psK = ps(ctx, f"E{l}_psK", [P, 512])
                psN = ps(ctx, f"E{l}_psN", [P, 512])
                s_w, s_br, s_sig = S("w"), S("br"), S("sig")
                s_gu, s_gc, s_hm, s_ht, s_hT, s_dn, s_ys = S("gu"), S("gc"), S("hm"), S("ht"), S("hT"), S("dn"), S("ys")
                s_yd = [S("yd0"), S("yd1")]
                s_sel, s_rk, s_tab, s_scat, s_dve, s_z, s_zd = S("sel"), S("rk"), S("tab"), S("scat"), S("dve"), S("z"), S("zd")
                POOLT = min(3, nt - 1)

                with nc.Block() as block:
                    @block.sync
                    def _(sp):
                        sp.dma_start(brt[:], a["b_router"][l:l + 1, :].to_broadcast([P, NE])).then_inc(s_br, 16)
                        sp.dma_start(wgu[:, 0], kview(a["ws_gate"][l])).then_inc(s_w, 16)
                        sp.dma_start(wgu[:, 1], kview(a["ws_up"][l])).then_inc(s_w, 16)
                        sp.dma_start(wd[:], kview(a["ws_down"][l])).then_inc(s_w, 16)
                        sp.wait_ge(s_z, 1)
                        sp.dma_start(acc_d[l][NT * P:], zero[:]).then_inc(s_zd, 16)
                        for t in range(nt):
                            sp.wait_ge(s_ys, t + 1)
                            sp.dma_start(acc_d[l][t * P:(t + 1) * P], ysh[:, t % 2]).then_inc(s_yd[t % 2], 16)
                        for b in range(2):
                            sp.wait_ge(s_yd[b], 16 * ((nt - b + 1) // 2))
                        sp.wait_ge(s_zd, 16)

                    @block.tensor
                    def _(pe):
                        def gate_up(t):
                            for k in range(KD):
                                ins = nc.tensor.matmul(psG[:, t % 2].rearrange("p (v f) -> p v f", v=2), fT[:, k, t * P:(t + 1) * P], wgu[:, :, k],
                                                       start=(k == 0), stop=(k == KD - 1))
                            ins.then_inc(s_gu, 1)

                        def turn(t):
                            pe.wait_ge(s_hm, t + 1)
                            if t >= 1:
                                pe.wait_ge(s_hT, t)
                            x = up[:, t % 2].rearrange("q (p k) -> q k p", k=KF)
                            for k in range(KF):
                                ins = nc.tensor.transpose(psH[:, k], x[:, k], ident)
                            ins.then_inc(s_ht, 1)

                        def down(t):
                            pe.wait_ge(s_hT, t + 1)
                            if t >= 1:
                                pe.wait_ge(s_ys, t)
                            for b in range(2):
                                for k in range(KF):
                                    ins = nc.tensor.matmul(psY[:, b], hT[:, t % 2, k], wd[:, k, b * 512:(b + 1) * 512], start=(k == 0), stop=(k == KF - 1))
                            ins.then_inc(s_dn, 1)

                        def ranks():
                            pe.wait_ge(s_sel, 1)
                            for t in range(nt):
                                for j in range(t + 1):
                                    nc.tensor.matmul(psK[:, t * NE:(t + 1) * NE], upper if j == t else ones, sel[:, j], start=(j == 0), stop=(j == t))
                            for j in range(nt):
                                ins = nc.tensor.matmul(psN[:, 0:NE], ones, sel[:, j], start=(j == 0), stop=(j == nt - 1))
                            ins.then_inc(s_rk, 1)

                        pe.wait_ge(s_w, 48)
                        gate_up(0)
                        for t in range(nt):
                            if t + 1 < nt:
                                if t + 1 == POOLT:
                                    ranks()
                                gate_up(t + 1)
                            turn(t)
                            down(t)

                    @block.scalar
                    def _(act):
                        nc.scalar.activation(sc[:], lg[:, 0:nt], ACT.Sigmoid).then_inc(s_sig, 1)

                        def copies(t):
                            act.wait_ge(s_gu, t + 1)
                            if t >= 2:
                                act.wait_ge(s_ht, t - 1)
                            nc.scalar.activation(sg[:, t % 2], psG[:, t % 2, 0:FF], ACT.Silu)
                            nc.scalar.activation(up[:, t % 2], psG[:, t % 2, FF:2 * FF], ACT.Copy).then_inc(s_gc, 1)

                        copies(0)
                        for t in range(nt):
                            if t + 1 < nt:
                                copies(t + 1)
                            act.wait_ge(s_ht, t + 1)
                            nc.scalar.activation(hT[:, t % 2], psH[:, 0:KF], ACT.Copy).then_inc(s_hT, 1)
                            act.wait_ge(s_dn, t + 1)
                            if t >= 2:
                                act.wait_ge(s_yd[t % 2], 16 * (t // 2))
                            nc.scalar.activation(ysh[:, t % 2].rearrange("p (b n) -> p b n", b=2), psY[:], ACT.Copy).then_inc(s_ys, 1)

                    @block.gpsimd
                    def _(pool):
                        nc.gpsimd.memset(zero[:], 0.0).then_inc(s_z, 1)
                        for t in range(POOLT):
                            pool.wait_ge(s_gc, t + 1)
                            nc.gpsimd.tensor_tensor(up[:, t % 2], up[:, t % 2], sg[:, t % 2], ALU.mult).then_inc(s_hm, 1)
                        pool.wait_ge(s_tab, 1)
                        for i in range(NB8):
                            pool.indirect_dma_start(slot_d[l], bass.IndirectOffsetOnAxis(ap=dest[:, i:i + 1].bitcast(U32), axis=0),
                                                    pay[:, i], None).then_inc(s_scat, 16)
                        pool.wait_ge(s_scat, 16 * NB8)

                    @block.vector
                    def _(dve):
                        link = Chain(dve, s_dve)
                        V = nc.vector
                        dve.wait_ge(s_sig, 1)
                        dve.wait_ge(s_br, 16)
                        link(V.tensor_tensor(bi[:], sc[:], bc(brt[:], nt), ALU.add))
                        big = bi[:].rearrange("p t (g e) -> p (t g) e", g=NG)
                        for i in range(nt * NG):
                            ins = V.max(srt[:, i], big[:, i])
                        link(ins)
                        link(V.tensor_tensor(gs[:].rearrange("p t g -> p (t g)"), srt[:, :, 0], srt[:, :, 1], ALU.add))
                        me = bcl(gs[:], NG)
                        other = gs[:].unsqueeze(2).to_broadcast([P, nt, NG, NG])
                        tri = cst[:, C_TRI:C_TRI + NG * NG]
                        f3 = lambda x: x.rearrange("p t i j -> p t (i j)")
                        V.tensor_tensor(cmp1[:], other, me, ALU.is_gt)
                        link(V.tensor_tensor(cmp2[:], other, me, ALU.is_equal))
                        link(V.tensor_tensor(f3(cmp2[:]), f3(cmp2[:]), bc(tri, nt), ALU.mult))
                        link(V.tensor_tensor(cmp1[:], cmp1[:], cmp2[:], ALU.add))
                        link(V.tensor_reduce(gm[:], cmp1[:].rearrange("p t i j -> p (t i) j"), AX, ALU.add))
                        link(V.tensor_scalar(gm[:], gm[:], float(TOPG) - 0.5, None, ALU.is_lt))
                        link(V.tensor_tensor(big, big, bcl(gm[:], NE // NG), ALU.mult))
                        link(V.tensor_scalar(gm[:], gm[:], -NEG, NEG, ALU.mult, ALU.add))
                        link(V.tensor_tensor(big, big, bcl(gm[:], NE // NG), ALU.add))
                        for t in range(nt):
                            ins = V.max(top8[:, t], bi[:, t])
                        link(ins)
                        for t in range(nt):
                            ins = V.match_replace(rep[:, t], top8[:, t], bi[:, t], -3e38)
                        link(ins)
                        link(V.tensor_tensor(sel[:], bi[:], rep[:], ALU.is_gt), s_sel)
                        link(V.tensor_tensor(wt[:], sc[:], sel[:], ALU.mult))
                        link(V.tensor_reduce(tot[:], wt[:], AX, ALU.add))
                        link(V.reciprocal(tot[:], tot[:]))
                        link(V.tensor_scalar(tot[:], tot[:], ROUTED, None, ALU.mult))
                        link(V.tensor_tensor(wt[:], wt[:], bcl(tot[:], NE), ALU.mult))
                        dve.wait_ge(s_rk, 1)
                        link(V.tensor_scalar(nb[:], psN[:, 0:NE], P + 0.5, 1.0, ALU.is_gt, ALU.add))
                        for j in range(2, nt):
                            link(V.scalar_tensor_tensor(nb[:], psN[:, 0:NE], P * j + 0.5, nb[:], ALU.is_gt, ALU.add))
                        link(V.tensor_tensor_scan(bend[:], ones[:, 0:NE], nb[:], 0.0, ALU.mult, ALU.add))
                        link(V.tensor_tensor(bst[:], bend[:], nb[:], ALU.subtract))
                        V.tensor_copy(starts_i[0:1, 0:NE], bst[0:1])
                        link(V.tensor_copy(starts_i[0:1, NE:NE + 1], bend[0:1, NE - 1:NE]))
                        link(V.tensor_scalar(bst[:], bst[:], -float(P), float(FAR), ALU.mult, ALU.add))
                        rk = psK[:, 0:nt * NE].rearrange("p (t e) -> p t e", e=NE)
                        link(V.tensor_tensor(v[:], bc(bst[:], nt), rk, ALU.subtract))
                        link(V.tensor_tensor(v[:], v[:], sel[:], ALU.mult))
                        for t in range(nt):
                            ins = V.max(v8[:, t], v[:, t])
                        link(ins)
                        for t in range(nt):
                            V.tensor_tensor(eq[:, t], v[:, t].unsqueeze(1).to_broadcast([P, 8, NE]), bcl(v8[:, t], NE), ALU.is_equal).then_inc(s_dve, 1)
                            link.count[id(s_dve)] += 1
                        dve.wait_ge(s_dve, link.count[id(s_dve)])
                        for t in range(nt):
                            ins = V.tensor_tensor(eq[:, t], eq[:, t], bc(wt[:, t], 8), ALU.mult)
                        link(ins)
                        link(V.tensor_reduce(w8[:].rearrange("p t k -> p (t k)"), eq[:].rearrange("p t k e -> p (t k) e"), AX, ALU.add))
                        v8f = v8[:].rearrange("p t k -> p (t k)")
                        link(V.tensor_scalar(d8[:], v8f, -1.0, float(FAR), ALU.mult, ALU.add))
                        V.tensor_scalar(d8p[:], d8[:], P - 1, None, ALU.bitwise_and)
                        link(V.tensor_scalar(d8b[:], d8[:], 7, None, ALU.arith_shift_right))
                        link(V.scalar_tensor_tensor(dest[:], d8p[:], float(TBL), d8b[:], ALU.mult, ALU.add))
                        tok = cst[:, C_TOK:C_TOK + nt]
                        V.tensor_copy(pay[:, :, 0].rearrange("p (t k) -> p t k", k=8), bcl(tok, 8))
                        V.tensor_copy(pay[:, :, 1].bitcast(F32), w8[:].rearrange("p t k -> p (t k)")).then_inc(s_tab, 1)
                        for t in range(POOLT, nt):
                            dve.wait_ge(s_gc, t + 1)
                            dve.wait_ge(s_hm, t)
                            V.tensor_tensor(up[:, t % 2], up[:, t % 2], sg[:, t % 2], ALU.mult).then_inc(s_hm, 1)

        def stage_experts(l, nt):
            with ExitStack() as ctx:
                S = lambda n: sem(f"F{l}_{n}_s")
                T = lambda n, shape, dt=F32: sb(ctx, f"F{l}_{n}", shape, dt)
                PARTS, AWAY = 6, 3
                slots = T("slots", [P, TBL, 2], I32)
                gu_raw = T("gu_raw", [P, 2, 2, KD, FF])
                d_raw = T("d_raw", [P, 2, KF, D])
                gu_hi = T("gu_hi", [P, 2, 2, KD, FF], F32R)
                gu_lo = T("gu_lo", [P, 2, 2, KD, FF], F32R)
                d_hi = T("d_hi", [P, 2, KF, D], F32R)
                d_lo = T("d_lo", [P, 2, KF, D], F32R)
                xb = T("xb", [P, D])
                xT_hi = T("xT_hi", [P, KD, P], F32R)
                xT_lo = T("xT_lo", [P, KD, P], F32R)
                sil = T("sil", [P, FF])
                hh = T("hh", [P, FF])
                hT_hi = T("hT_hi", [P, KF, P], F32R)
                hT_lo = T("hT_lo", [P, KF, P], F32R)
                yb = T("yb", [P, D])
                gi = T("gi", [P, 1], I32)
                si = T("si", [P, 2], I32)
                psX = ps(ctx, f"F{l}_psX", [P, 2, 4, P])
                psG = ps(ctx, f"F{l}_psG", [P, 512])
                psH = ps(ctx, f"F{l}_psH", [P, 4, P])
                psY = ps(ctx, f"F{l}_psY", [P, 2, 512])
                s_slots, s_xb0 = S("slots"), S("xb0")
                s_raw, s_x = [S(f"raw{i}") for i in range(AWAY)], S("x")
                s_guh, s_gul, s_dh, s_dl = S("guh"), S("gul"), S("dh"), S("dl")
                s_tx, s_gu, s_ht, s_dn = S("tx"), S("gu"), S("ht"), S("dn")
                s_xh, s_xl, s_sil, s_mul, s_hTh, s_hTl, s_ya, s_yd = (S(n) for n in ("xh", "xl", "sil", "mul", "hTh", "hTl", "ya", "yd"))
                s_bear = S("bear")
                s_gi, s_sidx, s_sc = S("gi"), S("sidx"), S("sc")

                def raw_loads(e, m):
                    return 16 * (PARTS // AWAY) * e + 16 * (m // AWAY + 1)

                def all_steps(eng, step, last):
                    def first_block(e, least):
                        return eng.value_load(starts_i[0:1, bass.ds(e, 1)], min_val=least, max_val=MAXBLK)

                    def expert(e, j, change):
                        b0, b1 = first_block(e, 0), first_block(e + 1, 1)
                        with eng.If(b1 > b0 + 1):
                            with eng.Fori(b0 + 1, b1) as b:
                                step(b, j, False, e, None)
                        change(b1)

                    with eng.Fori(0, NE // 2 - 1) as i:
                        for j in range(2):
                            e = 2 * i + j
                            expert(e, j, lambda b: step(b, j, True, e, i))
                    expert(NE - 2, 0, lambda b: step(b, 0, True, NE - 2, None))
                    expert(NE - 1, 1, last)

                with nc.Block() as block:
                    @block.sync
                    def _(sp):
                        def load(j, e, m):
                            if m < 4:
                                k = slice(m % 2 * KD // 2, (m % 2 + 1) * KD // 2)
                                dst, src = gu_raw[:, j, m // 2, k], a[("we_gate", "we_up")[m // 2]][l, bass.ds(e, 1)].rearrange("o (p k) n -> p (o k) n", p=P)[:, k]
                            else:
                                dst, src = d_raw[:, j, m % 2], a["we_down"][l, bass.ds(e, 1)].rearrange("o (p k) n -> p (o k) n", p=P)[:, m % 2]
                            sp.dma_start(dst, src).then_inc(s_raw[m % AWAY], 16)

                        sp.dma_start(slots[:].rearrange("p b c -> p (b c)"), slot_d[l].rearrange("(p b) c -> p (b c)", p=P)).then_inc(s_slots, 16)
                        for j in range(2):
                            for m in range(PARTS):
                                if PARTS * j + m >= AWAY:
                                    sp.wait_ge(s_raw[m % AWAY], raw_loads(j, m) - 16)
                                load(j, j, m)
                        with sp.Fori(0, NE // 2 - 1) as i:
                            for j in range(2):
                                e = 2 * i + j
                                for m in range(PARTS):
                                    if m == 0:
                                        sp.wait_ge(s_gul, 2 * e + 1)
                                    elif m == 2:
                                        sp.wait_ge(s_gul, 2 * e + 2)
                                    elif m == 4:
                                        sp.wait_ge(s_dl, e + 1)
                                    sp.sem_inc(s_bear, 1)
                                    sp.wait_ge(s_raw[m % AWAY], raw_loads(e + 2, m) - 16)
                                    sp.sem_inc(s_bear, 1)
                                    load(j, e + 2, m)

                    @block.gpsimd
                    def _(pool):
                        G = nc.gpsimd
                        G.memset(xb[:], 0.0).then_inc(s_xb0, 1)
                        pool.wait_ge(s_xb0, 1)
                        pool.wait_ge(s_slots, 16)

                        def gather(b):
                            G.tensor_copy(gi[:], slots[:, bass.ds(b, 1), 0]).then_inc(s_gi, 1)
                            pool.wait_ge(s_gi, b + 1)
                            pool.sem_inc(s_bear, 1)
                            pool.indirect_dma_start(xb[:], None, f_d[l][0:nt * P], bass.IndirectOffsetOnAxis(ap=gi[:].bitcast(U32), axis=0),
                                                    bounds_check=nt * P - 1, oob_is_err=False).then_inc(s_x, 16)

                        def scatter():
                            pool.indirect_dma_start(acc_d[l], bass.IndirectOffsetOnAxis(ap=si[:, 0:1].bitcast(U32), axis=0), yb[:], None,
                                                    compute_op=ALU.add).then_inc(s_sc, 16)

                        def split_down(j, e):
                            pool.wait_ge(s_dh, e + 1)
                            G.tensor_tensor(d_lo[:, j], d_raw[:, j], d_hi[:, j].bitcast(F32), ALU.subtract).then_inc(s_dl, 1)

                        def take_weights(b):
                            pool.wait_ge(s_sc, 16 * b + 16)
                            G.tensor_copy(si[:], slots[:, bass.ds(b, 1)].rearrange("p o c -> p (o c)")).then_inc(s_sidx, 1)

                        def give(b):
                            pool.wait_ge(s_ya, b + 2)
                            pool.wait_ge(s_yd, b + 2)
                            pool.sem_inc(s_bear, 1)
                            scatter()

                        gather(0)
                        G.memset(yb[:], 0.0).then_inc(s_xb0, 1)
                        G.tensor_copy(si[:], slots[:, TBL - 1]).then_inc(s_xb0, 1)
                        pool.wait_ge(s_xb0, 3)
                        scatter()
                        pool.wait_ge(s_tx, 1)
                        gather(1)
                        split_down(0, 0)
                        pool.wait_ge(s_tx, 2)
                        gather(2)
                        split_down(1, 1)

                        def step(b, j, change, e, i):
                            take_weights(b - 1)
                            pool.wait_ge(s_tx, b + 2)
                            gather(b + 2)
                            give(b - 1)
                            if change and i is not None:
                                split_down(j, e + 2)

                        def last(b):
                            take_weights(b - 1)
                            give(b - 1)
                            pool.wait_ge(s_sc, 16 * b + 16)
                            pool.wait_ge(s_x, 16 * b + 32)
                            pool.sem_inc(s_bear, 1)

                        all_steps(pool, step, last)

                    @block.tensor
                    def _(pe):
                        pe.sem_inc(s_ya, 1)
                        pe.sem_inc(s_yd, 1)

                        def product(ps_, terms, inc):
                            n = len(terms)
                            for i, (xh, xl, wh, wl) in enumerate(terms):
                                nc.tensor.matmul(ps_, xh, wh, start=(i == 0), stop=False)
                                nc.tensor.matmul(ps_, xh, wl, start=False, stop=False)
                                ins = nc.tensor.matmul(ps_, xl, wh, start=False, stop=(i == n - 1))
                            if inc is not None:
                                ins.then_inc(inc, 1)

                        def turn_rows():
                            v = xb[:].rearrange("q (p k) -> q k p", k=KD)
                            for k in range(KD):
                                ins = nc.tensor.transpose(psX[:, k // 4, k % 4], v[:, k], ident)
                            ins.then_inc(s_tx, 1)

                        def gate_up(j):
                            product(psG[:].rearrange("p (v f) -> p v f", v=2),
                                    [(xT_hi[:, k], xT_lo[:, k], gu_hi[:, j, :, k], gu_lo[:, j, :, k]) for k in range(KD)], s_gu)

                        def turn_hidden():
                            v = hh[:].rearrange("q (p k) -> q k p", k=KF)
                            for k in range(KF):
                                ins = nc.tensor.transpose(psH[:, k], v[:, k], ident)
                            ins.then_inc(s_ht, 1)

                        def down(j):
                            for n in range(2):
                                c = slice(n * 512, (n + 1) * 512)
                                product(psY[:, n], [(hT_hi[:, k], hT_lo[:, k], d_hi[:, j, k, c], d_lo[:, j, k, c]) for k in range(KF)], s_dn if n == 1 else None)

                        pe.wait_ge(s_x, 16)
                        turn_rows()
                        pe.wait_ge(s_xl, 2)
                        pe.wait_ge(s_gul, 2)
                        gate_up(0)
                        pe.wait_ge(s_x, 32)
                        turn_rows()

                        def down_of(b, j, e):
                            pe.wait_ge(s_hTl, b + 1)
                            pe.wait_ge(s_dl, e + 1)
                            pe.wait_ge(s_ya, b + 1)
                            pe.wait_ge(s_yd, b + 1)
                            down(j)

                        def step(b, j, change, e, i):
                            pe.wait_ge(s_mul, b)
                            turn_hidden()
                            pe.wait_ge(s_xl, 2 * b + 2)
                            if change:
                                pe.wait_ge(s_gul, 2 * e + 4)
                            gate_up(1 - j if change else j)
                            pe.wait_ge(s_x, 16 * b + 32)
                            turn_rows()
                            down_of(b - 1, j, e)

                        def last(b):
                            pe.wait_ge(s_mul, b)
                            turn_hidden()
                            down_of(b - 1, 1, NE - 1)

                        all_steps(pe, step, last)

                    @block.scalar
                    def _(act):
                        def rows():
                            for n in range(2):
                                nc.scalar.activation(xT_hi[:, 4 * n:4 * n + 4], psX[:, n], ACT.Copy).then_inc(s_xh, 1)

                        def silu():
                            nc.scalar.activation(sil[:], psG[:, 0:FF], ACT.Silu).then_inc(s_sil, 1)

                        def split_gate_up(j, e):
                            for v in range(2):
                                for m in (2 * v, 2 * v + 1):
                                    act.wait_ge(s_raw[m % AWAY], raw_loads(e, m))
                                nc.scalar.activation(gu_hi[:, j, v], gu_raw[:, j, v], ACT.Copy).then_inc(s_guh, 1)

                        def split_down(j, e):
                            for m in (4, 5):
                                act.wait_ge(s_raw[m % AWAY], raw_loads(e, m))
                            nc.scalar.activation(d_hi[:, j], d_raw[:, j], ACT.Copy).then_inc(s_dh, 1)

                        act.wait_ge(s_tx, 1)
                        rows()
                        split_gate_up(0, 0)
                        split_down(0, 0)
                        act.wait_ge(s_gu, 1)
                        silu()
                        act.wait_ge(s_tx, 2)
                        rows()
                        split_gate_up(1, 1)
                        split_down(1, 1)

                        def out_of(b):
                            act.wait_ge(s_dn, b + 1)
                            act.wait_ge(s_sidx, b + 1)
                            nc.scalar.activation(yb[:, 0:512], psY[:, 0], ACT.Copy, scale=si[:, 1:2].bitcast(F32)).then_inc(s_ya, 1)

                        def hidden(b):
                            act.wait_ge(s_ht, b + 1)
                            nc.scalar.activation(hT_hi[:], psH[:, 0:KF], ACT.Copy).then_inc(s_hTh, 1)

                        def step(b, j, change, e, i):
                            hidden(b - 1)
                            if change and i is not None:
                                act.wait_ge(s_gu, b)
                                split_gate_up(j, e + 2)
                            act.wait_ge(s_gu, b + 1)
                            silu()
                            act.wait_ge(s_tx, b + 2)
                            rows()
                            out_of(b - 1)
                            if change and i is not None:
                                split_down(j, e + 2)

                        def last(b):
                            hidden(b - 1)
                            out_of(b - 1)

                        all_steps(act, step, last)

                    @block.vector
                    def _(dve):
                        V = nc.vector

                        def rows(b):
                            for n in range(2):
                                dve.wait_ge(s_xh, 2 * b + n + 1)
                                k = slice(4 * n, 4 * n + 4)
                                V.tensor_tensor(xT_lo[:, k], psX[:, n], xT_hi[:, k].bitcast(F32), ALU.subtract).then_inc(s_xl, 1)

                        def product():
                            V.tensor_tensor(hh[:], sil[:], psG[:, FF:2 * FF], ALU.mult).then_inc(s_mul, 1)

                        def split_gate_up(j, e):
                            for v in range(2):
                                dve.wait_ge(s_guh, 2 * e + v + 1)
                                V.tensor_tensor(gu_lo[:, j, v], gu_raw[:, j, v], gu_hi[:, j, v].bitcast(F32), ALU.subtract).then_inc(s_gul, 1)

                        rows(0)
                        split_gate_up(0, 0)
                        dve.wait_ge(s_sil, 1)
                        product()
                        rows(1)
                        split_gate_up(1, 1)

                        def out_of(b):
                            dve.wait_ge(s_dn, b + 1)
                            dve.wait_ge(s_sidx, b + 1)
                            V.tensor_scalar(yb[:, 512:], psY[:, 1], si[:, 1:2].bitcast(F32), None, ALU.mult).then_inc(s_yd, 1)

                        def hidden(b):
                            dve.wait_ge(s_hTh, b + 1)
                            V.tensor_tensor(hT_lo[:], psH[:, 0:KF], hT_hi[:].bitcast(F32), ALU.subtract).then_inc(s_hTl, 1)

                        def step(b, j, change, e, i):
                            hidden(b - 1)
                            if change and i is not None:
                                split_gate_up(j, e + 2)
                            dve.wait_ge(s_sil, b + 1)
                            product()
                            rows(b + 1)
                            out_of(b - 1)

                        def last(b):
                            hidden(b - 1)
                            out_of(b - 1)

                        all_steps(dve, step, last)

        def stage_combine(l, nt, aT):
            with ExitStack() as ctx:
                S = lambda n: sem(f"H{l}_{n}_s")
                T = lambda n, shape, dt=F32: sb(ctx, f"H{l}_{n}", shape, dt)
                nv = 2 if nt > NL else 1
                ac = T("ac", [P, 3, D])
                gate = T("gate", [P, nv, D])
                amul = T("amul", [P, nv, D])
                aadd = T("aadd", [P, nv, D])
                an = T("an", [P, 2, D])
                junk = T("junk", [P, D], BF16)
                st = T("st", [P, nt, 3])
                psT = ps(ctx, f"H{l}_psT", [P, 2, KD, P])
                s_v, s_ac = S("v"), [S(f"ac{i}") for i in range(3)]
                s_g, s_h, s_rt, s_a0, s_a, s_tp, s_tev, s_act, s_dve = (S(n) for n in ("g", "h", "rt", "a0", "a", "tp", "tev", "act", "dve"))
                s_out = [S("out0"), S("out1")]
                with nc.Block() as block:
                    @block.sync
                    def _(sp):
                        for t in range(nt):
                            if t >= 3:
                                sp.wait_ge(s_h, t - 2)
                            sp.dma_start(ac[:, t % 3], acc_d[l][t * P:(t + 1) * P]).then_inc(s_ac[t % 3], 16)
                        if aT is None:
                            for t in range(nt):
                                sp.wait_ge(s_a0, t + 1)
                                sp.dma_start(out[0, t * P:(t + 1) * P], an[:, t % 2]).then_inc(s_out[t % 2], 16)
                            for b in range(2):
                                sp.wait_ge(s_out[b], 16 * ((nt - b + 1) // 2))

                    @block.scalar
                    def _(act):
                        link = Chain(act, s_act)
                        for v in range(nv):
                            act.dma_start(gate[:, v], mod_rows(l, v, 5)).then_inc(s_v, 16)
                            if aT is not None:
                                act.dma_start(amul[:, v], mod_rows(l + 1, v, 1)).then_inc(s_v, 16)
                                act.dma_start(aadd[:, v], mod_rows(l + 1, v, 0)).then_inc(s_v, 16)
                            else:
                                act.dma_start(amul[:, v], a["g_final"].rearrange("(o d) -> o d", o=1).to_broadcast([P, D])).then_inc(s_v, 16)
                        for t in range(nt):
                            act.wait_ge(s_h, t + 1)
                            link(nc.scalar.activation(junk[:], h[:, t], ACT.Square, accum_out=st[:, t, 0:1]))
                            nc.scalar.activation(st[:, t, 1:2], st[:, t, 0:1], ACT.Sqrt, bias=eps, scale=1.0 / D).then_inc(s_rt, 1)
                            if aT is not None:
                                act.wait_ge(s_tp, t + 1)
                                nc.scalar.activation(aT[:, :, t * P:(t + 1) * P], psT[:, t % 2], ACT.Copy).then_inc(s_tev, 1)

                    @block.vector
                    def _(dve):
                        link = Chain(dve, s_dve)
                        dve.wait_ge(s_v, 16 * nv * (3 if aT is not None else 2))

                        def gated(t):
                            dve.wait_ge(s_ac[t % 3], 16 * (t // 3 + 1))
                            nc.vector.tensor_tensor(ac[:, t % 3], ac[:, t % 3], gate[:, 0 if t < NL else 1], ALU.mult).then_inc(s_g, 1)

                        gated(0)
                        for t in range(nt):
                            if t + 1 < nt:
                                gated(t + 1)
                            dve.wait_ge(s_rt, t + 1)
                            link(nc.vector.reciprocal(st[:, t, 2:3], st[:, t, 1:2]))
                            if t >= 2:
                                if aT is not None:
                                    dve.wait_ge(s_tp, t - 1)
                                else:
                                    dve.wait_ge(s_out[t % 2], 16 * (t // 2))
                            nc.vector.scalar_tensor_tensor(an[:, t % 2], h[:, t], st[:, t, 2:3], amul[:, 0 if t < NL else 1], ALU.mult, ALU.mult).then_inc(s_a0, 1)

                    @block.gpsimd
                    def _(pool):
                        def added(t):
                            pool.wait_ge(s_g, t + 1)
                            nc.gpsimd.tensor_tensor(h[:, t], h[:, t], ac[:, t % 3], ALU.add).then_inc(s_h, 1)

                        added(0)
                        for t in range(nt):
                            if t + 1 < nt:
                                added(t + 1)
                            if aT is not None:
                                pool.wait_ge(s_a0, t + 1)
                                nc.gpsimd.tensor_tensor(an[:, t % 2], an[:, t % 2], aadd[:, 0 if t < NL else 1], ALU.add).then_inc(s_a, 1)

                    @block.tensor
                    def _(pe):
                        if aT is not None:
                            for t in range(nt):
                                pe.wait_ge(s_a, t + 1)
                                if t >= 2:
                                    pe.wait_ge(s_tev, t - 1)
                                v = an[:, t % 2].rearrange("q (p k) -> q k p", k=KD)
                                for k in range(KD):
                                    ins = nc.tensor.transpose(psT[:, t % 2, k], v[:, k], ident)
                                ins.then_inc(s_tp, 1)

        def stage_attend1(aT, o):
            with ExitStack() as ctx:
                S = lambda n: sem(f"I_{n}_s")
                T = lambda n, shape, dt=F32: sb(ctx, f"I_{n}", shape, dt)
                w = T("w", [P, 2, KD, DC])
                qkT = T("qkT", [P, 2, 2, NT * P])
                vv = T("vv", [P, 2, NT, DV])
                qk = T("qk", [P, 2, 4, DHALF])
                t1 = T("t1", [P, 2, 4, DHALF])
                t2 = T("t2", [P, 2, 4, DHALF])
                prob = T("prob", [P, 2, 2, NT * P])
                pT = T("pT", [P, 2, NT, P])
                nmax = T("nmax", [P, 2, 2])
                ssum = T("ssum", [P, 2, 2])
                lamv = T("lamv", [P, 4, DHALF])
                lamj = T("lamj", [P, DHALF])
                lam2 = T("lam2", [P, 2])
                nlam = T("nlam", [P, 1])
                osq = T("osq", [P, D])
                ost = T("ost", [P, NL, DH])
                psS = ps(ctx, "I_psS", [P, 2, 1024])
                psP = ps(ctx, "I_psP", [P, 8, P])
                psO = ps(ctx, "I_psO", [P, NL, DV])
                psC = ps(ctx, "I_psC", [P, 512])
                s_lam, s_lamd, s_w = S("lam"), S("lamd"), [S("w0"), S("w1")]
                (s_pr, s_prd, s_pra, s_qk, s_tr, s_tre, s_s, s_nm, s_e, s_cb, s_p1, s_t, s_evd, s_eva, s_pv, s_o, s_act, s_dve, s_lame, s_fin, s_finr) = (
                    S(n) for n in ("pr", "prd", "pra", "qk", "tr", "tre", "s", "nm", "e", "cb", "p1", "t", "evd", "eva", "pv", "o", "act", "dve", "lame", "fin", "finr"))
                cos = cst[:, C_COS:C_COS + NL * SD].rearrange("p (t d) -> p t d", t=NL)
                sin = cst[:, C_SIN:C_SIN + NL * SD].rearrange("p (t d) -> p t d", t=NL)
                slots_ = [(hd, s) for hd in range(DH + 1) for s in range(NT)]

                def tile_no(hd, s):
                    return hd * NT + s

                def order(hd, s):
                    work = []
                    if hd < DH:
                        work.append(("project", hd, s))
                    if hd >= 1 and 2 <= s < NL + 2:
                        work.append(("values", hd - 1, s - 2))
                    if s >= 1 and hd < DH:
                        work.append(("turn_qk", hd, s - 1))
                    if s == 0 and 1 <= hd:
                        work.append(("turn_qk", hd - 1, NT - 1))
                    if hd >= 1 and s < NL:
                        work.append(("scores", hd - 1, s))
                    if hd >= 1 and 1 <= s < NL + 1:
                        work.append(("turn", hd - 1, s - 1))
                    return work

                every = [x for hd, s in slots_ for x in order(hd, s)]

                def units_before(hd, s):
                    return sum(x[0] == "turn" for x in every[:every.index(("turn_qk", hd, s))])

                def turned_before(hd, t):
                    return sum(x[0] == "turn_qk" for x in every[:every.index(("turn", hd, t))])

                with nc.Block() as block:
                    @block.sync
                    def _(sp):
                        for n, name in enumerate(("lam_q1", "lam_k1", "lam_q2", "lam_k2")):
                            sp.dma_start(lamv[:, n], a[name][0:1, :].to_broadcast([P, DHALF])).then_inc(s_lam, 16)
                        for hd in range(DH):
                            if hd >= 2:
                                sp.wait_ge(s_pr, NT * (hd - 1))
                            sp.dma_start(w[:, hd % 2], kview(a["wc_in"][0])[:, :, hd * DC:(hd + 1) * DC]).then_inc(s_w[hd % 2], 16)

                    @block.tensor
                    def _(pe):
                        def project(hd, s):
                            n = tile_no(hd, s)
                            if s == 0:
                                pe.wait_ge(s_w[hd % 2], 16 * (hd // 2 + 1))
                            if n >= 1:
                                pe.wait_ge(s_prd, n)
                                pe.wait_ge(s_pra, n)
                            c0 = 0 if s < NL else 2 * DHALF
                            for k in range(KD):
                                ins = nc.tensor.matmul(psC[:, c0:DC], aT[:, k, s * P:(s + 1) * P], w[:, hd % 2, k, c0:DC], start=(k == 0), stop=(k == KD - 1))
                            ins.then_inc(s_pr, 1)

                        def turn_qk(hd, s):
                            n = tile_no(hd, s)
                            pe.wait_ge(s_qk, n + 1)
                            if n >= 1:
                                pe.wait_ge(s_tre, n)
                            u = units_before(hd, s)
                            if u >= 1:
                                pe.wait_ge(s_eva, u)
                            if s < NL:
                                nc.tensor.transpose(psP[:, 6], qk[:, n % 2, 0:2].rearrange("p m d -> p (m d)"), ident)
                            nc.tensor.transpose(psP[:, 7], qk[:, n % 2, 2:4].rearrange("p m d -> p (m d)"), ident).then_inc(s_tr, 1)

                        def scores(hd, t):
                            u = hd * NL + t
                            if t == 0:
                                pe.wait_ge(s_tre, NT * (hd + 1))
                            for m in range(2):
                                if u >= 1:
                                    pe.wait_ge(s_e, 2 * (u - 1) + m + 1)
                                r = slice(64 * m, 64 * m + 64)
                                q = qkT[r, hd % 2, 0, t * P:(t + 1) * P]
                                nc.tensor.matmul(psS[:, m, 0:512], q, qkT[r, hd % 2, 1, 0:512], start=True, stop=True)
                                nc.tensor.matmul(psS[:, m, 512:768], q, qkT[r, hd % 2, 1, 512:768], start=True, stop=True).then_inc(s_s, 1)

                        def turn(hd, t):
                            u = hd * NL + t
                            pe.wait_ge(s_cb, u + 1)
                            if u >= 1:
                                pe.wait_ge(s_evd, u)
                                pe.wait_ge(s_eva, u)
                            n = turned_before(hd, t)
                            if n >= 1:
                                pe.wait_ge(s_tre, n)
                            for b in range(NT):
                                ins = nc.tensor.transpose(psP[:, b], prob[:, u % 2, 0, b * P:(b + 1) * P], ident)
                            ins.then_inc(s_t, 1)

                        def values(hd, t):
                            u = hd * NL + t
                            pe.wait_ge(s_evd, u + 1)
                            pe.wait_ge(s_eva, u + 1)
                            if t == 0 and hd >= 1:
                                pe.wait_ge(s_o, hd)
                            if t == 0:
                                pe.wait_ge(s_pra, NT * (hd + 1))
                            for b in range(NT):
                                ins = nc.tensor.matmul(psO[:, t], pT[:, u % 2, b], vv[:, hd % 2, b], start=(b == 0), stop=(b == NT - 1))
                            ins.then_inc(s_pv, 1)

                        for hd, s in slots_:
                            for what, x, y in order(hd, s):
                                {"project": project, "values": values, "turn_qk": turn_qk, "scores": scores, "turn": turn}[what](x, y)

                    @block.vector
                    def _(dve):
                        link = Chain(dve, s_dve)
                        V = nc.vector
                        dve.wait_ge(s_lam, 64)
                        for m in range(2):
                            link(V.tensor_tensor_reduce(lamj[:], lamv[:, 2 * m], lamv[:, 2 * m + 1], 1.0, 0.0, ALU.mult, ALU.add, lam2[:, m:m + 1]))
                        V.tensor_copy(lam2[:], lam2[:]).then_inc(s_lamd, 1)
                        dve.wait_ge(s_lame, 1)
                        link(V.tensor_tensor(nlam[:], lam2[:, 1:2], lam2[:, 0:1], ALU.subtract))
                        link(V.tensor_scalar(nlam[:], nlam[:], -LAM_INIT, None, ALU.add))

                        def rotate(hd, s):
                            n = tile_no(hd, s)
                            dve.wait_ge(s_pr, n + 1)
                            if n >= 2:
                                dve.wait_ge(s_qk, n - 1)
                                dve.wait_ge(s_tr, n - 1)
                            if s < NL:
                                src = psC[:, 0:4 * DHALF].rearrange("p (g d) -> p g d", d=DHALF)
                                q = DHALF // 4
                                V.tensor_tensor(t1[:, n % 2], src, bc(cos[:, s], 4), ALU.mult)
                                s4 = src.rearrange("p g (b two q) -> p g b two q", two=2, q=q)
                                t4 = t2[:, n % 2].rearrange("p g (b two q) -> p g b two q", two=2, q=q)
                                n4 = bc(sin[:, s], 4).rearrange("p g (b two q) -> p g b two q", two=2, q=q)
                                for b in range(2):
                                    V.tensor_tensor(t4[:, :, b, 0], s4[:, :, b, 1], n4[:, :, b, 0], ALU.mult)
                                    ins = V.tensor_tensor(t4[:, :, b, 1], s4[:, :, b, 0], n4[:, :, b, 1], ALU.mult)
                            else:
                                ins = V.tensor_copy(t1[:, n % 2, 2:4], psC[:, 2 * DHALF:4 * DHALF].rearrange("p (g d) -> p g d", d=DHALF))
                            link(ins, s_prd)

                        def maximum(hd, t):
                            u = hd * NL + t
                            for m in range(2):
                                dve.wait_ge(s_s, 2 * u + m + 1)
                                if u >= 2 and m == 0:
                                    dve.wait_ge(s_e, 2 * u - 2)
                                link(V.tensor_reduce(nmax[:, u % 2, m:m + 1], psS[:, m, 0:NT * P], AX, ALU.max, negate=True), s_nm)

                        def combine(hd, t):
                            u = hd * NL + t
                            dve.wait_ge(s_e, 2 * u + 2)
                            link(V.reciprocal(ssum[:, u % 2], ssum[:, u % 2]))
                            link(V.tensor_tensor(ssum[:, u % 2, 1:2], ssum[:, u % 2, 1:2], nlam[:], ALU.mult), s_p1)
                            link(V.tensor_scalar(prob[:, u % 2, 1], prob[:, u % 2, 1], ssum[:, u % 2, 1:2], None, ALU.mult))
                            link(V.scalar_tensor_tensor(prob[:, u % 2, 0], prob[:, u % 2, 0], ssum[:, u % 2, 0:1], prob[:, u % 2, 1], ALU.mult, ALU.add), s_cb)

                        def evac(hd, t):
                            u = hd * NL + t
                            dve.wait_ge(s_t, u + 1)
                            if u >= 2:
                                dve.wait_ge(s_pv, u - 1)
                            V.tensor_copy(pT[:, u % 2, 0:4], psP[:, 0:4]).then_inc(s_evd, 1)

                        def head_out(hd):
                            dve.wait_ge(s_pv, NL * (hd + 1))
                            V.tensor_copy(o[:, 0:NL, hd * DV:(hd + 1) * DV], psO[:]).then_inc(s_o, 1)

                        for hd, s in slots_:
                            if hd < DH:
                                rotate(hd, s)
                            if hd >= 1:
                                if s < NL:
                                    maximum(hd - 1, s)
                                    combine(hd - 1, s)
                                if 1 <= s < NL + 1:
                                    evac(hd - 1, s - 1)
                                if s == NL + 1:
                                    head_out(hd - 1)
                        dve.wait_ge(s_o, DH)
                        for t in range(NL):
                            if t >= 1:
                                dve.wait_ge(s_dve, link.count[id(s_dve)])
                            link(V.tensor_tensor(osq[:], o[:, t], o[:, t], ALU.mult))
                            link(V.tensor_reduce(ost[:, t], osq[:].rearrange("p (h d) -> p h d", d=DV), AX, ALU.add))
                        V.tensor_copy(ost[:], ost[:]).then_inc(s_fin, 1)
                        dve.wait_ge(s_finr, 1)
                        link(V.reciprocal(ost[:], ost[:]))
                        for t in range(NL):
                            ov = o[:, t].rearrange("p (h d) -> p h d", d=DV)
                            link(V.tensor_tensor(ov, ov, bcl(ost[:, t], DV), ALU.mult))

                    @block.gpsimd
                    def _(pool):
                        for hd in range(DH):
                            for s in range(NT):
                                n = tile_no(hd, s)
                                pool.wait_ge(s_prd, n + 1)
                                if n >= 2:
                                    pool.wait_ge(s_tr, n - 1)
                                if s < NL:
                                    nc.gpsimd.tensor_tensor(qk[:, n % 2], t1[:, n % 2], t2[:, n % 2], ALU.add).then_inc(s_qk, 1)
                                else:
                                    nc.gpsimd.tensor_copy(qk[:, n % 2, 2:4], t1[:, n % 2, 2:4]).then_inc(s_qk, 1)

                    @block.scalar
                    def _(act):
                        link = Chain(act, s_act)
                        act.wait_ge(s_lamd, 1)
                        nc.scalar.activation(lam2[:], lam2[:], ACT.Exp).then_inc(s_lame, 1)

                        def copy_v(hd, s):
                            n = tile_no(hd, s)
                            act.wait_ge(s_pr, n + 1)
                            act.wait_ge(s_prd, n + 1)
                            if s == 0 and hd >= 2:
                                act.wait_ge(s_pv, NL * (hd - 1))
                            nc.scalar.activation(vv[:, hd % 2, s], psC[:, 4 * DHALF:DC], ACT.Copy).then_inc(s_pra, 1)

                        def copy_qk(hd, s):
                            n = tile_no(hd, s)
                            act.wait_ge(s_tr, n + 1)
                            if s == 0 and hd >= 2:
                                act.wait_ge(s_s, 2 * NL * (hd - 1))
                            if s < NL:
                                nc.scalar.activation(qkT[:, hd % 2, 0, s * P:(s + 1) * P], psP[:, 6], ACT.Copy, scale=float(DHALF) ** -0.5)
                            nc.scalar.activation(qkT[:, hd % 2, 1, s * P:(s + 1) * P], psP[:, 7], ACT.Copy).then_inc(s_tre, 1)

                        def exps(hd, t):
                            u = hd * NL + t
                            if u >= 2:
                                act.wait_ge(s_t, u - 1)
                            for m in range(2):
                                act.wait_ge(s_nm, 2 * u + m + 1)
                                nc.scalar.activation(prob[:, u % 2, m], psS[:, m, 0:NT * P], ACT.Exp, bias=nmax[:, u % 2, m:m + 1],
                                                     accum_out=ssum[:, u % 2, m:m + 1]).then_inc(s_e, 1)

                        def evac(hd, t):
                            u = hd * NL + t
                            act.wait_ge(s_t, u + 1)
                            if u >= 2:
                                act.wait_ge(s_pv, u - 1)
                            nc.scalar.activation(pT[:, u % 2, 4:6], psP[:, 4:6], ACT.Copy).then_inc(s_eva, 1)

                        for hd, s in slots_:
                            if hd < DH:
                                copy_v(hd, s)
                            for what, x, y in order(hd, s):
                                if what == "turn_qk":
                                    copy_qk(x, y)
                                elif what == "scores":
                                    exps(x, y)
                                elif what == "turn":
                                    evac(x, y)
                        act.wait_ge(s_fin, 1)
                        nc.scalar.activation(ost[:], ost[:], ACT.Sqrt, bias=eps, scale=1.0 / DV).then_inc(s_finr, 1)

        stage_modulation()
        end_stage()
        if stop == "A":
            return
        with ExitStack() as right:
            with ExitStack() as att:
                t_ = dict(qmT=sb(att, "qmT", [MQ, MH, NT * P]), kmT=sb(att, "kmT", [MQ, MH, NT * P]),
                          vM=sb(att, "vM", [P, NT, MH * MV]), qsT=sb(att, "qsT", [P, SH // 2, NT * P]),
                          ksT=sb(att, "ksT", [P, NT * P]), vS=sb(att, "vS", [P, NT, SKV * SD]))
                stage_project0(t_)
                end_stage()
                if stop == "B":
                    return
                o = sb(right, "o", [P, NT, D], side="right")
                stage_attend0(t_, o)
                end_stage()
            if stop == "C":
                return
            lg = sb(right, "lg", [P, NT, NE], side="right")
            fT = sb(right, "fT", [P, KD, NT * P], side="right")
            stage_out(0, NT, o, fT, lg, a["wa_out"][0], None)
            end_stage()
            if stop == "D":
                return
            stage_route(0, NT, fT, lg)
            end_stage()
        if stop == "E":
            return
        stage_experts(0, NT)
        end_stage()
        if stop == "F":
            return
        with ExitStack() as right:
            o = sb(right, "o1", [P, NT, D], side="right")
            with ExitStack() as left:
                aT = sb(left, "aT", [P, KD, NT * P])
                stage_combine(0, NT, aT)
                end_stage()
                stage_attend1(aT, o)
                end_stage()
            if stop == "I":
                return
            lg = sb(right, "lg1", [P, NT, NE], side="right")
            fT = sb(right, "fT1", [P, KD, NT * P], side="right")
            stage_out(1, NL, o, fT, lg, a["wc_out"][0], a["gc_sub"][0])
            end_stage()
            stage_route(1, NL, fT, lg)
            end_stage()
        stage_experts(1, NL)
        end_stage()
        stage_combine(1, NL, None)
        end_stage()


_INS = ['x', 'c', 'ctx', 'c_ctx', 'w_ada', 'b_ada', 'g_mix', 'g_ffn', 'wa_in', 'ga_q', 'ga_kv', 'wa_uq', 'wa_ukv',
        'wa_sink', 'wa_out', 'wc_in', 'lam_q1', 'lam_k1', 'lam_q2', 'lam_k2', 'gc_sub', 'wc_out', 'w_router',
        'b_router', 'we_gate', 'we_up', 'we_down', 'ws_gate', 'ws_up', 'ws_down', 'g_final']


def kernel(**inputs):
    import concourse.bacc as bacc
    from concourse.bass_utils import run_bass_kernel_spmd

    nc = bacc.Bacc("TRN2", target_bir_lowering=False, num_devices=1)
    arrays, args = {}, {}
    for name in _INS:
        arrays[f"in_{name}_dram"] = np.ascontiguousarray(inputs[name])
    arrays["in_cst_dram"] = shape_constants()
    for name in _INS + ["cst"]:
        x = arrays[f"in_{name}_dram"]
        args[name] = nc.dram_tensor(f"in_{name}_dram", x.shape, mybir.dt.from_np(x.dtype), kind="ExternalInput").ap()
    out = nc.dram_tensor("out_0_dram", (1, SEQ, D), F32, kind="ExternalOutput").ap()
    build(nc, args, out)
    r = run_bass_kernel_spmd(nc, [arrays], core_ids=[0])
    return r.results[0]["out_0_dram"]
```

```python
from contextlib import ExitStack

import numpy as np
import concourse.bass as bass
from concourse import mybir

F32 = mybir.dt.float32
BF16 = mybir.dt.bfloat16
I32 = mybir.dt.int32
U32 = mybir.dt.uint32
F32R = mybir.dt.float32r
ALU = mybir.AluOpType
ACT = mybir.ActivationFunctionType
AX = mybir.AxisListType.X

P = 128
D = 1024
KD = D // P
SEQ, CTX = 512, 256
NL, NT = SEQ // P, (SEQ + CTX) // P
EPS = 1e-6
NEG = -1e30
GRID_W, ROPE_BASE = 64, 10000.0

QR, KVR, ROPE, NOPE, MV, MH = 384, 256, 32, 64, 64, 8
MQ = NOPE + ROPE
SH, SKV, SD = 8, 2, 64
DH, DHALF, DV = 8, 64, 128
DC = 4 * DHALF + DV
LAM_INIT = 0.8 - 0.6 * float(np.exp(-0.3))
EVEN_IN = QR + KVR + ROPE + SH * SD + 2 * SKV * SD

NE, NG, TOPG, TOPK, FF = 64, 8, 4, 8, 256
ROUTED = 2.5
KF = FF // P
MAXBLK = NT * TOPK + NE
TBL = MAXBLK + 4
FAR = 16384

C_ID, C_U, C_ONE, C_MP, C_MN = 0, P, 2 * P, 3 * P, 4 * P
C_IOTA = 5 * P
C_EPS = C_IOTA + 1
C_TOK = C_EPS + 1
C_TRI = C_TOK + NT
C_COS = C_TRI + NG * NG
C_SIN = C_COS + NL * SD
C_COSM = C_SIN + NL * SD
C_SINM = C_COSM + NL * ROPE
C_COL = C_SINM + NL * ROPE
C_N = C_COL + P


def shape_constants():
    c = np.zeros((P, C_N), np.float32)
    p = np.arange(P)
    c[:, C_ID:C_ID + P] = np.eye(P)
    c[:, C_U:C_U + P] = p[:, None] < p[None, :]
    c[:, C_ONE:C_ONE + P] = 1
    c[:, C_COL:C_COL + P] = p
    c[:, C_MP:C_MP + P] = np.where(p[None, :] >= p[:, None], 0, NEG)
    c[:, C_MN:C_MN + P] = np.where(p[None, :] <= p[:, None], 0, NEG)
    c[:, C_IOTA] = p
    c[:, C_EPS] = EPS
    for t in range(NT):
        c[:, C_TOK + t] = t * P + p
    g = np.arange(NG)
    c[:, C_TRI:C_TRI + NG * NG] = (g[None, :] < g[:, None]).reshape(-1)
    for dim, cc, cs in ((SD, C_COS, C_SIN), (ROPE, C_COSM, C_SINM)):
        half, q = dim // 2, dim // 4
        inv = (np.float32(ROPE_BASE) ** (-np.arange(0, half, 2, dtype=np.float32) / np.float32(half))).astype(np.float32)
        for t in range(NL):
            tok = t * P + p
            r = (tok // GRID_W).astype(np.float32)[:, None] * inv
            w = (tok % GRID_W).astype(np.float32)[:, None] * inv
            c[:, cc + t * dim:cc + (t + 1) * dim] = np.cos(np.concatenate([r, r, w, w], 1))
            s = np.sin(np.concatenate([-r, r, -w, w], 1))
            c[:, cs + t * dim:cs + (t + 1) * dim] = s
    return c


class Chain:

    def __init__(self, eng, sem):
        self.eng, self.sem, self.count = eng, sem, {}

    def __call__(self, ins, sem=None):
        sem = self.sem if sem is None else sem
        self.count[id(sem)] = self.count.get(id(sem), 0) + 1
        ins.then_inc(sem, 1)
        self.eng.wait_ge(sem, self.count[id(sem)])


def product(nc, acc, terms, sem=None, start=True, stop=True):
    n = len(terms)
    for i, (xh, xl, wh, wl) in enumerate(terms):
        nc.tensor.matmul(acc, xh, wh, start=(start and i == 0), stop=False)
        nc.tensor.matmul(acc, xh, wl, start=False, stop=False)
        ins = nc.tensor.matmul(acc, xl, wh, start=False, stop=(stop and i == n - 1))
    if sem is not None:
        ins.then_inc(sem, 1)


def build(nc, a, out):
    with ExitStack() as whole:
        def sb(ctx, name, shape, dt=F32, side="left"):
            return ctx.enter_context(nc.sbuf_tensor(name, shape, dt, side=side))

        def ps(ctx, name, shape, dt=F32):
            return ctx.enter_context(nc.psum_tensor(name, shape, dt))

        held = []

        def sem(name):
            held.append(nc.alloc_semaphore(name))
            return held[-1]

        def end_stage():
            nc.clear_and_free_semaphores(held)
            held.clear()
            nc.all_engine_barrier()

        def dram(name, shape, dt=F32):
            return nc.dram_tensor(name, shape, dt, kind="Internal").ap()

        mod_d = dram("mod_d", [2, 2, 6 * D])
        f_d = [dram(f"f_d{l}", [NT * P, D]) for l in range(2)]
        acc_d = [dram(f"acc_d{l}", [(NT + 1) * P, D]) for l in range(2)]

        cst = sb(whole, "cst", [P, C_N])
        h = sb(whole, "h", [P, NT, D])
        ident = cst[:, C_ID:C_ID + P]
        eps = cst[:, C_EPS:C_EPS + 1]
        ident_b = sb(whole, "ident_b", [P, P], BF16)
        mask_b = sb(whole, "mask_b", [P, 2, P], BF16)
        starts_i = sb(whole, "starts_i", [1, NE + 1], I32)

        def kview(w):
            return w.rearrange("(p k) n -> p k n", p=P)

        def stage_modulation():
            CH, NCH, WB, KH = 512, 6 * D // 512, 3, KD // 2
            NV = 12
            with ExitStack() as ctx:
                craw = sb(ctx, "craw", [P, 2, KD])
                cs = sb(ctx, "cs", [P, KD, 2])
                cs_hi = sb(ctx, "cs_hi", [P, KD, 2], F32R)
                cs_lo = sb(ctx, "cs_lo", [P, KD, 2], F32R)
                wada = sb(ctx, "wada", [P, WB, KD, CH])
                wa_hi = sb(ctx, "wa_hi", [P, 2, KD, CH], F32R)
                wa_lo = sb(ctx, "wa_lo", [P, 2, KD, CH], F32R)
                bias = sb(ctx, "bias", [2, 3, D])
                row = sb(ctx, "row", [2, 2, D])
                gains = sb(ctx, "gains", [2, 2, 2, D])
                psA = ps(ctx, "psA", [2, 4, CH])
                s_cst, s_c, s_h, s_gn = sem("A_cst"), sem("A_c"), sem("A_h"), sem("A_gn")
                s_b = [sem(f"A_b{i}") for i in range(3)]
                s_w = [sem(f"A_w{i}") for i in range(WB)]
                s_silu, s_csh, s_csl, s_hi, s_lo = sem("A_silu"), sem("A_csh"), sem("A_csl"), sem("A_hi"), sem("A_lo")
                s_mm, s_ev, s_dve, s_row = sem("A_mm"), sem("A_ev"), sem("A_dve"), sem("A_row")
                s_out = [sem("A_out0"), sem("A_out1")]
                wv = [a["w_ada"][l].rearrange("(p k) n -> p k n", p=P) for l in range(2)]
                with nc.Block() as block:
                    @block.sync
                    def _(sp):
                        sp.dma_start(craw[:, 0, :], a["c"][0].rearrange("(p k) -> p k", p=P)).then_inc(s_c, 16)
                        sp.dma_start(craw[:, 1, :], a["c_ctx"].rearrange("(p k) -> p k", p=P)).then_inc(s_c, 16)
                        for i in range(2 * NCH):
                            if i >= WB:
                                sp.wait_ge(s_lo, 2 * (i - WB + 1))
                            l, n = i // NCH, i % NCH
                            sp.dma_start(wada[:, i % WB], wv[l][:, :, n * CH:(n + 1) * CH]).then_inc(s_w[i % WB], 16)
                            if i == WB - 1:
                                sp.dma_start(cst[:], a["cst"]).then_inc(s_cst, 16)
                        sp.dma_start(h[:, 0:NL], a["x"][0].rearrange("(t p) d -> p t d", p=P)).then_inc(s_h, 16)
                        sp.dma_start(h[:, NL:NT], a["ctx"][0].rearrange("(t p) d -> p t d", p=P)).then_inc(s_h, 16)
                        sp.wait_ge(s_h, 32)

                    @block.scalar
                    def _(act):
                        act.wait_ge(s_c, 32)
                        for v in range(2):
                            ins = nc.scalar.activation(cs[:, :, v], craw[:, v, :], ACT.Silu)
                        ins.then_inc(s_silu, 1)
                        act.wait_ge(s_silu, 1)
                        nc.scalar.activation(cs_hi[:], cs[:], ACT.Copy).then_inc(s_csh, 1)
                        for i in range(2 * NCH):
                            act.wait_ge(s_w[i % WB], 16 * (i // WB + 1))
                            if i >= 2:
                                act.wait_ge(s_mm, i - 1)
                            for u in range(2):
                                k = slice(u * KH, (u + 1) * KH)
                                nc.scalar.activation(wa_hi[:, i % 2, k], wada[:, i % WB, k], ACT.Copy).then_inc(s_hi, 1)

                    @block.gpsimd
                    def _(pool):
                        def load_bias(g):
                            pool.dma_start(bias[:, g % 3], a["b_ada"][g // 6:g // 6 + 1, g % 6 * D:(g % 6 + 1) * D].to_broadcast([2, D])).then_inc(s_b[g % 3], 16)

                        for g in range(3):
                            load_bias(g)
                        for l in range(2):
                            pool.dma_start(gains[:, l, 0], a["g_mix"][l:l + 1].to_broadcast([2, D])).then_inc(s_gn, 16)
                            pool.dma_start(gains[:, l, 1], a["g_ffn"][l:l + 1].to_broadcast([2, D])).then_inc(s_gn, 16)
                        for g in range(NV):
                            pool.wait_ge(s_row, g + 1)
                            pool.dma_start(mod_d[g // 6, :, g % 6 * D:(g % 6 + 1) * D], row[:, g % 2]).then_inc(s_out[g % 2], 16)
                            if g + 3 < NV:
                                load_bias(g + 3)
                        for q in range(2):
                            pool.wait_ge(s_out[q], 16 * NV // 2)

                    @block.tensor
                    def _(pe):
                        pe.wait_ge(s_csl, 1)
                        for i in range(2 * NCH):
                            if i >= 4:
                                pe.wait_ge(s_ev, i - 3)
                            b = i % 2
                            for k in range(KD):
                                if k % KH == 0:
                                    pe.wait_ge(s_lo, 2 * i + k // KH + 1)
                                nc.tensor.matmul(psA[:, i % 4], cs_hi[:, k], wa_hi[:, b, k], start=(k == 0), stop=False)
                                nc.tensor.matmul(psA[:, i % 4], cs_hi[:, k], wa_lo[:, b, k], start=False, stop=False)
                                ins = nc.tensor.matmul(psA[:, i % 4], cs_lo[:, k], wa_hi[:, b, k], start=False, stop=(k == KD - 1))
                            ins.then_inc(s_mm, 1)

                    @block.vector
                    def _(dve):
                        link = Chain(dve, s_dve)
                        dve.wait_ge(s_csh, 1)
                        nc.vector.tensor_tensor(cs_lo[:], cs[:], cs_hi[:].bitcast(F32), ALU.subtract).then_inc(s_csl, 1)

                        def out_of(i):
                            g, c = i // 2, slice(i % 2 * CH, (i % 2 + 1) * CH)
                            if i == 0:
                                dve.wait_ge(s_gn, 64)
                            if i % 2 == 0:
                                dve.wait_ge(s_b[g % 3], 16 * (g // 3 + 1))
                                if g >= 2:
                                    dve.wait_ge(s_out[g % 2], 16 * (g // 2))
                            dve.wait_ge(s_mm, i + 1)
                            seg = row[:, g % 2, c]
                            nc.vector.tensor_tensor(seg, psA[:, i % 4], bias[:, g % 3, c], ALU.add).then_inc(s_ev, 1)
                            dve.wait_ge(s_ev, i + 1)
                            if g % 3 == 1:
                                link(nc.vector.scalar_tensor_tensor(seg, seg, 1.0, gains[:, g // 6, g % 6 // 3, c], ALU.add, ALU.mult))
                            if i % 2 == 1:
                                nc.vector.tensor_copy(row[:, g % 2, 0:1], row[:, g % 2, 0:1]).then_inc(s_row, 1)

                        for i in range(2 * NCH):
                            if i >= 2:
                                dve.wait_ge(s_mm, i - 1)
                            for u in range(2):
                                k = slice(u * KH, (u + 1) * KH)
                                dve.wait_ge(s_hi, 2 * i + u + 1)
                                nc.vector.tensor_tensor(wa_lo[:, i % 2, k], wada[:, i % WB, k], wa_hi[:, i % 2, k].bitcast(F32), ALU.subtract).then_inc(s_lo, 1)
                            if i >= 1:
                                out_of(i - 1)
                            if i == WB:
                                dve.wait_ge(s_cst, 16)
                                nc.vector.tensor_copy(ident_b[:], ident)
                                nc.vector.tensor_copy(mask_b[:, 0], cst[:, C_MP:C_MP + P])
                                nc.vector.tensor_copy(mask_b[:, 1], cst[:, C_MN:C_MN + P])
                        out_of(2 * NCH - 1)

        def mod_rows(l, v, j):
            return mod_d[l, v:v + 1, j * D:(j + 1) * D].to_broadcast([P, D])

        def rope(dst, src, cos, sin, t1, t2, q, link):
            nc.vector.tensor_tensor(t1, src, cos, ALU.mult)
            s4 = src.rearrange("p g (b two q) -> p g b two q", two=2, q=q)
            t4 = t2.rearrange("p g (b two q) -> p g b two q", two=2, q=q)
            n4 = sin.rearrange("p g (b two q) -> p g b two q", two=2, q=q)
            for b in range(2):
                nc.vector.tensor_tensor(t4[:, :, b, 0], s4[:, :, b, 1], n4[:, :, b, 0], ALU.mult)
                ins = nc.vector.tensor_tensor(t4[:, :, b, 1], s4[:, :, b, 0], n4[:, :, b, 1], ALU.mult)
            link(ins)
            return nc.vector.tensor_tensor(dst, t1, t2, ALU.add)

        def bc(ap, n):
            return ap.unsqueeze(1).to_broadcast([ap.shape[0], n, ap.shape[1]])

        def bcl(ap, n):
            return ap.unsqueeze(len(ap.shape)).to_broadcast(list(ap.shape) + [n])

        def stage_project0(t_):
            qmT, kmT, vM, qsT, ksT, vS = (t_[n] for n in ("qmT", "kmT", "vM", "qsT", "ksT", "vS"))
            with ExitStack() as ctx:
                amul = sb(ctx, "B_amul", [P, D])
                aadd = sb(ctx, "B_aadd", [P, D])
                an = sb(ctx, "B_an", [P, D])
                aT = sb(ctx, "B_aT", [P, KD, P])
                w_in = sb(ctx, "w_in", [P, KD, EVEN_IN])
                w_uq = sb(ctx, "w_uq", [P, QR // P, MH * MQ])
                w_ukv = sb(ctx, "w_ukv", [P, KVR // P, MH * (NOPE + MV)])
                gq = sb(ctx, "B_gq", [P, QR // P])
                gkv = sb(ctx, "B_gkv", [P, KVR // P])
                junk = sb(ctx, "B_junk", [P, D], BF16)
                cn = sb(ctx, "B_cn", [P, QR + KVR])
                cT = sb(ctx, "B_cT", [P, 5, P])
                krr = sb(ctx, "B_krr", [P, ROPE])
                qst = sb(ctx, "B_qst", [P, SH // 2, 2, SD])
                kst = sb(ctx, "B_kst", [P, SKV * SD])
                qm = sb(ctx, "B_qm", [P, MH, MQ])
                km = sb(ctx, "B_km", [P, MH, MQ])
                t1 = sb(ctx, "B_t1", [P, 512])
                t2 = sb(ctx, "B_t2", [P, 512])
                st = sb(ctx, "B_st", [P, 3, 3])
                psC = ps(ctx, "B_psC", [P, 2, 512])
                psT = ps(ctx, "B_psT", [P, 2, KD, P])
                psU = ps(ctx, "B_psU", [P, 1024])
                s_win, s_w, s_ab = [sem(f"B_win{i}") for i in range(4)], sem("B_w"), sem("B_ab")
                s_rt, s_an0, s_an = sem("B_rt"), sem("B_an0"), sem("B_an")
                s_tp, s_tev, s_ch, s_chev = sem("B_tp"), sem("B_tev"), sem("B_ch"), sem("B_chev")
                s_ss, s_crt, s_cn = sem("B_ss"), sem("B_crt"), sem("B_cn")
                s_u, s_uev = sem("B_u"), sem("B_uev")
                s_dve, s_act = sem("B_dve"), sem("B_act")
                chunks = [(0, QR), (QR, KVR + ROPE), (QR + KVR + ROPE, SH * SD), (EVEN_IN - 2 * SKV * SD, 2 * SKV * SD)]
                cos = cst[:, C_COS:C_COS + NL * SD].rearrange("p (t d) -> p t d", t=NL)
                sin = cst[:, C_SIN:C_SIN + NL * SD].rearrange("p (t d) -> p t d", t=NL)
                cosm = cst[:, C_COSM:C_COSM + NL * ROPE].rearrange("p (t d) -> p t d", t=NL)
                sinm = cst[:, C_SINM:C_SINM + NL * ROPE].rearrange("p (t d) -> p t d", t=NL)
                uses = []
                for s in range(NT + 1):
                    if s < NT:
                        uses.append(("A", s))
                    if s >= 1:
                        uses += [("QS", s - 1), ("QM", s - 1)]
                    if s < NT:
                        uses.append(("C", s))
                    if s >= 1:
                        uses.append(("KM", s - 1))
                use = {u: n for n, u in enumerate(uses)}

                with nc.Block() as block:
                    @block.sync
                    def _(sp):
                        sp.dma_start(amul[:], mod_rows(0, 0, 1)).then_inc(s_ab, 16)
                        sp.dma_start(aadd[:], mod_rows(0, 0, 0)).then_inc(s_ab, 16)
                        wv = kview(a["wa_in"][0])
                        for i, (c0, n) in enumerate(chunks):
                            sp.dma_start(w_in[:, :, c0:c0 + n], wv[:, :, c0:c0 + n]).then_inc(s_win[i], 16)
                        sp.dma_start(w_uq[:], kview(a["wa_uq"][0])).then_inc(s_w, 16)
                        sp.dma_start(w_ukv[:], kview(a["wa_ukv"][0])).then_inc(s_w, 16)
                        sp.dma_start(gq[:], a["ga_q"][0].rearrange("(p k) -> p k", p=P)).then_inc(s_w, 16)
                        sp.dma_start(gkv[:], a["ga_kv"][0].rearrange("(p k) -> p k", p=P)).then_inc(s_w, 16)
                        sp.wait_ge(s_an, NL)
                        sp.dma_start(amul[:], mod_rows(0, 1, 1)).then_inc(s_ab, 16)
                        sp.dma_start(aadd[:], mod_rows(0, 1, 0)).then_inc(s_ab, 16)

                    @block.gpsimd
                    def _(pool):
                        for t in range(NT):
                            pool.wait_ge(s_an0, t + 1)
                            nc.gpsimd.tensor_tensor(an[:], an[:], aadd[:], ALU.add).then_inc(s_an, 1)

                    @block.scalar
                    def _(act):
                        link = Chain(act, s_act)

                        def norm(t):
                            if t >= 1:
                                act.wait_ge(s_an0, t)
                            link(nc.scalar.activation(junk[:], h[:, t], ACT.Square, accum_out=st[:, 0, 0:1]))
                            nc.scalar.activation(st[:, 0, 1:2], st[:, 0, 0:1], ACT.Sqrt, bias=eps, scale=1.0 / D).then_inc(s_rt, 1)

                        def root_c(t):
                            act.wait_ge(s_ss, 2 * t + 2)
                            nc.scalar.activation(st[:, 1, 1:2], st[:, 1, 0:1], ACT.Sqrt, bias=eps, scale=1.0 / QR)
                            nc.scalar.activation(st[:, 2, 1:2], st[:, 2, 0:1], ACT.Sqrt, bias=eps, scale=1.0 / KVR).then_inc(s_crt, 1)

                        def evac(kind, t):
                            n = use[kind, t]
                            act.wait_ge(s_tp, n + 1)
                            src = psT[:, n % 2]
                            tok = slice(t * P, (t + 1) * P)
                            if kind == "A":
                                ins = nc.scalar.activation(aT[:], src, ACT.Copy)
                            elif kind == "C":
                                if t == 0:
                                    act.wait_ge(s_w, 16 * 4)
                                for k in range(3):
                                    nc.scalar.activation(cT[:, k], src[:, k], ACT.Copy, scale=gq[:, k:k + 1])
                                for k in range(2):
                                    ins = nc.scalar.activation(cT[:, 3 + k], src[:, 3 + k], ACT.Copy, scale=gkv[:, k:k + 1])
                            elif kind == "QS":
                                nc.scalar.activation(qsT[:, :, tok], src[:, 0:4], ACT.Copy, scale=float(SD) ** -0.5)
                                ins = nc.scalar.activation(ksT[:, tok], src[:, 4], ACT.Copy)
                            elif kind == "QM":
                                ins = nc.scalar.activation(qmT[:, :, tok], src[0:MQ], ACT.Copy, scale=float(MQ) ** -0.5)
                            else:
                                ins = nc.scalar.activation(kmT[:, :, tok], src[0:MQ], ACT.Copy)
                            ins.then_inc(s_tev, 1)

                        norm(0)
                        for s in range(NT + 1):
                            if s < NT:
                                evac("A", s)
                            if s + 1 < NT:
                                norm(s + 1)
                            if s >= 1:
                                evac("QS", s - 1)
                            if s < NT:
                                root_c(s)
                            if s >= 1:
                                evac("QM", s - 1)
                            if s < NT:
                                evac("C", s)
                            if s >= 1:
                                evac("KM", s - 1)

                    @block.vector
                    def _(dve):
                        link = Chain(dve, s_dve)

                        def norm(t):
                            dve.wait_ge(s_rt, t + 1)
                            link(nc.vector.reciprocal(st[:, 0, 2:3], st[:, 0, 1:2]))
                            dve.wait_ge(s_ab, 32 if t < NL else 64)
                            if t >= 1:
                                dve.wait_ge(s_ch, 4 * (t - 1) + 1)
                            nc.vector.scalar_tensor_tensor(an[:], h[:, t], st[:, 0, 2:3], amul[:], ALU.mult, ALU.mult).then_inc(s_an0, 1)

                        def chunk(t, c):
                            g = 4 * t + c
                            dve.wait_ge(s_ch, g + 1)
                            src = psC[:, g % 2]
                            lat = t < NL
                            if c < 2:
                                n, o = (QR, 0) if c == 0 else (KVR, QR)
                                if c == 0 and t >= 1:
                                    dve.wait_ge(s_tp, use["C", t - 1] + 1)
                                ins = nc.vector.tensor_copy(cn[:, o:o + n], src[:, 0:n])
                                if c == 1:
                                    if lat:
                                        link(ins)
                                        v = lambda x: x.rearrange("p (g d) -> p g d", g=1)
                                        ins = rope(v(krr[:]), v(src[:, n:n + ROPE]), v(cosm[:, t]), v(sinm[:, t]),
                                                   v(t1[:, 0:ROPE]), v(t2[:, 0:ROPE]), ROPE // 4, link)
                                    else:
                                        link(ins)
                                        ins = nc.vector.tensor_copy(krr[:], src[:, n:n + ROPE])
                                link(ins, s_chev)
                                link(nc.vector.tensor_tensor_reduce(t1[:, 0:n], cn[:, o:o + n], cn[:, o:o + n], 1.0, 0.0,
                                                                    ALU.mult, ALU.add, st[:, 1 + c, 0:1]), s_ss)
                            elif c == 2:
                                if t >= 1:
                                    dve.wait_ge(s_tp, use["QS", t - 1] + 1)
                                o = qst[:].rearrange("p j g d -> p g j d")
                                if lat:
                                    heads = src.rearrange("p (h d) -> p h d", d=SD)
                                    tt1 = t1[:].rearrange("p (h d) -> p h d", d=SD)
                                    tt2 = t2[:].rearrange("p (h d) -> p h d", d=SD)
                                    ins = rope_into(o, heads, t, tt1, tt2, link)
                                else:
                                    ins = nc.vector.tensor_copy(o, src.rearrange("p (g j d) -> p g j d", g=2, d=SD))
                                link(ins, s_chev)
                            else:
                                n = SKV * SD
                                if lat:
                                    v = lambda x: x.rearrange("p (h d) -> p h d", d=SD)
                                    link(rope(v(kst[:]), v(src[:, 0:n]), bc(cos[:, t], SKV), bc(sin[:, t], SKV),
                                              v(t1[:, 0:n]), v(t2[:, 0:n]), SD // 4, link))
                                else:
                                    nc.vector.tensor_copy(kst[:], src[:, 0:n])
                                link(nc.vector.tensor_copy(vS[:, t], src[:, n:2 * n]), s_chev)

                        def rope_into(o, heads, t, tt1, tt2, link):
                            nc.vector.tensor_tensor(tt1, heads, bc(cos[:, t], SH), ALU.mult)
                            q = SD // 4
                            s4 = heads.rearrange("p g (b two q) -> p g b two q", two=2, q=q)
                            t4 = tt2.rearrange("p g (b two q) -> p g b two q", two=2, q=q)
                            n4 = bc(sin[:, t], SH).rearrange("p g (b two q) -> p g b two q", two=2, q=q)
                            for b in range(2):
                                nc.vector.tensor_tensor(t4[:, :, b, 0], s4[:, :, b, 1], n4[:, :, b, 0], ALU.mult)
                                ins = nc.vector.tensor_tensor(t4[:, :, b, 1], s4[:, :, b, 0], n4[:, :, b, 1], ALU.mult)
                            link(ins)
                            g4 = lambda x: x.rearrange("p (g j) d -> p g j d", g=2)
                            return nc.vector.tensor_tensor(o, g4(tt1), g4(tt2), ALU.add)

                        def scale_c(t):
                            dve.wait_ge(s_crt, t + 1)
                            link(nc.vector.reciprocal(st[:, 1:3, 2], st[:, 1:3, 1]))
                            nc.vector.tensor_scalar(cn[:, 0:QR], cn[:, 0:QR], st[:, 1, 2:3], None, ALU.mult)
                            link(nc.vector.tensor_scalar(cn[:, QR:], cn[:, QR:], st[:, 2, 2:3], None, ALU.mult), s_cn)

                        def up_q(t):
                            dve.wait_ge(s_u, 2 * t + 1)
                            if t >= 1:
                                dve.wait_ge(s_tp, use["QM", t - 1] + 1)
                            src = psU[:, 0:MH * MQ].rearrange("p (h d) -> p h d", d=MQ)
                            ins = nc.vector.tensor_copy(qm[:, :, 0:NOPE], src[:, :, 0:NOPE])
                            r = src[:, :, NOPE:MQ]
                            if t < NL:
                                v = lambda x: x[:, 0:MH * ROPE].rearrange("p (h d) -> p h d", d=ROPE)
                                link(ins)
                                ins = rope(qm[:, :, NOPE:MQ], r, bc(cosm[:, t], MH), bc(sinm[:, t], MH), v(t1), v(t2), ROPE // 4, link)
                            else:
                                ins = nc.vector.tensor_copy(qm[:, :, NOPE:MQ], r)
                            link(ins, s_uev)

                        def up_kv(t):
                            dve.wait_ge(s_u, 2 * t + 2)
                            if t >= 1:
                                dve.wait_ge(s_tp, use["KM", t - 1] + 1)
                            src = psU[:].rearrange("p (h d) -> p h d", d=NOPE + MV)
                            nc.vector.tensor_copy(km[:, :, NOPE:MQ], bc(krr[:], MH))
                            nc.vector.tensor_copy(km[:, :, 0:NOPE], src[:, :, 0:NOPE])
                            link(nc.vector.tensor_copy(vM[:, t].rearrange("p (h d) -> p h d", d=MV), src[:, :, NOPE:]), s_uev)

                        norm(0)
                        for s in range(NT + 1):
                            if s >= 1:
                                up_kv(s - 1)
                            if s < NT:
                                chunk(s, 0)
                                chunk(s, 1)
                                scale_c(s)
                                if s + 1 < NT:
                                    norm(s + 1)
                                chunk(s, 2)
                                chunk(s, 3)
                                up_q(s)

                    @block.tensor
                    def _(pe):
                        def turn(kind, t):
                            n = use[kind, t]
                            if n >= 2:
                                pe.wait_ge(s_tev, n - 1)
                            dst = psT[:, n % 2]
                            if kind == "A":
                                pe.wait_ge(s_an, t + 1)
                                v = an[:].rearrange("q (p k) -> q k p", k=KD)
                                for k in range(KD):
                                    ins = nc.tensor.transpose(dst[:, k], v[:, k], ident)
                            elif kind == "C":
                                pe.wait_ge(s_cn, t + 1)
                                v = cn[:, 0:QR].rearrange("q (p k) -> q k p", k=3)
                                for k in range(3):
                                    nc.tensor.transpose(dst[:, k], v[:, k], ident)
                                v = cn[:, QR:].rearrange("q (p k) -> q k p", k=2)
                                for k in range(2):
                                    ins = nc.tensor.transpose(dst[:, 3 + k], v[:, k], ident)
                            elif kind == "QS":
                                pe.wait_ge(s_chev, 4 * t + 4)
                                for j in range(SH // 2):
                                    nc.tensor.transpose(dst[:, j], qst[:, j].rearrange("p g d -> p (g d)"), ident)
                                ins = nc.tensor.transpose(dst[:, 4], kst[:], ident)
                            else:
                                pe.wait_ge(s_uev, 2 * t + (1 if kind == "QM" else 2))
                                x = qm if kind == "QM" else km
                                for i in range(MH):
                                    ins = nc.tensor.transpose(dst[0:MQ, i], x[:, i], ident)
                            ins.then_inc(s_tp, 1)

                        def chunk(t, c):
                            g = 4 * t + c
                            if g >= 2:
                                pe.wait_ge(s_chev, g - 1)
                            if c == 0:
                                pe.wait_ge(s_tev, use["A", t] + 1)
                            if t == 0:
                                pe.wait_ge(s_win[c], 16)
                            c0, n = chunks[c]
                            for k in range(KD):
                                ins = nc.tensor.matmul(psC[:, g % 2, 0:n], aT[:, k], w_in[:, k, c0:c0 + n], start=(k == 0), stop=(k == KD - 1))
                            ins.then_inc(s_ch, 1)

                        def up(t, i):
                            n = 2 * t + i
                            if n >= 1:
                                pe.wait_ge(s_uev, n)
                            if i == 0:
                                pe.wait_ge(s_tev, use["C", t] + 1)
                            if n == 0:
                                pe.wait_ge(s_w, 16 * 4)
                            w, k0, nk, cols = (w_uq, 0, 3, MH * MQ) if i == 0 else (w_ukv, 3, 2, MH * (NOPE + MV))
                            for c0 in range(0, cols, 512):
                                c1 = min(c0 + 512, cols)
                                for k in range(nk):
                                    ins = nc.tensor.matmul(psU[:, c0:c1], cT[:, k0 + k], w[:, k, c0:c1], start=(k == 0), stop=(k == nk - 1))
                            ins.then_inc(s_u, 1)

                        for s in range(NT + 1):
                            if s < NT:
                                turn("A", s)
                            if s >= 1:
                                up(s - 1, 1)
                            if s < NT:
                                chunk(s, 0)
                            if s >= 1:
                                turn("QS", s - 1)
                            if s < NT:
                                chunk(s, 1)
                            if s >= 1:
                                turn("QM", s - 1)
                            if s < NT:
                                chunk(s, 2)
                                turn("C", s)
                            if s >= 1:
                                turn("KM", s - 1)
                            if s < NT:
                                chunk(s, 3)
                                up(s, 0)

        def stage_attend0(t_, o, fT, ahead):
            qmT, kmT, vM, qsT, ksT, vS = (t_[n] for n in ("qmT", "kmT", "vM", "qsT", "ksT", "vS"))
            units = [(t, kind, hd) for t in range(NT) for kind in range(2) for hd in range(8)]
            N = len(units)

            def keys(t, kind):
                lat = [] if t >= NL else list(range(NL)) if kind == 0 else list(range(max(0, t - 1), min(NL, t + 2)))
                return lat + list(range(NL, NT)), 512 - P * len(lat)

            with ExitStack() as ctx:
                prob = sb(ctx, "C_prob", [P, 3, NT * P])
                pT = sb(ctx, "C_pT", [P, 2, NT, P])
                sink = sb(ctx, "C_sink", [P, 8])
                nsink = sb(ctx, "C_nsink", [P, 8])
                nmax = sb(ctx, "C_nmax", [P, 2 * NT, 8])
                ssum = sb(ctx, "C_ssum", [P, 2 * NT, 8])
                sdif = sb(ctx, "C_sdif", [P, 2, 8])
                psS = ps(ctx, "C_psS", [P, 2, 1024])
                psP = ps(ctx, "C_psP", [P, 2, 4, P])
                psO = ps(ctx, "C_psO", [P, 2, 512])
                s_sink, s_s, s_nm, s_e = sem("C_sink_in"), sem("C_s"), sem("C_nm"), sem("C_e")
                s_t, s_pv, s_evd, s_eva = sem("C_t"), sem("C_pv"), sem("C_evd"), sem("C_eva")
                s_sd, s_se, s_o, s_dve, s_act = sem("C_sd"), sem("C_se"), sem("C_o"), sem("C_dve"), sem("C_act")

                def place(n, b):
                    first = (n + 1) // 2
                    return (0, b) if b < first else (1, b - first)

                with nc.Block() as block:
                    @block.sync
                    def _(sp):
                        sp.dma_start(sink[:], a["wa_sink"][0:1, :].to_broadcast([P, 8])).then_inc(s_sink, 16)
                        for k in range(len(ahead)):
                            sp.dma_start(raw_in(fT, k), a["wa_out"][0].rearrange("(k p) n -> p k n", p=P)[:, k]).then_inc(ahead[k], 16)

                    @block.tensor
                    def _(pe):
                        def scores(i):
                            t, kind, hd = units[i]
                            if i >= 2:
                                pe.wait_ge(s_e, i - 1)
                            ks, c0 = keys(t, kind)
                            if kind == 0:
                                q, kT = qmT[:, hd, t * P:(t + 1) * P], kmT[:, hd]
                            else:
                                g, j = divmod(hd, SH // SKV)
                                q, kT = qsT[64 * g:64 * g + 64, j, t * P:(t + 1) * P], ksT[64 * g:64 * g + 64]
                            masks = []
                            if kind == 1 and t < NL:
                                masks = [(c0 + n * P, 0 if k < t else 1) for n, k in enumerate(ks) if k < NL and k != t]
                            if c0 < 512:
                                nc.tensor.matmul(psS[:, i % 2, c0:512], q, kT[:, ks[0] * P:ks[0] * P + 512 - c0], start=True, stop=not masks)
                            for n, (c, m) in enumerate(masks):
                                nc.tensor.matmul(psS[:, i % 2, c:c + P], ident_b[:], mask_b[:, m], start=False, stop=n == len(masks) - 1)
                            nc.tensor.matmul(psS[:, i % 2, 512:512 + CTX], q, kT[:, SEQ:], start=True, stop=True).then_inc(s_s, 1)

                        def turn(i):
                            t, kind, hd = units[i]
                            pe.wait_ge(s_e, i + 1)
                            if i >= 1:
                                pe.wait_ge(s_evd, i)
                                pe.wait_ge(s_eva, i)
                            n = len(keys(t, kind)[0])
                            for b in range(n):
                                bank, c = place(n, b)
                                ins = nc.tensor.transpose(psP[:, bank, c], prob[:, i % 3, b * P:(b + 1) * P], ident)
                            ins.then_inc(s_t, 1)

                        def values(i):
                            t, kind, hd = units[i]
                            pe.wait_ge(s_evd, i + 1)
                            pe.wait_ge(s_eva, i + 1)
                            g = i // 8
                            if i % 8 == 0 and g >= 2:
                                pe.wait_ge(s_o, g - 1)
                            ks, _ = keys(t, kind)
                            for n, k in enumerate(ks):
                                v = vM[:, k, hd * MV:(hd + 1) * MV] if kind == 0 else vS[:, k, hd // 4 * SD:hd // 4 * SD + SD]
                                ins = nc.tensor.matmul(psO[:, g % 2, hd * 64:(hd + 1) * 64], pT[:, i % 2, n], v, start=(n == 0), stop=(n == len(ks) - 1))
                            ins.then_inc(s_pv, 1)

                        for i in range(N + 3):
                            if i < N:
                                scores(i)
                            if 2 <= i < N + 2:
                                turn(i - 2)
                            if i >= 3:
                                values(i - 3)

                    @block.vector
                    def _(dve):
                        link = Chain(dve, s_dve)
                        dve.wait_ge(s_sink, 16)
                        link(nc.vector.tensor_scalar(nsink[:], sink[:], -1.0, None, ALU.mult))

                        def maximum(i):
                            t, kind, hd = units[i]
                            g = i // 8
                            dve.wait_ge(s_s, i + 1)
                            ks, c0 = keys(t, kind)
                            m = nmax[:, g, hd:hd + 1]
                            ins = nc.vector.tensor_reduce(m, psS[:, i % 2, c0:512 + CTX], AX, ALU.max, negate=True)
                            if kind == 1:
                                link(ins)
                                ins = nc.vector.tensor_tensor(m, m, nsink[:, hd:hd + 1], ALU.min)
                            link(ins, s_nm)

                        def evac(i):
                            n = len(keys(*units[i][:2])[0])
                            dve.wait_ge(s_t, i + 1)
                            if i >= 2:
                                dve.wait_ge(s_pv, i - 1)
                            f = (n + 1) // 2
                            nc.vector.tensor_copy(pT[:, i % 2, 0:f], psP[:, 0, 0:f]).then_inc(s_evd, 1)

                        def divide(g):
                            t, kind = g // 2, g % 2
                            sl = ssum[:, g]
                            if kind == 1:
                                dve.wait_ge(s_se, t + 1)
                                link(nc.vector.tensor_tensor(sl, sl, sdif[:, t % 2], ALU.add))
                            else:
                                dve.wait_ge(s_e, 8 * g + 8)
                            link(nc.vector.reciprocal(sl, sl))
                            dve.wait_ge(s_pv, 8 * g + 8)
                            nc.vector.tensor_tensor(o[:, t, kind * 512:(kind + 1) * 512].rearrange("p (h d) -> p h d", d=64),
                                                    psO[:, g % 2].rearrange("p (h d) -> p h d", d=64), bcl(sl, 64), ALU.mult).then_inc(s_o, 1)

                        for i in range(N + 4):
                            if i < N:
                                maximum(i)
                            if 2 <= i < N + 2:
                                evac(i - 2)
                            if i % 8 == 1 and i > 8 and (i // 8 - 1) % 2 == 1:
                                g = i // 8 - 1
                                if g // 2 >= 2:
                                    dve.wait_ge(s_se, g // 2 - 1)
                                link(nc.vector.tensor_tensor(sdif[:, g // 2 % 2], sink[:], nmax[:, g], ALU.add), s_sd)
                            if i >= 11 and (i - 11) % 8 == 0:
                                divide((i - 11) // 8)

                    @block.scalar
                    def _(act):
                        link = Chain(act, s_act)
                        for i in range(N + 4):
                            if i < N:
                                t, kind, hd = units[i]
                                ks, c0 = keys(t, kind)
                                act.wait_ge(s_nm, i + 1)
                                if i >= 3:
                                    act.wait_ge(s_t, i - 2)
                                g = i // 8
                                nc.scalar.activation(prob[:, i % 3, 0:len(ks) * P], psS[:, i % 2, c0:512 + CTX], ACT.Exp,
                                                     bias=nmax[:, g, hd:hd + 1], accum_out=ssum[:, g, hd:hd + 1]).then_inc(s_e, 1)
                            if 2 <= i < N + 2:
                                j = i - 2
                                n = len(keys(*units[j][:2])[0])
                                f = (n + 1) // 2
                                act.wait_ge(s_t, j + 1)
                                if j >= 2:
                                    act.wait_ge(s_pv, j - 1)
                                nc.scalar.activation(pT[:, j % 2, f:n], psP[:, 1, 0:n - f], ACT.Copy).then_inc(s_eva, 1)
                            if i % 8 == 1 and i > 8 and (i // 8 - 1) % 2 == 1:
                                g = i // 8 - 1
                                act.wait_ge(s_sd, g // 2 + 1)
                                nc.scalar.activation(sdif[:, g // 2 % 2], sdif[:, g // 2 % 2], ACT.Exp).then_inc(s_se, 1)

        def raw_in(fT, k):
            return fT[:].rearrange("p k n -> p (k n)")[:, k * D:(k + 1) * D]

        def stage_out(l, nt, o, fT, lg, w_out_in, gain_in, ahead):
            with ExitStack() as ctx:
                w_hi = sb(ctx, f"D{l}_wh", [P, KD, D], F32R)
                w_lo = sb(ctx, f"D{l}_wl", [P, KD, D], F32R)
                w_r = sb(ctx, f"D{l}_wr", [P, KD, NE])
                gsub = sb(ctx, f"D{l}_gs", [P, 1])
                gate = sb(ctx, f"D{l}_gate", [P, 2, D])
                fmul = sb(ctx, f"D{l}_fmul", [P, 2, D])
                fadd = sb(ctx, f"D{l}_fadd", [P, 2, D])
                oT_hi = sb(ctx, f"D{l}_oTh", [P, 2, KD, P], F32R)
                oT_lo = sb(ctx, f"D{l}_oTl", [P, 2, KD, P], F32R)
                y = sb(ctx, f"D{l}_y", [P, D])
                f = sb(ctx, f"D{l}_f", [P, 2, D])
                st = sb(ctx, f"D{l}_st", [P, 3])
                w_raw = [raw_in(fT, k) for k in range(KD - 2)] + [f[:, 0], f[:, 1]]
                psT = ps(ctx, f"D{l}_psT", [P, 2, KD, P])
                psY = ps(ctx, f"D{l}_psY", [P, 2, 512])
                psR = ps(ctx, f"D{l}_psR", [P, 512])
                S = lambda n: sem(f"D{l}_{n}_s")
                s_w, s_wr, s_v, s_to, s_oT, s_y, s_yev, s_h = ahead + [S(f"w{i}") for i in range(len(ahead), KD)], S("wr"), S("v"), S("to"), S("oT"), S("y"), S("yev"), S("h")
                s_rt, s_f0, s_f, s_r, s_lg, s_act, s_dve = S("rt"), S("f0"), S("f"), S("r"), S("lg"), S("act"), S("dve")
                s_fd, s_gs, s_gsm, s_wh, s_wl, s_ol = [S("fd0"), S("fd1")], S("gs"), S("gsm"), S("wh"), S("wl"), S("ol")
                held.extend(ahead)
                nv = 2 if nt > NL else 1

                uses = [("O", 0)]
                for t in range(nt + 1):
                    if t + 1 < nt:
                        uses.append(("O", t + 1))
                    if t >= 1:
                        uses.append(("F", t - 1))
                use = {u: n for n, u in enumerate(uses)}

                with nc.Block() as block:
                    @block.sync
                    def _(sp):
                        if gain_in is not None:
                            sp.dma_start(gsub[:], gain_in.rearrange("(p o) -> p o", o=1)).then_inc(s_gs, 16)
                        for k in range(len(ahead), KD):
                            sp.dma_start(w_raw[k], w_out_in.rearrange("(k p) n -> p k n", p=P)[:, k]).then_inc(s_w[k], 16)
                        for dst, j in ((gate, 2), (fmul, 4), (fadd, 3)):
                            for v in range(nv):
                                sp.dma_start(dst[:, v], mod_rows(l, v, j)).then_inc(s_v, 16)
                        sp.dma_start(w_r[:], kview(a["w_router"][l])).then_inc(s_wr, 16)
                        for t in range(nt):
                            sp.wait_ge(s_f, t + 1)
                            sp.dma_start(f_d[l][t * P:(t + 1) * P], f[:, t % 2]).then_inc(s_fd[t % 2], 16)
                        for b in range(2):
                            sp.wait_ge(s_fd[b], 16 * ((nt - b + 1) // 2))

                    @block.scalar
                    def _(act):
                        link = Chain(act, s_act)
                        if gain_in is not None:
                            act.wait_ge(s_gs, 16)
                            link(nc.scalar.mul(gsub[:], gsub[:], 1.0 - LAM_INIT), s_gsm)

                        def evac(kind, t):
                            n = use[kind, t]
                            act.wait_ge(s_to, n + 1)
                            if kind == "O":
                                for b in range(2):
                                    sl = slice(4 * b, 4 * b + 4)
                                    ins = nc.scalar.activation(oT_hi[:, t % 2, sl], psT[:, n % 2, sl], ACT.Copy, scale=1.0 if gain_in is None else gsub[:, 0:1])
                            else:
                                ins = nc.scalar.activation(fT[:, :, t * P:(t + 1) * P], psT[:, n % 2], ACT.Copy)
                            ins.then_inc(s_oT, 1)

                        def norm(t):
                            act.wait_ge(s_h, t + 1)
                            if t >= 1:
                                act.wait_ge(s_f0, t)
                            if t >= 2:
                                act.wait_ge(s_fd[t % 2], 16 * (t // 2))
                            link(nc.scalar.activation(f[:, t % 2], h[:, t], ACT.Square, accum_out=st[:, 0:1]))
                            nc.scalar.activation(st[:, 1:2], st[:, 0:1], ACT.Sqrt, bias=eps, scale=1.0 / D).then_inc(s_rt, 1)

                        evac("O", 0)
                        for k in range(KD):
                            act.wait_ge(s_w[k], 16)
                            nc.scalar.activation(w_hi[:, k], w_raw[k], ACT.Copy).then_inc(s_wh, 1)
                        for t in range(nt + 1):
                            if t + 1 < nt:
                                evac("O", t + 1)
                            if t >= 1:
                                evac("F", t - 1)
                            if t < nt:
                                norm(t)

                    @block.vector
                    def _(dve):
                        link = Chain(dve, s_dve)

                        def low(t):
                            dve.wait_ge(s_oT, use["O", t] + 1)
                            if gain_in is None:
                                nc.vector.tensor_tensor(oT_lo[:, t % 2], psT[:, use["O", t] % 2], oT_hi[:, t % 2].bitcast(F32), ALU.subtract).then_inc(s_ol, 1)
                            else:
                                nc.vector.scalar_tensor_tensor(oT_lo[:, t % 2], psT[:, use["O", t] % 2], gsub[:, 0:1], oT_hi[:, t % 2].bitcast(F32),
                                                               ALU.mult, ALU.subtract).then_inc(s_ol, 1)

                        low(0)
                        for k in range(KD):
                            dve.wait_ge(s_wh, k + 1)
                            nc.vector.tensor_tensor(w_lo[:, k], w_raw[k], w_hi[:, k].bitcast(F32), ALU.subtract).then_inc(s_wl, 1)

                        def logits(t):
                            dve.wait_ge(s_r, t + 1)
                            nc.vector.tensor_copy(lg[:, t], psR[:, 0:NE]).then_inc(s_lg, 1)

                        for t in range(nt):
                            v = 0 if t < NL else 1
                            if t + 1 < nt:
                                low(t + 1)
                            if t == 0:
                                dve.wait_ge(s_v, 16 * 3 * nv)
                            dve.wait_ge(s_y, t + 1)
                            if t >= 1:
                                dve.wait_ge(s_h, t)
                            for b in range(2):
                                sl = slice(512 * b, 512 * b + 512)
                                ins = nc.vector.tensor_tensor(y[:, sl], psY[:, b], gate[:, v, sl], ALU.mult)
                            ins.then_inc(s_yev, 1)
                            if t >= 1:
                                logits(t - 1)
                            dve.wait_ge(s_rt, t + 1)
                            link(nc.vector.reciprocal(st[:, 2:3], st[:, 1:2]))
                            if t >= 2:
                                dve.wait_ge(s_fd[t % 2], 16 * (t // 2))
                                dve.wait_ge(s_to, use["F", t - 2] + 1)
                            nc.vector.scalar_tensor_tensor(f[:, t % 2], h[:, t], st[:, 2:3], fmul[:, v], ALU.mult, ALU.mult).then_inc(s_f0, 1)
                        logits(nt - 1)

                    @block.gpsimd
                    def _(pool):
                        for t in range(nt):
                            v = 0 if t < NL else 1
                            pool.wait_ge(s_yev, t + 1)
                            nc.gpsimd.tensor_tensor(h[:, t], h[:, t], y[:], ALU.add).then_inc(s_h, 1)
                            pool.wait_ge(s_f0, t + 1)
                            nc.gpsimd.tensor_tensor(f[:, t % 2], f[:, t % 2], fadd[:, v], ALU.add).then_inc(s_f, 1)

                    @block.tensor
                    def _(pe):
                        def turn(kind, t):
                            n = use[kind, t]
                            if n >= 2:
                                pe.wait_ge(s_oT, n - 1)
                                if uses[n - 2][0] == "O":
                                    pe.wait_ge(s_ol, uses[n - 2][1] + 1)
                            if kind == "F":
                                pe.wait_ge(s_f, t + 1)
                                v = f[:, t % 2].rearrange("q (p k) -> q k p", k=KD)
                            else:
                                v = o[:, t].rearrange("q (k p) -> q k p", p=P)
                            for k in range(KD):
                                ins = nc.tensor.transpose(psT[:, n % 2, k], v[:, k], ident)
                            ins.then_inc(s_to, 1)

                        turn("O", 0)
                        for t in range(nt + 1):
                            if t + 1 < nt:
                                turn("O", t + 1)
                            if t < nt:
                                pe.wait_ge(s_ol, t + 1)
                                if t >= 1:
                                    pe.wait_ge(s_yev, t)
                                for k in range(KD):
                                    if t == 0:
                                        pe.wait_ge(s_wl, k + 1)
                                    for b in range(2):
                                        c, xh = slice(b * 512, (b + 1) * 512), oT_hi[:, t % 2, k]
                                        nc.tensor.matmul(psY[:, b], xh, w_hi[:, k, c], start=(k == 0), stop=False)
                                        nc.tensor.matmul(psY[:, b], xh, w_lo[:, k, c], start=False, stop=False)
                                        ins = nc.tensor.matmul(psY[:, b], oT_lo[:, t % 2, k], w_hi[:, k, c], start=False, stop=(k == KD - 1))
                                ins.then_inc(s_y, 1)
                            if t >= 1:
                                turn("F", t - 1)
                                pe.wait_ge(s_oT, use["F", t - 1] + 1)
                                if t == 1:
                                    pe.wait_ge(s_wr, 16)
                                if t >= 2:
                                    pe.wait_ge(s_lg, t - 1)
                                for k in range(KD):
                                    ins = nc.tensor.matmul(psR[:, 0:NE], fT[:, k, (t - 1) * P:t * P], w_r[:, k], start=(k == 0), stop=(k == KD - 1))
                                ins.then_inc(s_r, 1)

        PARTS, AWAY = 6, 3

        class Moe:

            def __init__(self, ctx, l):
                self.gu_raw = sb(ctx, f"gu_raw{l}", [P, 2, 2, KD, FF])
                self.d_raw = sb(ctx, f"d_raw{l}", [P, 2, KF, D])
                self.tok = sb(ctx, f"tok{l}", [P, TBL], I32)
                self.wgt = sb(ctx, f"wgt{l}", [P, TBL])
                self.s_raw = [nc.alloc_semaphore(f"raw{l}_{i}") for i in range(AWAY)]

        def load_part(eng, l, moe, j, e, m):
            if m < 4:
                k = slice(m % 2 * KD // 2, (m % 2 + 1) * KD // 2)
                dst, src = moe.gu_raw[:, j, m // 2, k], a[("we_gate", "we_up")[m // 2]][l, bass.ds(e, 1)].rearrange("o (p k) n -> p (o k) n", p=P)[:, k]
            else:
                dst, src = moe.d_raw[:, j, m % 2], a["we_down"][l, bass.ds(e, 1)].rearrange("o (p k) n -> p (o k) n", p=P)[:, m % 2]
            eng.dma_start(dst, src).then_inc(moe.s_raw[m % AWAY], 16)

        def raw_loads(e, m):
            return 16 * (PARTS // AWAY) * e + 16 * (m // AWAY + 1)

        def stage_route(l, nt, fT, lg, room, moe):
            NB8 = nt * TOPK
            with ExitStack() as ctx:
                S = lambda n: sem(f"E{l}_{n}_s")
                T = lambda n, shape, dt=F32: sb(ctx, f"E{l}_{n}", shape, dt)
                wgu = T("wgu", [P, 2, KD, FF])
                wd = T("wd", [P, KF, D])
                sg = T("sg", [P, 2, FF])
                up = T("up", [P, 2, FF])
                hT = T("hT", [P, 2, KF, P])
                brt = T("brt", [P, NE])
                sc = T("sc", [P, nt, NE])
                bi = T("bi", [P, nt, NE])
                srt = T("srt", [P, nt * NG, 8])
                gs = T("gs", [P, nt, NG])
                cmp1 = T("cmp1", [P, nt, NG, NG])
                cmp2 = T("cmp2", [P, nt, NG, NG])
                gm = T("gm", [P, nt * NG])
                rep = T("rep", [P, nt, NE])
                top8 = T("top8", [P, nt, 8])
                sel = T("sel", [P, nt, NE])
                wt = T("wt", [P, nt, NE])
                tot = T("tot", [P, nt])
                nb = T("nb", [P, NE])
                bend = T("bend", [P, NE])
                bst = T("bst", [P, NE])
                v = T("v", [P, nt, NE])
                v8 = T("v8", [P, nt, 8])
                w8 = T("w8", [P, nt, 8])
                d8 = T("d8", [P, NB8], I32)
                d8i = T("d8i", [P, 2, NB8], I32)
                place = T("place", [P, NB8])
                blk = T("blk", [P, NB8])
                tokv = T("tokv", [P, NB8])
                rm = room[:].rearrange("p t d -> p (t d)")
                eq = rm[:, 0:nt * TOPK * NE].rearrange("p (t k e) -> p t k e", t=nt, k=TOPK)
                oneb = rm[:, 0:TOPK * TBL].rearrange("p (k n) -> p k n", n=TBL)
                ysh = rm[:, NT * TOPK * NE:NT * TOPK * NE + 2 * D].rearrange("p (u d) -> p u d", u=2)
                zero = rm[:, NT * TOPK * NE + 2 * D:NT * TOPK * NE + 3 * D]
                pay = T("pay", [P, 2, TOPK, 3, TBL], F32R)
                onep = T("onep", [P, 2, TOPK, P], F32R)
                w8hl = T("w8hl", [P, 2, NB8], F32R)
                ones = cst[:, C_ONE:C_ONE + P]
                upper = cst[:, C_U:C_U + P]
                psG = ps(ctx, f"E{l}_psG", [P, 2, 512])
                psH = ps(ctx, f"E{l}_psH", [P, 4, P])
                psY = ps(ctx, f"E{l}_psY", [P, 2, 512])
                psK = ps(ctx, f"E{l}_psK", [P, 512])
                psN = ps(ctx, f"E{l}_psN", [P, 512])
                psS = ps(ctx, f"E{l}_psS", [P, 512])
                s_w, s_wd_, s_br, s_sig = [S("w0"), S("w1")], S("wd_"), S("br"), S("sig")
                s_gu, s_gc, s_hm, s_ht, s_hT, s_dn, s_ys = S("gu"), S("gc"), S("hm"), S("ht"), S("hT"), S("dn"), S("ys")
                s_yd = [S("yd0"), S("yd1")]
                s_sel, s_rk, s_tab, s_tmm, s_dve, s_z, s_zd = S("sel"), S("rk"), S("tab"), S("tmm"), S("dve"), S("z"), S("zd")

                with nc.Block() as block:
                    @block.sync
                    def _(sp):
                        sp.dma_start(brt[:], a["b_router"][l:l + 1, :].to_broadcast([P, NE])).then_inc(s_br, 16)
                        for i in range(2):
                            k = slice(i * KD // 2, (i + 1) * KD // 2)
                            sp.dma_start(wgu[:, 0, k], kview(a["ws_gate"][l])[:, k]).then_inc(s_w[i], 16)
                            sp.dma_start(wgu[:, 1, k], kview(a["ws_up"][l])[:, k]).then_inc(s_w[i], 16)
                        sp.dma_start(wd[:], kview(a["ws_down"][l])).then_inc(s_wd_, 16)
                        for e in range(2):
                            for m in range(PARTS):
                                load_part(sp, l, moe, e, e, m)
                        sp.wait_ge(s_z, 1)
                        sp.dma_start(acc_d[l][NT * P:], zero).then_inc(s_zd, 16)
                        for t in range(nt):
                            sp.wait_ge(s_ys, t + 1)
                            sp.dma_start(acc_d[l][t * P:(t + 1) * P], ysh[:, t % 2]).then_inc(s_yd[t % 2], 16)
                        for b in range(2):
                            sp.wait_ge(s_yd[b], 16 * ((nt - b + 1) // 2))
                        sp.wait_ge(s_zd, 16)

                    @block.tensor
                    def _(pe):
                        def gate_up(t):
                            for k in range(KD):
                                if t == 0 and k % (KD // 2) == 0:
                                    pe.wait_ge(s_w[k // (KD // 2)], 32)
                                ins = nc.tensor.matmul(psG[:, t % 2].rearrange("p (v f) -> p v f", v=2), fT[:, k, t * P:(t + 1) * P], wgu[:, :, k],
                                                       start=(k == 0), stop=(k == KD - 1))
                            ins.then_inc(s_gu, 1)

                        def turn(t):
                            pe.wait_ge(s_hm, t + 1)
                            if t >= 1:
                                pe.wait_ge(s_hT, t)
                            x = up[:, t % 2].rearrange("q (p k) -> q k p", k=KF)
                            for k in range(KF):
                                ins = nc.tensor.transpose(psH[:, k], x[:, k], ident)
                            ins.then_inc(s_ht, 1)

                        def down(t):
                            pe.wait_ge(s_hT, t + 1)
                            if t == 0:
                                pe.wait_ge(s_wd_, 16)
                            if t >= 1:
                                pe.wait_ge(s_ys, t)
                            for b in range(2):
                                for k in range(KF):
                                    ins = nc.tensor.matmul(psY[:, b], hT[:, t % 2, k], wd[:, k, b * 512:(b + 1) * 512], start=(k == 0), stop=(k == KF - 1))
                            ins.then_inc(s_dn, 1)

                        def ranks():
                            pe.wait_ge(s_sel, 1)
                            for t in range(nt):
                                for j in range(t + 1):
                                    nc.tensor.matmul(psK[:, t * NE:(t + 1) * NE], upper if j == t else ones, sel[:, j], start=(j == 0), stop=(j == t))
                            for j in range(nt):
                                ins = nc.tensor.matmul(psN[:, 0:NE], ones, sel[:, j], start=(j == 0), stop=(j == nt - 1))
                            ins.then_inc(s_rk, 1)

                        def table(t):
                            pe.wait_ge(s_tab, t + 1)
                            for k in range(TOPK):
                                ins = nc.tensor.matmul(psS[:, 0:3 * TBL].rearrange("p (c n) -> p c n", c=3), onep[:, t % 2, k], pay[:, t % 2, k],
                                                       start=(t == 0 and k == 0), stop=(t == nt - 1 and k == TOPK - 1))
                            ins.then_inc(s_tmm, 1)

                        gate_up(0)
                        if nt == NL:
                            ranks()
                        tables = iter(range(nt))
                        for t in range(nt):
                            if t + 1 < nt:
                                gate_up(t + 1)
                                if t >= 3:
                                    table(next(tables))
                            if t == 0 and nt > NL:
                                ranks()
                            turn(t)
                            down(t)
                            if t >= 2:
                                table(next(tables))
                        for q in tables:
                            table(q)

                    @block.scalar
                    def _(act):
                        nc.scalar.activation(sc[:], lg[:, 0:nt], ACT.Sigmoid).then_inc(s_sig, 1)

                        def copies(t):
                            act.wait_ge(s_gu, t + 1)
                            if t >= 2:
                                act.wait_ge(s_ht, t - 1)
                            nc.scalar.activation(sg[:, t % 2], psG[:, t % 2, 0:FF], ACT.Silu)
                            nc.scalar.activation(up[:, t % 2], psG[:, t % 2, FF:2 * FF], ACT.Copy).then_inc(s_gc, 1)

                        copies(0)
                        for t in range(nt):
                            if t + 1 < nt:
                                copies(t + 1)
                            act.wait_ge(s_ht, t + 1)
                            nc.scalar.activation(hT[:, t % 2], psH[:, 0:KF], ACT.Copy).then_inc(s_hT, 1)
                            act.wait_ge(s_dn, t + 1)
                            if t >= 2:
                                act.wait_ge(s_yd[t % 2], 16 * (t // 2))
                            nc.scalar.activation(ysh[:, t % 2].rearrange("p (b n) -> p b n", b=2), psY[:], ACT.Copy).then_inc(s_ys, 1)

                    @block.gpsimd
                    def _(pool):
                        nc.gpsimd.memset(zero, 0.0).then_inc(s_z, 1)
                        for t in range(nt):
                            pool.wait_ge(s_gc, t + 1)
                            nc.gpsimd.tensor_tensor(up[:, t % 2], up[:, t % 2], sg[:, t % 2], ALU.mult).then_inc(s_hm, 1)

                    @block.vector
                    def _(dve):
                        link = Chain(dve, s_dve)
                        V = nc.vector
                        dve.wait_ge(s_sig, 1)
                        dve.wait_ge(s_br, 16)
                        link(V.tensor_tensor(bi[:], sc[:], bc(brt[:], nt), ALU.add))
                        big = bi[:].rearrange("p t (g e) -> p (t g) e", g=NG)
                        for i in range(nt * NG):
                            ins = V.max(srt[:, i], big[:, i])
                        link(ins)
                        link(V.tensor_tensor(gs[:].rearrange("p t g -> p (t g)"), srt[:, :, 0], srt[:, :, 1], ALU.add))
                        me = bcl(gs[:], NG)
                        other = gs[:].unsqueeze(2).to_broadcast([P, nt, NG, NG])
                        tri = cst[:, C_TRI:C_TRI + NG * NG]
                        f3 = lambda x: x.rearrange("p t i j -> p t (i j)")
                        V.tensor_tensor(cmp1[:], other, me, ALU.is_gt)
                        link(V.tensor_tensor(cmp2[:], other, me, ALU.is_equal))
                        link(V.tensor_tensor(f3(cmp2[:]), f3(cmp2[:]), bc(tri, nt), ALU.mult))
                        link(V.tensor_tensor(cmp1[:], cmp1[:], cmp2[:], ALU.add))
                        link(V.tensor_reduce(gm[:], cmp1[:].rearrange("p t i j -> p (t i) j"), AX, ALU.add))
                        link(V.tensor_scalar(gm[:], gm[:], float(TOPG) - 0.5, None, ALU.is_lt))
                        link(V.tensor_tensor(big, big, bcl(gm[:], NE // NG), ALU.mult))
                        link(V.tensor_scalar(gm[:], gm[:], -NEG, NEG, ALU.mult, ALU.add))
                        link(V.tensor_tensor(big, big, bcl(gm[:], NE // NG), ALU.add))
                        for t in range(nt):
                            ins = V.max(top8[:, t], bi[:, t])
                        link(ins)
                        for t in range(nt):
                            ins = V.match_replace(rep[:, t], top8[:, t], bi[:, t], -3e38)
                        link(ins)
                        link(V.tensor_tensor(sel[:], bi[:], rep[:], ALU.is_gt), s_sel)
                        link(V.tensor_tensor(wt[:], sc[:], sel[:], ALU.mult))
                        link(V.tensor_reduce(tot[:], wt[:], AX, ALU.add))
                        link(V.reciprocal(tot[:], tot[:]))
                        link(V.tensor_scalar(tot[:], tot[:], ROUTED, None, ALU.mult))
                        link(V.tensor_tensor(wt[:], wt[:], bcl(tot[:], NE), ALU.mult))
                        dve.wait_ge(s_rk, 1)
                        link(V.tensor_scalar(nb[:], psN[:, 0:NE], P + 0.5, 1.0, ALU.is_gt, ALU.add))
                        for j in range(2, nt):
                            link(V.scalar_tensor_tensor(nb[:], psN[:, 0:NE], P * j + 0.5, nb[:], ALU.is_gt, ALU.add))
                        link(V.tensor_tensor_scan(bend[:], ones[:, 0:NE], nb[:], 0.0, ALU.mult, ALU.add))
                        link(V.tensor_tensor(bst[:], bend[:], nb[:], ALU.subtract))
                        V.tensor_copy(starts_i[0:1, 0:NE], bst[0:1])
                        link(V.tensor_copy(starts_i[0:1, NE:NE + 1], bend[0:1, NE - 1:NE]))
                        link(V.tensor_scalar(bst[:], bst[:], -float(P), float(FAR), ALU.mult, ALU.add))
                        rk = psK[:, 0:nt * NE].rearrange("p (t e) -> p t e", e=NE)
                        link(V.tensor_tensor(v[:], bc(bst[:], nt), rk, ALU.subtract))
                        link(V.tensor_tensor(v[:], v[:], sel[:], ALU.mult))
                        for t in range(nt):
                            ins = V.max(v8[:, t], v[:, t])
                        link(ins)
                        for t in range(nt):
                            V.tensor_tensor(eq[:, t], v[:, t].unsqueeze(1).to_broadcast([P, 8, NE]), bcl(v8[:, t], NE), ALU.is_equal).then_inc(s_dve, 1)
                            link.count[id(s_dve)] += 1
                        dve.wait_ge(s_dve, link.count[id(s_dve)])
                        for t in range(nt):
                            ins = V.tensor_tensor(eq[:, t], eq[:, t], bc(wt[:, t], 8), ALU.mult)
                        link(ins)
                        link(V.tensor_reduce(w8[:].rearrange("p t k -> p (t k)"), eq.rearrange("p t k e -> p (t k) e"), AX, ALU.add))
                        w8f = w8[:].rearrange("p t k -> p (t k)")
                        link(V.tensor_copy(w8hl[:, 0], w8f))
                        link(V.tensor_tensor(w8hl[:, 1], w8f, w8hl[:, 0].bitcast(F32), ALU.subtract))
                        v8f = v8[:].rearrange("p t k -> p (t k)")
                        link(V.tensor_scalar(d8[:], v8f, -1.0, float(FAR), ALU.mult, ALU.add))
                        V.tensor_scalar(d8i[:, 0], d8[:], P - 1, None, ALU.bitwise_and)
                        link(V.tensor_scalar(d8i[:, 1], d8[:], 7, None, ALU.arith_shift_right))
                        V.tensor_copy(blk[:], d8i[:, 1])
                        link(V.tensor_copy(place[:], d8i[:, 0]))
                        tok = cst[:, C_TOK:C_TOK + nt]
                        link(V.tensor_tensor(tokv[:].rearrange("p (t k) -> p t k", k=8), bcl(tok, 8), place[:].rearrange("p (t k) -> p t k", k=8), ALU.subtract))
                        link(V.tensor_scalar(tokv[:], tokv[:], -float(NT * P), None, ALU.add))
                        for t in range(nt):
                            c = slice(t * TOPK, (t + 1) * TOPK)
                            V.tensor_tensor(oneb, bc(cst[:, C_COL:C_COL + TBL], TOPK), bcl(blk[:, c], TBL), ALU.is_equal).then_inc(s_dve, 1)
                            link.count[id(s_dve)] += 1
                            dve.wait_ge(s_dve, link.count[id(s_dve)])
                            if t >= 2:
                                dve.wait_ge(s_tmm, t - 1)
                            V.tensor_tensor(onep[:, t % 2], bc(cst[:, C_COL:C_COL + P], TOPK), bcl(place[:, c], P), ALU.is_equal)
                            V.tensor_tensor(pay[:, t % 2, :, 0], oneb, bcl(tokv[:, c], TBL), ALU.mult)
                            for n in range(2):
                                ins = V.tensor_tensor(pay[:, t % 2, :, 1 + n], oneb, bcl(w8hl[:, n, c].bitcast(F32), TBL), ALU.mult)
                            link(ins, s_tab)
                        dve.wait_ge(s_tmm, nt)
                        V.tensor_scalar(moe.tok[:], psS[:, 0:TBL], cst[:, C_IOTA:C_IOTA + 1], float(NT * P), ALU.add, ALU.add)
                        link(V.tensor_copy(moe.wgt[:], psS[:, TBL:2 * TBL]))
                        V.tensor_tensor(moe.wgt[:], moe.wgt[:], psS[:, 2 * TBL:3 * TBL], ALU.add)

        def stage_experts(l, nt, moe):
            with ExitStack() as ctx:
                S = lambda n: sem(f"F{l}_{n}_s")
                T = lambda n, shape, dt=F32: sb(ctx, f"F{l}_{n}", shape, dt)
                gu_raw, d_raw, s_raw = moe.gu_raw, moe.d_raw, moe.s_raw
                held.extend(s_raw)
                gu_hi = T("gu_hi", [P, 2, 2, KD, FF], F32R)
                gu_lo = T("gu_lo", [P, 2, 2, KD, FF], F32R)
                d_hi = T("d_hi", [P, 2, KF, D], F32R)
                d_lo = T("d_lo", [P, 2, KF, D], F32R)
                xb = T("xb", [P, D])
                xT_hi = T("xT_hi", [P, KD, P], F32R)
                xT_lo = T("xT_lo", [P, KD, P], F32R)
                sil = T("sil", [P, FF])
                hh = T("hh", [P, FF])
                hT_hi = T("hT_hi", [P, KF, P], F32R)
                hT_lo = T("hT_lo", [P, KF, P], F32R)
                yb = T("yb", [P, D])
                gi = T("gi", [P, 1], I32)
                si = T("si", [P, 1], I32)
                psX = ps(ctx, f"F{l}_psX", [P, 2, 4, P])
                psG = ps(ctx, f"F{l}_psG", [P, 512])
                psH = ps(ctx, f"F{l}_psH", [P, 4, P])
                psY = ps(ctx, f"F{l}_psY", [P, 2, 512])
                s_xb0 = S("xb0")
                s_x = S("x")
                s_guh, s_gul, s_dh, s_dl = S("guh"), S("gul"), S("dh"), S("dl")
                s_tx, s_gu, s_ht, s_dn = S("tx"), S("gu"), S("ht"), S("dn")
                s_xh, s_xl, s_sil, s_mul, s_hTh, s_hTl, s_ya, s_yd = (S(n) for n in ("xh", "xl", "sil", "mul", "hTh", "hTl", "ya", "yd"))
                s_bear = S("bear")
                s_gi, s_sidx, s_sc = S("gi"), S("sidx"), S("sc")

                def all_steps(eng, step, last):
                    def first_block(e, least):
                        return eng.value_load(starts_i[0:1, bass.ds(e, 1)], min_val=least, max_val=MAXBLK)

                    def expert(e, j, change):
                        b0, b1 = first_block(e, 0), first_block(e + 1, 1)
                        with eng.If(b1 > b0 + 1):
                            with eng.Fori(b0 + 1, b1) as b:
                                step(b, j, False, e, False)
                        change(b1)

                    with eng.Fori(0, NE // 2 - 1) as i:
                        for j in range(2):
                            e = 2 * i + j
                            expert(e, j, lambda b: step(b, j, True, e, True))
                    expert(NE - 2, 0, lambda b: step(b, 0, True, NE - 2, False))
                    expert(NE - 1, 1, last)

                with nc.Block() as block:
                    @block.sync
                    def _(sp):
                        with sp.Fori(0, NE // 2 - 1) as i:
                            for j in range(2):
                                e = 2 * i + j
                                for m in range(PARTS):
                                    if m == 0:
                                        sp.wait_ge(s_gul, 2 * e + 1)
                                    elif m == 2:
                                        sp.wait_ge(s_gul, 2 * e + 2)
                                    elif m == 4:
                                        sp.wait_ge(s_dl, e + 1)
                                    sp.sem_inc(s_bear, 1)
                                    sp.wait_ge(s_raw[m % AWAY], raw_loads(e + 2, m) - 16)
                                    sp.sem_inc(s_bear, 1)
                                    load_part(sp, l, moe, j, e + 2, m)

                    @block.gpsimd
                    def _(pool):
                        G = nc.gpsimd
                        G.memset(xb[:], 0.0).then_inc(s_xb0, 1)
                        pool.wait_ge(s_xb0, 1)

                        def gather(b):
                            G.tensor_copy(gi[:], moe.tok[:, bass.ds(b, 1)]).then_inc(s_gi, 1)
                            pool.wait_ge(s_gi, b + 1)
                            pool.sem_inc(s_bear, 1)
                            pool.indirect_dma_start(xb[:], None, f_d[l][0:nt * P], bass.IndirectOffsetOnAxis(ap=gi[:].bitcast(U32), axis=0),
                                                    bounds_check=nt * P - 1, oob_is_err=False).then_inc(s_x, 16)

                        def scatter():
                            pool.indirect_dma_start(acc_d[l], bass.IndirectOffsetOnAxis(ap=si[:].bitcast(U32), axis=0), yb[:], None,
                                                    compute_op=ALU.add).then_inc(s_sc, 16)

                        def split_down(j, e):
                            pool.wait_ge(s_dh, e + 1)
                            G.tensor_tensor(d_lo[:, j], d_raw[:, j], d_hi[:, j].bitcast(F32), ALU.subtract).then_inc(s_dl, 1)

                        def take_rows(b):
                            pool.wait_ge(s_sc, 16 * b + 16)
                            G.tensor_copy(si[:], moe.tok[:, bass.ds(b, 1)]).then_inc(s_sidx, 1)

                        def give(b):
                            pool.wait_ge(s_ya, b + 2)
                            pool.wait_ge(s_yd, b + 2)
                            pool.sem_inc(s_bear, 1)
                            scatter()

                        gather(0)
                        G.memset(yb[:], 0.0).then_inc(s_xb0, 1)
                        G.tensor_copy(si[:], moe.tok[:, TBL - 1:TBL]).then_inc(s_xb0, 1)
                        pool.wait_ge(s_xb0, 3)
                        scatter()
                        split_down(0, 0)
                        pool.wait_ge(s_tx, 1)
                        gather(1)
                        pool.wait_ge(s_tx, 2)
                        gather(2)
                        split_down(1, 1)

                        def step(b, j, change, e, split):
                            take_rows(b - 1)
                            pool.wait_ge(s_tx, b + 2)
                            gather(b + 2)
                            give(b - 1)
                            if split:
                                split_down(j, e + 2)

                        def last(b):
                            take_rows(b - 1)
                            give(b - 1)
                            pool.wait_ge(s_sc, 16 * b + 16)
                            pool.wait_ge(s_x, 16 * b + 32)
                            pool.sem_inc(s_bear, 1)

                        all_steps(pool, step, last)

                    @block.tensor
                    def _(pe):
                        pe.sem_inc(s_ya, 1)
                        pe.sem_inc(s_yd, 1)

                        def turn_rows():
                            v = xb[:].rearrange("q (p k) -> q k p", k=KD)
                            for k in range(KD):
                                ins = nc.tensor.transpose(psX[:, k // 4, k % 4], v[:, k], ident)
                            ins.then_inc(s_tx, 1)

                        def gate_up(j):
                            product(nc, psG[:].rearrange("p (v f) -> p v f", v=2),
                                    [(xT_hi[:, k], xT_lo[:, k], gu_hi[:, j, :, k], gu_lo[:, j, :, k]) for k in range(KD)], s_gu)

                        def turn_hidden():
                            v = hh[:].rearrange("q (p k) -> q k p", k=KF)
                            for k in range(KF):
                                ins = nc.tensor.transpose(psH[:, k], v[:, k], ident)
                            ins.then_inc(s_ht, 1)

                        def down(j):
                            for n in range(2):
                                c = slice(n * 512, (n + 1) * 512)
                                product(nc, psY[:, n], [(hT_hi[:, k], hT_lo[:, k], d_hi[:, j, k, c], d_lo[:, j, k, c]) for k in range(KF)], s_dn if n == 1 else None)

                        pe.wait_ge(s_x, 16)
                        turn_rows()
                        pe.wait_ge(s_xl, 2)
                        pe.wait_ge(s_gul, 2)
                        gate_up(0)
                        pe.wait_ge(s_x, 32)
                        turn_rows()

                        def down_of(b, j, e):
                            pe.wait_ge(s_hTl, b + 1)
                            pe.wait_ge(s_dl, e + 1)
                            pe.wait_ge(s_ya, b + 1)
                            pe.wait_ge(s_yd, b + 1)
                            down(j)

                        def step(b, j, change, e, split):
                            pe.wait_ge(s_mul, b)
                            turn_hidden()
                            pe.wait_ge(s_xl, 2 * b + 2)
                            if change:
                                pe.wait_ge(s_gul, 2 * e + 4)
                            gate_up(1 - j if change else j)
                            pe.wait_ge(s_x, 16 * b + 32)
                            turn_rows()
                            down_of(b - 1, j, e)

                        def last(b):
                            pe.wait_ge(s_mul, b)
                            turn_hidden()
                            down_of(b - 1, 1, NE - 1)

                        all_steps(pe, step, last)

                    @block.scalar
                    def _(act):
                        def rows():
                            for n in range(2):
                                nc.scalar.activation(xT_hi[:, 4 * n:4 * n + 4], psX[:, n], ACT.Copy).then_inc(s_xh, 1)

                        def silu():
                            nc.scalar.activation(sil[:], psG[:, 0:FF], ACT.Silu).then_inc(s_sil, 1)

                        def split_gate_up(j, e, loading=True):
                            for v in range(2):
                                if loading:
                                    for m in (2 * v, 2 * v + 1):
                                        act.wait_ge(s_raw[m % AWAY], raw_loads(e, m))
                                nc.scalar.activation(gu_hi[:, j, v], gu_raw[:, j, v], ACT.Copy).then_inc(s_guh, 1)

                        def split_down(j, e, loading=True):
                            if loading:
                                for m in (4, 5):
                                    act.wait_ge(s_raw[m % AWAY], raw_loads(e, m))
                            nc.scalar.activation(d_hi[:, j], d_raw[:, j], ACT.Copy).then_inc(s_dh, 1)

                        for m in range(PARTS - AWAY, PARTS):
                            act.wait_ge(s_raw[m % AWAY], raw_loads(1, m))
                        split_gate_up(0, 0, False)
                        split_down(0, 0, False)
                        act.wait_ge(s_tx, 1)
                        rows()
                        split_gate_up(1, 1, False)
                        split_down(1, 1, False)
                        act.wait_ge(s_gu, 1)
                        silu()
                        act.wait_ge(s_tx, 2)
                        rows()

                        def out_of(b):
                            act.wait_ge(s_dn, b + 1)
                            act.wait_ge(s_sidx, b + 1)
                            nc.scalar.activation(yb[:, 0:512], psY[:, 0], ACT.Copy, scale=moe.wgt[:, bass.ds(b, 1)]).then_inc(s_ya, 1)

                        def hidden(b):
                            act.wait_ge(s_ht, b + 1)
                            nc.scalar.activation(hT_hi[:], psH[:, 0:KF], ACT.Copy).then_inc(s_hTh, 1)

                        def step(b, j, change, e, split):
                            hidden(b - 1)
                            if split:
                                act.wait_ge(s_gu, b)
                                split_gate_up(j, e + 2)
                            act.wait_ge(s_gu, b + 1)
                            silu()
                            act.wait_ge(s_tx, b + 2)
                            rows()
                            out_of(b - 1)
                            if split:
                                split_down(j, e + 2)

                        def last(b):
                            hidden(b - 1)
                            out_of(b - 1)

                        all_steps(act, step, last)

                    @block.vector
                    def _(dve):
                        V = nc.vector

                        def rows(b):
                            for n in range(2):
                                dve.wait_ge(s_xh, 2 * b + n + 1)
                                k = slice(4 * n, 4 * n + 4)
                                V.tensor_tensor(xT_lo[:, k], psX[:, n], xT_hi[:, k].bitcast(F32), ALU.subtract).then_inc(s_xl, 1)

                        def product():
                            V.tensor_tensor(hh[:], sil[:], psG[:, FF:2 * FF], ALU.mult).then_inc(s_mul, 1)

                        def split_gate_up(j, e):
                            for v in range(2):
                                dve.wait_ge(s_guh, 2 * e + v + 1)
                                V.tensor_tensor(gu_lo[:, j, v], gu_raw[:, j, v], gu_hi[:, j, v].bitcast(F32), ALU.subtract).then_inc(s_gul, 1)

                        split_gate_up(0, 0)
                        rows(0)
                        split_gate_up(1, 1)
                        dve.wait_ge(s_sil, 1)
                        product()
                        rows(1)

                        def out_of(b):
                            dve.wait_ge(s_dn, b + 1)
                            dve.wait_ge(s_sidx, b + 1)
                            V.tensor_scalar(yb[:, 512:], psY[:, 1], moe.wgt[:, bass.ds(b, 1)], None, ALU.mult).then_inc(s_yd, 1)

                        def hidden(b):
                            dve.wait_ge(s_hTh, b + 1)
                            V.tensor_tensor(hT_lo[:], psH[:, 0:KF], hT_hi[:].bitcast(F32), ALU.subtract).then_inc(s_hTl, 1)

                        def step(b, j, change, e, split):
                            hidden(b - 1)
                            if split:
                                split_gate_up(j, e + 2)
                            dve.wait_ge(s_sil, b + 1)
                            product()
                            rows(b + 1)
                            out_of(b - 1)

                        def last(b):
                            hidden(b - 1)
                            out_of(b - 1)

                        all_steps(dve, step, last)

        def stage_combine(l, nt, aT):
            with ExitStack() as ctx:
                S = lambda n: sem(f"H{l}_{n}_s")
                T = lambda n, shape, dt=F32: sb(ctx, f"H{l}_{n}", shape, dt)
                nv = 2 if nt > NL else 1
                ac = T("ac", [P, 3, D])
                gate = T("gate", [P, nv, D])
                amul = T("amul", [P, nv, D])
                aadd = T("aadd", [P, nv, D])
                an = T("an", [P, 2, D])
                junk = T("junk", [P, D], BF16)
                st = T("st", [P, nt, 3])
                psT = ps(ctx, f"H{l}_psT", [P, 2, KD, P])
                s_v, s_ac = S("v"), [S(f"ac{i}") for i in range(3)]
                s_g, s_h, s_rt, s_a0, s_a, s_tp, s_tev, s_act, s_dve = (S(n) for n in ("g", "h", "rt", "a0", "a", "tp", "tev", "act", "dve"))
                s_thi, s_g0, s_out = S("thi"), S("g0"), [S("out0"), S("out1")]
                n_rows = 1 if aT is None else 2
                with nc.Block() as block:
                    @block.sync
                    def _(sp):
                        for t in range(nt):
                            if t >= 3:
                                sp.wait_ge(s_h, t - 2)
                            sp.dma_start(ac[:, t % 3], acc_d[l][t * P:(t + 1) * P]).then_inc(s_ac[t % 3], 16)
                        if aT is None:
                            for t in range(nt):
                                sp.wait_ge(s_a0, t + 1)
                                sp.dma_start(out[0, t * P:(t + 1) * P], an[:, t % 2]).then_inc(s_out[t % 2], 16)
                            for b in range(2):
                                sp.wait_ge(s_out[b], 16 * ((nt - b + 1) // 2))

                    @block.scalar
                    def _(act):
                        link = Chain(act, s_act)
                        act.dma_start(gate[:, 0], mod_rows(l, 0, 5)).then_inc(s_g0, 16)
                        if nv == 2:
                            act.dma_start(gate[:, 1], mod_rows(l, 1, 5)).then_inc(s_v, 16)
                        for v in range(nv):
                            if aT is not None:
                                act.dma_start(amul[:, v], mod_rows(l + 1, v, 1)).then_inc(s_v, 16)
                                act.dma_start(aadd[:, v], mod_rows(l + 1, v, 0)).then_inc(s_v, 16)
                            else:
                                act.dma_start(amul[:, v], a["g_final"].rearrange("(o d) -> o d", o=1).to_broadcast([P, D])).then_inc(s_v, 16)
                        def norm(t):
                            act.wait_ge(s_h, t + 1)
                            link(nc.scalar.activation(junk[:], h[:, t], ACT.Square, accum_out=st[:, t, 0:1]))
                            nc.scalar.activation(st[:, t, 1:2], st[:, t, 0:1], ACT.Sqrt, bias=eps, scale=1.0 / D).then_inc(s_rt, 1)

                        norm(0)
                        for t in range(nt):
                            if t + 1 < nt:
                                norm(t + 1)
                            if aT is not None:
                                act.wait_ge(s_tp, t + 1)
                                nc.scalar.activation(aT[0][:, :, t * P:(t + 1) * P], psT[:, t % 2], ACT.Copy).then_inc(s_thi, 1)

                    @block.vector
                    def _(dve):
                        link = Chain(dve, s_dve)
                        def gated(t):
                            dve.wait_ge(s_ac[t % 3], 16 * (t // 3 + 1))
                            nc.vector.tensor_tensor(ac[:, t % 3], ac[:, t % 3], gate[:, 0 if t < NL else 1], ALU.mult).then_inc(s_g, 1)

                        def low(t):
                            dve.wait_ge(s_thi, t + 1)
                            c = slice(t * P, (t + 1) * P)
                            nc.vector.tensor_tensor(aT[1][:, :, c], psT[:, t % 2], aT[0][:, :, c].bitcast(F32), ALU.subtract).then_inc(s_tev, 1)

                        dve.wait_ge(s_g0, 16)
                        gated(0)
                        for t in range(nt):
                            if t + 1 < nt:
                                gated(t + 1)
                            if t == 0:
                                dve.wait_ge(s_v, 16 * (nv - 1 + nv * n_rows))
                            dve.wait_ge(s_rt, t + 1)
                            link(nc.vector.reciprocal(st[:, t, 2:3], st[:, t, 1:2]))
                            if t >= 2:
                                if aT is not None:
                                    dve.wait_ge(s_tp, t - 1)
                                else:
                                    dve.wait_ge(s_out[t % 2], 16 * (t // 2))
                            nc.vector.scalar_tensor_tensor(an[:, t % 2], h[:, t], st[:, t, 2:3], amul[:, 0 if t < NL else 1], ALU.mult, ALU.mult).then_inc(s_a0, 1)
                            if aT is not None and t >= 1:
                                low(t - 1)
                        if aT is not None:
                            low(nt - 1)

                    @block.gpsimd
                    def _(pool):
                        def added(t):
                            pool.wait_ge(s_g, t + 1)
                            nc.gpsimd.tensor_tensor(h[:, t], h[:, t], ac[:, t % 3], ALU.add).then_inc(s_h, 1)

                        added(0)
                        for t in range(nt):
                            if t + 1 < nt:
                                added(t + 1)
                            if aT is not None:
                                pool.wait_ge(s_a0, t + 1)
                                nc.gpsimd.tensor_tensor(an[:, t % 2], an[:, t % 2], aadd[:, 0 if t < NL else 1], ALU.add).then_inc(s_a, 1)

                    @block.tensor
                    def _(pe):
                        if aT is not None:
                            for t in range(nt):
                                pe.wait_ge(s_a, t + 1)
                                if t >= 2:
                                    pe.wait_ge(s_tev, t - 1)
                                v = an[:, t % 2].rearrange("q (p k) -> q k p", k=KD)
                                for k in range(KD):
                                    ins = nc.tensor.transpose(psT[:, t % 2, k], v[:, k], ident)
                                ins.then_inc(s_tp, 1)

        def stage_attend1(aT, o):
            with ExitStack() as ctx:
                S = lambda n: sem(f"I_{n}_s")
                T = lambda n, shape, dt=F32: sb(ctx, f"I_{n}", shape, dt)
                w_raw = T("w_raw", [P, KD, DC])
                w_hi = T("w_hi", [P, 2, KD, DC], F32R)
                w_lo = T("w_lo", [P, 2, KD, DC], F32R)
                WS = 4
                qkT = T("qkT", [P, 2, 2, NT * P])
                vv = T("vv", [P, 2, NT, DV])
                qk = T("qk", [P, 2, 4, DHALF])
                t1 = T("t1", [P, 2, 4, DHALF])
                t2 = T("t2", [P, 2, 4, DHALF])
                prob = T("prob", [P, 2, 2, NT * P])
                pT = T("pT", [P, 2, NT, P])
                nmax = T("nmax", [P, 2, 2])
                ssum = T("ssum", [P, 2, 2])
                lamv = T("lamv", [P, 4, DHALF])
                lamj = T("lamj", [P, DHALF])
                lam2 = T("lam2", [P, 2])
                nlam = T("nlam", [P, 1])
                ost = T("ost", [P, NL, DH])
                psS = ps(ctx, "I_psS", [P, 2, 1024])
                psP = ps(ctx, "I_psP", [P, 8, P])
                psO = ps(ctx, "I_psO", [P, NL, DV])
                psC = ps(ctx, "I_psC", [P, 512])
                s_lam, s_lamd, s_w, s_wh, s_wl = S("lam"), S("lamd"), [S(f"w{i}") for i in range(WS)], S("wh"), S("wl")
                (s_pr, s_prd, s_pra, s_qk, s_tr, s_tre, s_s, s_nm, s_e, s_cb, s_p1, s_t, s_evd, s_eva, s_pv, s_o, s_act, s_dve, s_lame, s_fin, s_finr, s_rec) = (
                    S(n) for n in ("pr", "prd", "pra", "qk", "tr", "tre", "s", "nm", "e", "cb", "p1", "t", "evd", "eva", "pv", "o", "act", "dve", "lame", "fin", "finr", "rec"))
                cos = cst[:, C_COS:C_COS + NL * SD].rearrange("p (t d) -> p t d", t=NL)
                sin = cst[:, C_SIN:C_SIN + NL * SD].rearrange("p (t d) -> p t d", t=NL)
                beats = [(hd, s) for hd in range(DH + 1) for s in range(NT)]

                def tile_no(hd, s):
                    return hd * NT + s

                def order(hd, s):
                    work = []
                    if hd < DH and s < NT - 1:
                        work.append(("project", hd, s))
                    if hd >= 1 and 2 <= s < NL + 2:
                        work.append(("values", hd - 1, s - 2))
                    if s >= 1 and hd < DH:
                        work.append(("turn_qk", hd, s - 1))
                    if s == 0 and 1 <= hd:
                        work.append(("turn_qk", hd - 1, NT - 1))
                    if hd >= 1 and s < NL:
                        work.append(("scores", hd - 1, s))
                    if s == NT - 2 and hd < DH:
                        work.append(("project", hd, NT - 1))
                    if hd >= 1 and 1 <= s < NL + 1:
                        work.append(("turn", hd - 1, s - 1))
                    return work

                every = [x for hd, s in beats for x in order(hd, s)]

                def units_before(hd, s):
                    return sum(x[0] == "turn" for x in every[:every.index(("turn_qk", hd, s))])

                def turned_before(hd, t):
                    return sum(x[0] == "turn_qk" for x in every[:every.index(("turn", hd, t))])

                with nc.Block() as block:
                    @block.sync
                    def _(sp):
                        for n, name in enumerate(("lam_q1", "lam_k1", "lam_q2", "lam_k2")):
                            sp.dma_start(lamv[:, n], a[name][0:1, :].to_broadcast([P, DHALF])).then_inc(s_lam, 16)
                        for hd in range(DH):
                            if hd >= 1:
                                sp.wait_ge(s_wl, WS * hd)
                            for i in range(WS):
                                k = slice(i * KD // WS, (i + 1) * KD // WS)
                                sp.dma_start(w_raw[:, k], kview(a["wc_in"][0])[:, k, hd * DC:(hd + 1) * DC]).then_inc(s_w[i], 16)

                    @block.tensor
                    def _(pe):
                        def project(hd, s):
                            n = tile_no(hd, s)
                            if n >= 1:
                                pe.wait_ge(s_prd, n)
                                pe.wait_ge(s_pra, n)
                            c0 = 0 if s < NL else 2 * DHALF
                            c, b = slice(s * P, (s + 1) * P), hd % 2
                            for i in range(WS):
                                if s == 0:
                                    pe.wait_ge(s_wl, WS * hd + i + 1)
                                last = i == WS - 1
                                product(nc, psC[:, c0:DC], [(aT[0][:, k, c], aT[1][:, k, c], w_hi[:, b, k, c0:DC], w_lo[:, b, k, c0:DC])
                                                            for k in range(i * KD // WS, (i + 1) * KD // WS)], s_pr if last else None, i == 0, last)

                        def turn_qk(hd, s):
                            n = tile_no(hd, s)
                            pe.wait_ge(s_qk, n + 1)
                            if n >= 1:
                                pe.wait_ge(s_tre, n)
                            u = units_before(hd, s)
                            if u >= 1:
                                pe.wait_ge(s_eva, u)
                            if s < NL:
                                nc.tensor.transpose(psP[:, 6], qk[:, n % 2, 0:2].rearrange("p m d -> p (m d)"), ident)
                            nc.tensor.transpose(psP[:, 7], qk[:, n % 2, 2:4].rearrange("p m d -> p (m d)"), ident).then_inc(s_tr, 1)

                        def scores(hd, t):
                            u = hd * NL + t
                            if t == 0:
                                pe.wait_ge(s_tre, NT * (hd + 1))
                            for m in range(2):
                                if u >= 1:
                                    pe.wait_ge(s_e, 2 * (u - 1) + m + 1)
                                r = slice(64 * m, 64 * m + 64)
                                q = qkT[r, hd % 2, 0, t * P:(t + 1) * P]
                                nc.tensor.matmul(psS[:, m, 0:512], q, qkT[r, hd % 2, 1, 0:512], start=True, stop=True)
                                nc.tensor.matmul(psS[:, m, 512:768], q, qkT[r, hd % 2, 1, 512:768], start=True, stop=True).then_inc(s_s, 1)

                        def turn(hd, t):
                            u = hd * NL + t
                            pe.wait_ge(s_cb, u + 1)
                            if u >= 1:
                                pe.wait_ge(s_evd, u)
                                pe.wait_ge(s_eva, u)
                            n = turned_before(hd, t)
                            if n >= 1:
                                pe.wait_ge(s_tre, n)
                            for b in range(NT):
                                ins = nc.tensor.transpose(psP[:, b], prob[:, u % 2, 0, b * P:(b + 1) * P], ident)
                            ins.then_inc(s_t, 1)

                        def values(hd, t):
                            u = hd * NL + t
                            pe.wait_ge(s_evd, u + 1)
                            pe.wait_ge(s_eva, u + 1)
                            if t == 0 and hd >= 1:
                                pe.wait_ge(s_o, hd)
                            if t == 0:
                                pe.wait_ge(s_pra, NT * (hd + 1))
                            for b in range(NT):
                                ins = nc.tensor.matmul(psO[:, t], pT[:, u % 2, b], vv[:, hd % 2, b], start=(b == 0), stop=(b == NT - 1))
                            ins.then_inc(s_pv, 1)

                        for hd, s in beats:
                            for what, x, y in order(hd, s):
                                {"project": project, "values": values, "turn_qk": turn_qk, "scores": scores, "turn": turn}[what](x, y)

                    @block.vector
                    def _(dve):
                        link = Chain(dve, s_dve)
                        V = nc.vector
                        dve.wait_ge(s_lam, 64)
                        for m in range(2):
                            link(V.tensor_tensor_reduce(lamj[:], lamv[:, 2 * m], lamv[:, 2 * m + 1], 1.0, 0.0, ALU.mult, ALU.add, lam2[:, m:m + 1]))
                        V.tensor_copy(lam2[:], lam2[:]).then_inc(s_lamd, 1)
                        dve.wait_ge(s_lame, 1)
                        link(V.tensor_tensor(nlam[:], lam2[:, 1:2], lam2[:, 0:1], ALU.subtract))
                        link(V.tensor_scalar(nlam[:], nlam[:], -LAM_INIT, None, ALU.add))

                        def split_low(hd, i):
                            dve.wait_ge(s_wh, WS * hd + i + 1)
                            k = slice(i * KD // WS, (i + 1) * KD // WS)
                            V.tensor_tensor(w_lo[:, hd % 2, k], w_raw[:, k], w_hi[:, hd % 2, k].bitcast(F32), ALU.subtract).then_inc(s_wl, 1)

                        for i in range(WS):
                            split_low(0, i)

                        def rotate(hd, s):
                            n = tile_no(hd, s)
                            dve.wait_ge(s_pr, n + 1)
                            if n >= 2:
                                dve.wait_ge(s_qk, n - 1)
                                dve.wait_ge(s_tr, n - 1)
                            if s < NL:
                                src = psC[:, 0:4 * DHALF].rearrange("p (g d) -> p g d", d=DHALF)
                                q = DHALF // 4
                                V.tensor_tensor(t1[:, n % 2], src, bc(cos[:, s], 4), ALU.mult)
                                s4 = src.rearrange("p g (b two q) -> p g b two q", two=2, q=q)
                                t4 = t2[:, n % 2].rearrange("p g (b two q) -> p g b two q", two=2, q=q)
                                n4 = bc(sin[:, s], 4).rearrange("p g (b two q) -> p g b two q", two=2, q=q)
                                for b in range(2):
                                    V.tensor_tensor(t4[:, :, b, 0], s4[:, :, b, 1], n4[:, :, b, 0], ALU.mult)
                                    ins = V.tensor_tensor(t4[:, :, b, 1], s4[:, :, b, 0], n4[:, :, b, 1], ALU.mult)
                            else:
                                ins = V.tensor_copy(t1[:, n % 2, 2:4], psC[:, 2 * DHALF:4 * DHALF].rearrange("p (g d) -> p g d", d=DHALF))
                            link(ins, s_prd)

                        def maximum(hd, t):
                            u = hd * NL + t
                            for m in range(2):
                                dve.wait_ge(s_s, 2 * u + m + 1)
                                if u >= 2 and m == 0:
                                    dve.wait_ge(s_e, 2 * u - 2)
                                link(V.tensor_reduce(nmax[:, u % 2, m:m + 1], psS[:, m, 0:NT * P], AX, ALU.max, negate=True), s_nm)

                        def combine(hd, t):
                            u = hd * NL + t
                            dve.wait_ge(s_e, 2 * u + 2)
                            link(V.reciprocal(ssum[:, u % 2], ssum[:, u % 2]))
                            link(V.tensor_tensor(ssum[:, u % 2, 1:2], ssum[:, u % 2, 1:2], nlam[:], ALU.mult), s_p1)
                            link(V.tensor_scalar(prob[:, u % 2, 1], prob[:, u % 2, 1], ssum[:, u % 2, 1:2], None, ALU.mult))
                            link(V.scalar_tensor_tensor(prob[:, u % 2, 0], prob[:, u % 2, 0], ssum[:, u % 2, 0:1], prob[:, u % 2, 1], ALU.mult, ALU.add), s_cb)

                        def evac(hd, t):
                            u = hd * NL + t
                            dve.wait_ge(s_t, u + 1)
                            if u >= 2:
                                dve.wait_ge(s_pv, u - 1)
                            V.tensor_copy(pT[:, u % 2, 0:4], psP[:, 0:4]).then_inc(s_evd, 1)

                        def head_out(hd):
                            dve.wait_ge(s_pv, NL * (hd + 1))
                            oh = o[:, 0:NL, hd * DV:(hd + 1) * DV]
                            link(V.tensor_copy(oh, psO[:]))
                            link(V.tensor_tensor(psO[:], oh, oh, ALU.mult))
                            link(V.tensor_reduce(ost[:, :, hd], psO[:], AX, ALU.add), s_o)

                        for hd, s in beats:
                            if hd < DH:
                                rotate(hd, s)
                            if hd >= 1:
                                if s < NL:
                                    maximum(hd - 1, s)
                                    combine(hd - 1, s)
                                if 1 <= s < NL + 1:
                                    evac(hd - 1, s - 1)
                                if s == NL + 1:
                                    head_out(hd - 1)
                            if hd + 1 < DH and 1 <= s <= WS:
                                split_low(hd + 1, s - 1)
                        V.tensor_copy(ost[:], ost[:]).then_inc(s_fin, 1)
                        dve.wait_ge(s_finr, 1)
                        link(V.reciprocal(ost[:], ost[:]), s_rec)
                        for t in range(1, NL):
                            ov = o[:, t].rearrange("p (h d) -> p h d", d=DV)
                            V.tensor_tensor(ov, ov, bcl(ost[:, t], DV), ALU.mult)

                    @block.gpsimd
                    def _(pool):
                        for hd in range(DH):
                            for s in range(NT):
                                n = tile_no(hd, s)
                                pool.wait_ge(s_prd, n + 1)
                                if n >= 2:
                                    pool.wait_ge(s_tr, n - 1)
                                if s < NL:
                                    nc.gpsimd.tensor_tensor(qk[:, n % 2], t1[:, n % 2], t2[:, n % 2], ALU.add).then_inc(s_qk, 1)
                                else:
                                    nc.gpsimd.tensor_copy(qk[:, n % 2, 2:4], t1[:, n % 2, 2:4]).then_inc(s_qk, 1)
                        pool.wait_ge(s_rec, 1)
                        ov = o[:, 0].rearrange("p (h d) -> p h d", d=DV)
                        nc.gpsimd.tensor_tensor(ov, ov, bcl(ost[:, 0], DV), ALU.mult)

                    @block.scalar
                    def _(act):
                        link = Chain(act, s_act)
                        act.wait_ge(s_lamd, 1)
                        nc.scalar.activation(lam2[:], lam2[:], ACT.Exp).then_inc(s_lame, 1)

                        def split_high(hd, i):
                            act.wait_ge(s_w[i], 16 * (hd + 1))
                            if i == 0:
                                if hd >= 2:
                                    act.wait_ge(s_pr, NT * (hd - 1))
                            k = slice(i * KD // WS, (i + 1) * KD // WS)
                            nc.scalar.activation(w_hi[:, hd % 2, k], w_raw[:, k], ACT.Copy).then_inc(s_wh, 1)

                        for i in range(WS):
                            split_high(0, i)

                        def copy_v(hd, s):
                            n = tile_no(hd, s)
                            act.wait_ge(s_pr, n + 1)
                            act.wait_ge(s_prd, n + 1)
                            if s == 0 and hd >= 2:
                                act.wait_ge(s_pv, NL * (hd - 1))
                            nc.scalar.activation(vv[:, hd % 2, s], psC[:, 4 * DHALF:DC], ACT.Copy).then_inc(s_pra, 1)

                        def copy_qk(hd, s):
                            n = tile_no(hd, s)
                            act.wait_ge(s_tr, n + 1)
                            if s == 0 and hd >= 2:
                                act.wait_ge(s_s, 2 * NL * (hd - 1))
                            if s < NL:
                                nc.scalar.activation(qkT[:, hd % 2, 0, s * P:(s + 1) * P], psP[:, 6], ACT.Copy, scale=float(DHALF) ** -0.5)
                            nc.scalar.activation(qkT[:, hd % 2, 1, s * P:(s + 1) * P], psP[:, 7], ACT.Copy).then_inc(s_tre, 1)

                        def exps(hd, t):
                            u = hd * NL + t
                            if u >= 2:
                                act.wait_ge(s_t, u - 1)
                            for m in range(2):
                                act.wait_ge(s_nm, 2 * u + m + 1)
                                nc.scalar.activation(prob[:, u % 2, m], psS[:, m, 0:NT * P], ACT.Exp, bias=nmax[:, u % 2, m:m + 1],
                                                     accum_out=ssum[:, u % 2, m:m + 1]).then_inc(s_e, 1)

                        def evac(hd, t):
                            u = hd * NL + t
                            act.wait_ge(s_t, u + 1)
                            if u >= 2:
                                act.wait_ge(s_pv, u - 1)
                            nc.scalar.activation(pT[:, u % 2, 4:6], psP[:, 4:6], ACT.Copy).then_inc(s_eva, 1)

                        for hd, s in beats:
                            if hd < DH:
                                copy_v(hd, s)
                            for what, x, y in order(hd, s):
                                if what == "turn_qk":
                                    copy_qk(x, y)
                                elif what == "scores":
                                    exps(x, y)
                                elif what == "turn":
                                    evac(x, y)
                            if hd + 1 < DH and 1 <= s <= WS:
                                split_high(hd + 1, s - 1)
                        act.wait_ge(s_fin, 1)
                        nc.scalar.activation(ost[:], ost[:], ACT.Sqrt, bias=eps, scale=1.0 / DV).then_inc(s_finr, 1)

        stage_modulation()
        end_stage()
        with ExitStack() as right:
            with ExitStack() as att:
                t_ = dict(qmT=sb(att, "qmT", [MQ, MH, NT * P]), kmT=sb(att, "kmT", [MQ, MH, NT * P]),
                          vM=sb(att, "vM", [P, NT, MH * MV]), qsT=sb(att, "qsT", [P, SH // 2, NT * P]),
                          ksT=sb(att, "ksT", [P, NT * P]), vS=sb(att, "vS", [P, NT, SKV * SD]))
                stage_project0(t_)
                end_stage()
                o = sb(right, "o", [P, NT, D], side="right")
                lg = sb(right, "lg", [P, NT, NE], side="right")
                fT = sb(right, "fT", [P, KD, NT * P], side="right")
                ahead = [nc.alloc_semaphore(f"w_out{k}") for k in range(KD - 2)]
                stage_attend0(t_, o, fT, ahead)
                end_stage()
            stage_out(0, NT, o, fT, lg, a["wa_out"][0], None, ahead)
            end_stage()
            moe_ctx = ExitStack()
            moe = Moe(moe_ctx, 0)
            stage_route(0, NT, fT, lg, o, moe)
            end_stage()
        stage_experts(0, NT, moe)
        end_stage()
        moe_ctx.close()
        with ExitStack() as right:
            o = sb(right, "o1", [P, NT, D], side="right")
            with ExitStack() as left:
                aT = [sb(left, f"aT_{part}", [P, KD, NT * P], F32R) for part in ("hi", "lo")]
                stage_combine(0, NT, aT)
                end_stage()
                stage_attend1(aT, o)
                end_stage()
            lg = sb(right, "lg1", [P, NT, NE], side="right")
            fT = sb(right, "fT1", [P, KD, NT * P], side="right")
            stage_out(1, NL, o, fT, lg, a["wc_out"][0], a["gc_sub"][0], [])
            end_stage()
            moe_ctx = ExitStack()
            moe = Moe(moe_ctx, 1)
            stage_route(1, NL, fT, lg, o, moe)
            end_stage()
        stage_experts(1, NL, moe)
        end_stage()
        moe_ctx.close()
        stage_combine(1, NL, None)
        end_stage()


_INS = ['x', 'c', 'ctx', 'c_ctx', 'w_ada', 'b_ada', 'g_mix', 'g_ffn', 'wa_in', 'ga_q', 'ga_kv', 'wa_uq', 'wa_ukv',
        'wa_sink', 'wa_out', 'wc_in', 'lam_q1', 'lam_k1', 'lam_q2', 'lam_k2', 'gc_sub', 'wc_out', 'w_router',
        'b_router', 'we_gate', 'we_up', 'we_down', 'ws_gate', 'ws_up', 'ws_down', 'g_final']


def kernel(**inputs):
    import concourse.bacc as bacc
    from concourse.bass_utils import run_bass_kernel_spmd

    nc = bacc.Bacc("TRN2", target_bir_lowering=False, num_devices=1)
    arrays, args = {}, {}
    for name in _INS:
        arrays[f"in_{name}_dram"] = np.ascontiguousarray(inputs[name])
    arrays["in_cst_dram"] = shape_constants()
    for name in _INS + ["cst"]:
        x = arrays[f"in_{name}_dram"]
        args[name] = nc.dram_tensor(f"in_{name}_dram", x.shape, mybir.dt.from_np(x.dtype), kind="ExternalInput").ap()
    out = nc.dram_tensor("out_0_dram", (1, SEQ, D), F32, kind="ExternalOutput").ap()
    build(nc, args, out)
    r = run_bass_kernel_spmd(nc, [arrays], core_ids=[0])
    return r.results[0]["out_0_dram"]
```
